# Optimizing a Trainium2 kernel written in Bass

```python
import math
import jax, jax.numpy as jnp
from jax import lax
import numpy as np

D_MODEL = 1024
BATCH = 1
SEQ = 2048
DEPTH = 1

GDN_HEADS = 4
GDN_DK = 128
GDN_DV = 128
CONV_K = 4
CHUNK = 64
ATTN_HEADS = 8
ATTN_DH = 64
DILATED_PAIRS = ((128, 1), (512, 4), (2048, 16))
QBLK = 128
NUM_BUCKETS = 32
REL_MAX_DIST = 2048
N_GROUPS = 4
EXPERTS_PER_GROUP = 8
N_EXPERTS = N_GROUPS * EXPERTS_PER_GROUP
TOP_K = 2
D_EXPERT = 256
MOE_BLK = 128

EPS = 1e-6
NEG_INF = -1e30

GDN_QK_W = GDN_HEADS * GDN_DK
GDN_V_W = GDN_HEADS * GDN_DV
ATTN_W = ATTN_HEADS * ATTN_DH
MIX_W = GDN_V_W + ATTN_W
GDN_CONV_W = 2 * GDN_QK_W + GDN_V_W
IN_COLS = GDN_CONV_W + GDN_V_W + 2 * GDN_HEADS + 3 * ATTN_W

kernel_name = "hybrid_gdn_dilated_attn_hmoe_block"

def rmsnorm(x, g):
    xf = x.astype(jnp.float32)
    y = xf * lax.rsqrt(jnp.mean(xf * xf, axis=-1, keepdims=True) + EPS)
    return (y * g.astype(jnp.float32)).astype(x.dtype)

def l2norm(x):
    return x * lax.rsqrt(jnp.sum(x * x, axis=-1, keepdims=True) + EPS)

def causal_dwconv(x, w):
    k = w.shape[0]
    return lax.conv_general_dilated(
        x, w.astype(x.dtype)[:, None, :], window_strides=(1,), padding=[(k - 1, 0)],
        dimension_numbers=("NWC", "WIO", "NWC"), feature_group_count=x.shape[-1])

def t5_bucket(dist):
    max_exact = NUM_BUCKETS // 2
    d_f = jnp.maximum(dist, 1).astype(jnp.float32)
    large = max_exact + (jnp.log(d_f / max_exact) / math.log(REL_MAX_DIST / max_exact)
                         * (NUM_BUCKETS - max_exact)).astype(jnp.int32)
    large = jnp.minimum(large, NUM_BUCKETS - 1)
    return jnp.where(dist < max_exact, dist, large)

def gated_delta_rule(q, k, v, beta, g):
    bsz, seq, nh, dk = q.shape
    dv = v.shape[-1]
    n = seq // CHUNK

    def chunks(t):
        return t.reshape(bsz, n, CHUNK, nh, -1).transpose(0, 3, 1, 2, 4)

    q, k, v = chunks(q), chunks(k), chunks(v)
    beta = beta.reshape(bsz, n, CHUNK, nh).transpose(0, 3, 1, 2)
    G = jnp.cumsum(g.reshape(bsz, n, CHUNK, nh).transpose(0, 3, 1, 2), axis=-1)
    idx = jnp.arange(CHUNK)
    diff = G[..., :, None] - G[..., None, :]
    dec_incl = jnp.exp(jnp.where(idx[:, None] >= idx[None, :], diff, -jnp.inf))
    dec_strict = jnp.where(idx[:, None] > idx[None, :], dec_incl, 0.0)
    kb = k * beta[..., None]
    a_mat = jnp.einsum("bhnik,bhnjk->bhnij", kb, k) * dec_strict + jnp.eye(CHUNK, dtype=q.dtype)
    rhs = jnp.concatenate([v * beta[..., None], kb * jnp.exp(G)[..., None]], axis=-1)
    sol = lax.linalg.triangular_solve(a_mat, rhs, left_side=True, lower=True, unit_diagonal=True)
    u0, w = sol[..., :dv], sol[..., dv:]
    a_qk = jnp.einsum("bhnik,bhnjk->bhnij", q, k) * dec_incl
    qg = q * jnp.exp(G)[..., None]
    kg = k * jnp.exp(G[..., -1:] - G)[..., None]
    gl = jnp.exp(G[..., -1])

    def step(state, inp):
        u0_c, w_c, qg_c, kg_c, aqk_c, gl_c = inp
        u = u0_c - jnp.einsum("bhck,bhkv->bhcv", w_c, state)
        o = jnp.einsum("bhck,bhkv->bhcv", qg_c, state) + jnp.einsum("bhij,bhjv->bhiv", aqk_c, u)
        state = gl_c[..., None, None] * state + jnp.einsum("bhck,bhcv->bhkv", kg_c, u)
        return state, o

    xs = tuple(jnp.moveaxis(t, 2, 0) for t in (u0, w, qg, kg, a_qk, gl))
    s0 = jnp.zeros((bsz, nh, dk, dv), jnp.float32)
    _, o = lax.scan(step, s0, xs)
    return o.transpose(1, 0, 3, 2, 4).reshape(bsz, seq, nh, dv)

def dilated_branch(q, k, v, rel_bias, window, dil):
    bsz, seq, nh, dh = q.shape
    steps = window // dil
    L = seq // dil
    Lp = -(-L // QBLK) * QBLK
    nb = Lp // QBLK

    def to_sub(t):
        t = t.reshape(bsz, L, dil, nh, dh).transpose(0, 2, 1, 3, 4)
        t = jnp.pad(t, ((0, 0), (0, 0), (0, Lp - L), (0, 0), (0, 0)))
        return t.reshape(bsz, dil, nb, QBLK, nh, dh)

    def band(t):
        prev = jnp.pad(t, ((0, 0), (0, 0), (1, 0), (0, 0), (0, 0), (0, 0)))[:, :, :-1]
        return jnp.concatenate([prev, t], axis=3)

    qb = to_sub(q)
    kk, vv = band(to_sub(k)), band(to_sub(v))
    s = jnp.einsum("brnqhd,brnkhd->brnhqk", qb, kk) * (dh ** -0.5)
    qi = jnp.arange(QBLK)[:, None]
    kj = jnp.arange(2 * QBLK)[None, :]
    delta = qi + QBLK - kj
    in_win = (delta >= 0) & (delta <= steps)
    bias = rel_bias.astype(jnp.float32)[t5_bucket(jnp.maximum(delta, 0) * dil)]
    s = s + bias.transpose(2, 0, 1)
    key_pos = jnp.arange(nb)[:, None] * QBLK - QBLK + kj
    valid = in_win[None] & (key_pos >= 0)[:, None, :]
    s = jnp.where(valid[:, None], s, NEG_INF)
    m = jnp.max(s, axis=-1, keepdims=True)
    p = jnp.exp(s - m)
    den = jnp.sum(p, axis=-1)
    o = jnp.einsum("brnhqk,brnkhd->brnqhd", p, vv) / den.transpose(0, 1, 2, 4, 3)[..., None]
    lse = (m[..., 0] + jnp.log(den)).transpose(0, 1, 2, 4, 3)
    o = o.reshape(bsz, dil, Lp, nh, dh)[:, :, :L].transpose(0, 2, 1, 3, 4).reshape(bsz, seq, nh, dh)
    lse = lse.reshape(bsz, dil, Lp, nh)[:, :, :L].transpose(0, 2, 1, 3).reshape(bsz, seq, nh)
    return o, lse

def hybrid_mixer(h, w_in, w_conv, a_log, dt_bias, gdn_norm, attn_norm, w_out, rel_bias):
    bsz, seq, _ = h.shape
    f32 = jnp.float32
    p = h @ w_in
    s1 = GDN_CONV_W
    s2 = s1 + GDN_V_W
    s3 = s2 + GDN_HEADS
    s4 = s3 + GDN_HEADS
    qkv_a, z, b_raw, a_raw, qkv_b = p[..., :s1], p[..., s1:s2], p[..., s2:s3], p[..., s3:s4], p[..., s4:]

    qkv_a = jax.nn.silu(causal_dwconv(qkv_a, w_conv)).astype(f32)
    qa = l2norm(qkv_a[..., :GDN_QK_W].reshape(bsz, seq, GDN_HEADS, GDN_DK)) * (GDN_DK ** -0.5)
    ka = l2norm(qkv_a[..., GDN_QK_W:2 * GDN_QK_W].reshape(bsz, seq, GDN_HEADS, GDN_DK))
    va = qkv_a[..., 2 * GDN_QK_W:].reshape(bsz, seq, GDN_HEADS, GDN_DV)
    beta = jax.nn.sigmoid(b_raw.astype(f32))
    g = -jnp.exp(a_log.astype(f32)) * jax.nn.softplus(a_raw.astype(f32) + dt_bias.astype(f32))
    oa = gated_delta_rule(qa, ka, va, beta, g)
    oa = rmsnorm(oa, gdn_norm) * jax.nn.silu(z.astype(f32).reshape(bsz, seq, GDN_HEADS, GDN_DV))
    oa = oa.reshape(bsz, seq, GDN_V_W)

    qkv_b = qkv_b.astype(f32)
    qb = qkv_b[..., :ATTN_W].reshape(bsz, seq, ATTN_HEADS, ATTN_DH)
    kb = qkv_b[..., ATTN_W:2 * ATTN_W].reshape(bsz, seq, ATTN_HEADS, ATTN_DH)
    vb = qkv_b[..., 2 * ATTN_W:].reshape(bsz, seq, ATTN_HEADS, ATTN_DH)
    outs, lses = [], []
    for window, dil in DILATED_PAIRS:
        o_i, lse_i = dilated_branch(qb, kb, vb, rel_bias, window, dil)
        outs.append(o_i)
        lses.append(lse_i)
    wts = jax.nn.softmax(jnp.stack(lses, axis=-1), axis=-1)
    ob = jnp.sum(jnp.stack(outs, axis=-1) * wts[:, :, :, None, :], axis=-1)
    ob = rmsnorm(ob.reshape(bsz, seq, ATTN_W), attn_norm)

    y = jnp.concatenate([oa, ob], axis=-1).astype(h.dtype)
    return y @ w_out

def hierarchical_moe(h, w_rg, w_re, w_gate, w_up, w_down):
    bsz, seq, d = h.shape
    f32 = jnp.float32
    T = bsz * seq
    xt = h.reshape(T, d)
    xf = xt.astype(f32)
    gp = jax.nn.softmax(xf @ w_rg.astype(f32), axis=-1)
    gprob, gidx = lax.top_k(gp, 1)
    el = (xf @ w_re.astype(f32)).reshape(T, N_GROUPS, EXPERTS_PER_GROUP)
    el = jnp.take_along_axis(el, gidx[:, :, None], axis=1)[:, 0]
    eprob, eidx = lax.top_k(jax.nn.softmax(el, axis=-1), TOP_K)
    eprob = eprob / jnp.sum(eprob, axis=-1, keepdims=True)
    gates = gprob * eprob
    expert = gidx * EXPERTS_PER_GROUP + eidx

    A = T * TOP_K
    flat_e = expert.reshape(A).astype(jnp.int32)
    flat_tok = jnp.repeat(jnp.arange(T, dtype=jnp.int32), TOP_K)
    flat_w = gates.reshape(A)
    order = jnp.argsort(flat_e)
    se, stok, sw = flat_e[order], flat_tok[order], flat_w[order]
    counts = jax.ops.segment_sum(jnp.ones((A,), jnp.int32), flat_e, num_segments=N_EXPERTS)
    starts = jnp.cumsum(counts) - counts
    padded = (counts + MOE_BLK - 1) // MOE_BLK * MOE_BLK
    pends = jnp.cumsum(padded)
    pstarts = pends - padded
    dest = pstarts[se] + jnp.arange(A, dtype=jnp.int32) - starts[se]
    P = -(-A // MOE_BLK) * MOE_BLK + N_EXPERTS * MOE_BLK
    nblk = P // MOE_BLK
    buf_tok = jnp.zeros((P,), jnp.int32).at[dest].set(stok)
    buf_w = jnp.zeros((P,), f32).at[dest].set(sw)
    blk_start = jnp.arange(nblk, dtype=jnp.int32) * MOE_BLK
    blk_e = jnp.minimum(jnp.searchsorted(pends, blk_start, side="right"), N_EXPERTS - 1)
    xs = xt[buf_tok].reshape(nblk, MOE_BLK, d)

    def expert_block(args):
        xb, e = args
        hid = jax.nn.silu(xb @ w_gate[e]) * (xb @ w_up[e])
        return hid @ w_down[e]

    ys = lax.map(expert_block, (xs, blk_e)).reshape(P, d)
    out = jnp.zeros((T, d), ys.dtype).at[buf_tok].add(ys * buf_w[:, None].astype(ys.dtype))
    return out.reshape(bsz, seq, d)

def setup_inputs(seed: int = 0) -> dict:
    key = jax.random.key(seed)
    ks = jax.random.split(key, 22)
    f32 = jnp.float32
    D = D_MODEL

    def nrm(k, shape, scale):
        return jax.random.normal(k, shape, f32) * scale

    dt = jnp.exp(jax.random.uniform(ks[8], (DEPTH, GDN_HEADS), f32, math.log(1e-3), math.log(1e-1)))
    return {
        "x": nrm(ks[0], (BATCH, SEQ, D), 1.0),
        "c": nrm(ks[1], (BATCH, D), 1.0),
        "w_ada": nrm(ks[2], (DEPTH, D, 6 * D), 0.5 * D ** -0.5),
        "b_ada": nrm(ks[3], (DEPTH, 6 * D), 0.02),
        "norm_mix": 1.0 + nrm(ks[4], (DEPTH, D), 0.02),
        "w_in": nrm(ks[5], (DEPTH, D, IN_COLS), D ** -0.5),
        "w_conv": nrm(ks[6], (DEPTH, CONV_K, GDN_CONV_W), CONV_K ** -0.5),
        "a_log": jnp.log(jax.random.uniform(ks[7], (DEPTH, GDN_HEADS), f32, 1.0, 16.0)),
        "dt_bias": dt + jnp.log(-jnp.expm1(-dt)),
        "gdn_norm": 1.0 + nrm(ks[9], (DEPTH, GDN_DV), 0.02),
        "attn_norm": 1.0 + nrm(ks[10], (DEPTH, ATTN_W), 0.02),
        "w_out": nrm(ks[11], (DEPTH, MIX_W, D), MIX_W ** -0.5),
        "rel_bias": nrm(ks[12], (NUM_BUCKETS, ATTN_HEADS), 0.5),
        "norm_ffn": 1.0 + nrm(ks[13], (DEPTH, D), 0.02),
        "w_router_group": nrm(ks[14], (DEPTH, D, N_GROUPS), D ** -0.5),
        "w_router_expert": nrm(ks[15], (DEPTH, D, N_EXPERTS), D ** -0.5),
        "w_gate": nrm(ks[16], (DEPTH, N_EXPERTS, D, D_EXPERT), D ** -0.5),
        "w_up": nrm(ks[17], (DEPTH, N_EXPERTS, D, D_EXPERT), D ** -0.5),
        "w_down": nrm(ks[18], (DEPTH, N_EXPERTS, D_EXPERT, D), D_EXPERT ** -0.5),
        "norm_final": 1.0 + nrm(ks[19], (D,), 0.02),
    }

def reference(x, c, w_ada, b_ada, norm_mix, w_in, w_conv, a_log, dt_bias, gdn_norm, attn_norm,
              w_out, rel_bias, norm_ffn, w_router_group, w_router_expert, w_gate, w_up, w_down,
              norm_final):
    for l in range(DEPTH):
        mod = c @ w_ada[l] + b_ada[l]
        sh_a, sc_a, gt_a, sh_f, sc_f, gt_f = jnp.split(mod[:, None, :], 6, axis=-1)
        h = rmsnorm(x, norm_mix[l]) * (1.0 + sc_a) + sh_a
        x = x + gt_a * hybrid_mixer(h, w_in[l], w_conv[l], a_log[l], dt_bias[l], gdn_norm[l],
                                    attn_norm[l], w_out[l], rel_bias)
        h = rmsnorm(x, norm_ffn[l]) * (1.0 + sc_f) + sh_f
        x = x + gt_f * hierarchical_moe(h, w_router_group[l], w_router_expert[l], w_gate[l],
                                        w_up[l], w_down[l])
    return rmsnorm(x, norm_final)


_drawn_inputs = setup_inputs


def setup_inputs(seed=0):
    import zlib

    import numpy as np

    out = dict(_drawn_inputs(seed))
    spreads = {}
    factors = {'norm_mix': 3.374,
     'gdn_norm': 4.375,
     'attn_norm': 3.958,
     'norm_ffn': 2.683,
     'norm_final': 2.801}
    for name, (base, spread) in spreads.items():
        noise = np.random.default_rng([zlib.crc32(name.encode()), seed]).standard_normal(out[name].shape)
        drawn = base * np.exp(spread * noise) if base else spread * noise
        out[name] = __import__('jax').numpy.asarray(drawn.astype(out[name].dtype))
    for name, factor in factors.items():
        out[name] = (out[name] * factor).astype(out[name].dtype)
    return out
```

```python
import concourse.bass as bass
from concourse import mybir
from contextlib import ExitStack, contextmanager

F32 = mybir.dt.float32
I32 = mybir.dt.int32
U32 = mybir.dt.uint32
ALU = mybir.AluOpType
ACT = mybir.ActivationFunctionType
AX = mybir.AxisListType

P = 128
T = 2048
NT = T // P
D = 1024
KD = D // P
EPS = 1e-6
NEG = -1e30
BANK = 512

GH = 4
GW = GH * P
CONV = 4
NCONV = 3 * GH
AH = 8
DH = 64
AW = AH * DH
BR = ((1, 16), (4, 4), (16, 1))
NB = len(BR)
BIAS_W = 384
NE = 32
NG = 4
EG = NE // NG
DE = 256
NBLK = (2 * T + NE * (P - 1)) // P
NTOK = 2 * GW + 8

C_ID = 0
C_UI = C_ID + P
C_US = C_UI + P
C_ONE = C_US + P
C_FLIP = C_ONE + P
C_NI = C_FLIP + P
C_PS = C_NI + P
C_L = C_PS + P
C_L1T = C_L + 7 * P
C_IOTA = C_L1T + P
C_BLK = C_IOTA + NE
C_TOK = C_BLK + NBLK
C_END = C_TOK + NT


def bucket_constants():
    import math
    import numpy as np
    c = np.zeros((P, C_END), np.float32)
    r, k = np.arange(P)[:, None], np.arange(P)[None, :]
    c[:, C_ID:C_ID + P] = r == k
    c[:, C_UI:C_UI + P] = r <= k
    c[:, C_US:C_US + P] = r < k
    c[:, C_ONE:C_ONE + P] = 1
    c[:, C_FLIP:C_FLIP + P] = r + k == P - 1
    c[:, C_NI:C_NI + P] = np.where(r <= k, 0, NEG)
    c[:, C_PS:C_PS + P] = np.where(r > k, 0, -NEG)
    for n in range(7):
        b = 1 << n
        m = (r // (2 * b) == k // (2 * b)) & (r % (2 * b) >= b) & (k % (2 * b) < b)
        c[:, C_L + n * P:C_L + (n + 1) * P] = m
        if n == 0:
            c[:, C_L1T:C_L1T + P] = m.T
    c[:, C_IOTA:C_IOTA + NE] = np.arange(NE)
    c[:, C_BLK:C_BLK + NBLK] = P * np.arange(NBLK)
    c[:, C_TOK:C_TOK + NT] = np.arange(NT)[None, :] * P + r
    one = np.zeros((NE, NB, BIAS_W), np.float32)
    off = np.full((AH, NB, BIAS_W), NEG, np.float32)
    for n, (dil, _) in enumerate(BR):
        for y in range(P - 1, 2 * P):
            dist = (2 * P - 1 - y) * dil
            if dist < 16:
                b = dist
            else:
                b = 16 + int(np.float32(np.log(np.float32(dist / 16))) / np.float32(math.log(2048 / 16)) * np.float32(16))
            one[min(b, 31), n, y] = 1
            off[:, n, y] = 0
    return c, one.reshape(NE, NB * BIAS_W), off.reshape(AH, NB * BIAS_W)


class Chain:

    def __init__(self, eng, sem):
        self.eng, self.sem, self.base, self.n = eng, sem, 0, 0

    def __call__(self, ins):
        self.n += 1
        ins.then_inc(self.sem, 1)
        self.eng.wait_ge(self.sem, self.base + self.n)

    @contextmanager
    def loop(self, times, per):
        start, self.n = self.base + self.n, 0
        with self.eng.Fori(0, times) as i:
            self.base = i * per + start
            yield i
            assert self.n == per, (self.n, per)
        self.base, self.n = start + times * per, 0


class Signal:

    def __init__(self, sem, step, credit):
        self.inc, self.step, self.credit = (sem, step), step, credit

    def n(self, n):
        return self.inc[0], n * self.step + self.credit * self.step


class Room:

    def __init__(self, nc, tag):
        self.nc, self.tag, self.ctx, self.all, self.sem_list = nc, tag, ExitStack(), [], []

    def __enter__(self):
        return self

    def __exit__(self, *a):
        self.ctx.close()
        if self.sem_list:
            self.nc.clear_and_free_semaphores(self.sem_list)
            self.nc.all_engine_barrier()

    def sb(self, name, shape, dt=F32):
        return self.ctx.enter_context(self.nc.sbuf_tensor(f"{self.tag}_{name}", shape, dt))

    def plain(self, name):
        self.sem_list.append(self.nc.alloc_semaphore(name=f"{self.tag}_{name}"))
        return self.sem_list[-1]

    def sig(self, name, step=1, credit=1):
        s = Signal(self.plain(name), step, credit)
        self.all.append(s)
        return s

    def sigs(self, name, n=2, step=1, credit=1):
        return [self.sig(f"{name}{k}", step, credit) for k in range(n)]

    def block(self):
        for s in self.all:
            self.nc.sync.sem_inc(s.inc[0], s.step * s.credit)
        return self.nc.Block()


def row_bc(ap, n, offset=0):
    return bass.AP(ap.tensor, ap.offset + offset, [[0, P], [1, n]])


def one(ap, i):
    r = ap[(bass.ds(i, 1),) + (slice(None),) * (ap.ndim - 1)]
    names = " ".join("bcde"[:ap.ndim - 2])
    return r.rearrange(f"a p {names} -> (a p) {names}")


def adaln(nc, m, a):
    N = 6 * D // BANK // 2
    with Room(nc, "ada") as R:
        ct = R.sb("ct", [P, KD])
        cb = R.sb("cb", [P, KD, P])
        w = R.sb("w", [P, 2, KD, BANK])
        bb = R.sb("bb", [P, 2, BANK])
        nrm = R.sb("nrm", [P, 2, D])
        xb = R.sb("xb", [P, 2, D])
        junk = R.sb("junk", [P, 2, D])
        eps = R.sb("eps", [P, 1])
        ssq = R.sb("ssq", [P, NT])
        std = R.sb("std", [P, NT])
        c_in, small_in = R.sig("c_in", 16), R.sig("small_in", 16)
        cb_ready, eps_set, std_ready = R.sig("cb_ready"), R.sig("eps_set"), R.sig("std_ready")
        w_in = R.sigs("w_in", 2, 16)
        mm_done, mod_ready = R.sigs("mm_done"), R.sigs("mod_ready")
        x_in, x_used = R.sigs("x_in", 2, 16), R.sigs("x_used")
        dve_self = R.plain("dve_self")
        ps = m.ps
        with R.block() as block:
            @block.sync
            def _(sp):
                sp.dma_start(ct[:, :], a["c"]).then_inc(*c_in.inc)
                sp.dma_start(nrm[:, 0, :], row_bc(a["norm_mix"], D)).then_inc(*small_in.inc)
                sp.dma_start(nrm[:, 1, :], row_bc(a["norm_ffn"], D)).then_inc(*small_in.inc)
                sp.dma_start(m.cst[:, :], a["cst"]).then_inc(*small_in.inc)
                with sp.Fori(0, N) as i:
                    for b in range(2):
                        sp.wait_ge(*mod_ready[b].n(i))
                        sp.dma_start(w[:, b, :, :], one(a["w_ada"], 2 * i + b)).then_inc(*w_in[b].inc)
                        sp.dma_start(bb[:, b, :], row_bc(a["b_ada"], BANK, (2 * i + b) * BANK)).then_inc(*w_in[b].inc)
                sp.wait_ge(*small_in.n(3))

            @block.tensor
            def _(pe):
                pe.wait_ge(*cb_ready.n(1))
                with pe.Fori(0, N) as i:
                    for b in range(2):
                        pe.wait_ge(*w_in[b].n(2 * i + 2))
                        pe.wait_ge(*mod_ready[b].n(i))
                        for k in range(KD):
                            last = nc.tensor.matmul(ps[:, b, :], cb[:, k, :], w[:, b, k, :], start=(k == 0), stop=(k == KD - 1))
                        last.then_inc(*mm_done[b].inc)

            @block.vector
            def _(dve):
                link = Chain(dve, dve_self)
                nc.vector.memset(eps[:, :], EPS).then_inc(*eps_set.inc)
                dve.wait_ge(*c_in.n(1))
                nc.vector.tensor_copy(cb[:, :, :], ct[:, :].unsqueeze(2).to_broadcast([P, KD, P])).then_inc(*cb_ready.inc)
                with dve.Fori(0, N) as i:
                    for b in range(2):
                        dve.wait_ge(*mm_done[b].n(i + 1))
                        nc.vector.tensor_tensor(m.mod[:, bass.ds((2 * i + b) * BANK, BANK)], ps[:, b, :], bb[:, b, :], ALU.add).then_inc(*mod_ready[b].inc)
                for b in range(2):
                    dve.wait_ge(*mod_ready[b].n(N))
                dve.wait_ge(*small_in.n(3))
                for n in range(2):
                    s = m.mod[:, (3 * n + 1) * D:(3 * n + 2) * D]
                    link(nc.vector.scalar_tensor_tensor(s, s, 1.0, nrm[:, n, :], ALU.add, ALU.mult))
                dve.wait_ge(*std_ready.n(1))
                link(nc.vector.reciprocal(m.rstd[:, :], std[:, :]))

            @block.scalar
            def _(act):
                act.wait_ge(*eps_set.n(1))
                with act.Fori(0, NT // 2) as i:
                    for b in range(2):
                        act.wait_ge(*x_used[b].n(i))
                        act.dma_start(xb[:, b, :], one(a["x"], 2 * i + b)).then_inc(*x_in[b].inc)
                    for b in range(2):
                        act.wait_ge(*x_in[b].n(i + 1))
                        nc.scalar.activation(junk[:, b, :], xb[:, b, :], ACT.Square, accum_out=ssq[:, bass.ds(2 * i + b, 1)]).then_inc(*x_used[b].inc)
                for b in range(2):
                    act.wait_ge(*x_used[b].n(NT // 2))
                nc.scalar.activation(std[:, :], ssq[:, :], ACT.Sqrt, bias=eps[:, :], scale=1.0 / D).then_inc(*std_ready.inc)


def project_tokens(nc, m, a):
    with Room(nc, "pt") as R:
        xb = R.sb("xb", [P, 2, D])
        h = R.sb("h", [P, 2, D])
        ht = R.sb("ht", [P, 2, KD, P])
        wt = R.sb("wt", [P, KD, NTOK])
        z = R.sb("z", [P, 2, GW])
        v = R.sb("v", [P, 2, AW])
        w_in = R.sig("w_in", 16)
        x_in, xg_ready, h_ready, tr_done = R.sigs("x_in", 2, 16), R.sigs("xg_ready"), R.sigs("h_ready"), R.sigs("tr_done")
        ht_ready, ht_kept = R.sigs("ht_ready"), R.sigs("ht_kept")
        z_mm, v_mm, ba_mm = R.sigs("z_mm"), R.sigs("v_mm"), R.sigs("ba_mm")
        z_ready, v_ready, ba_kept = R.sigs("z_ready"), R.sigs("v_ready"), R.sigs("ba_kept")
        z_out, v_out = R.sigs("z_out", 2, 16), R.sigs("v_out", 2, 16)
        ps = m.ps
        gain, shift = m.mod[:, D:2 * D], m.mod[:, 0:D]
        with R.block() as block:
            @block.sync
            def _(sp):
                sp.dma_start(wt[:, :, :], a["w_tok"]).then_inc(*w_in.inc)
                with sp.Fori(0, NT // 2) as i:
                    for b in range(2):
                        sp.wait_ge(*xg_ready[b].n(i))
                        sp.dma_start(xb[:, b, :], one(a["x"], 2 * i + b)).then_inc(*x_in[b].inc)

            @block.vector
            def _(dve):
                def make_h(i, b):
                    dve.wait_ge(*x_in[b].n(i + 1))
                    dve.wait_ge(*tr_done[b].n(i))
                    nc.vector.scalar_tensor_tensor(h[:, b, :], xb[:, b, :], m.rstd[:, bass.ds(2 * i + b, 1)], gain, ALU.mult, ALU.mult).then_inc(*xg_ready[b].inc)
                    dve.wait_ge(*xg_ready[b].n(i + 1))
                    nc.vector.tensor_tensor(h[:, b, :], h[:, b, :], shift, ALU.add).then_inc(*h_ready[b].inc)

                def drain(i, ahead):
                    for b in range(2):
                        dve.wait_ge(*ht_ready[b].n(i + 1))
                        nc.vector.tensor_copy(m.ht[:, :, bass.ds((2 * i + b) * P, P)], ht[:, b, :, :]).then_inc(*ht_kept[b].inc)
                        if ahead:
                            make_h(i + 1, b)
                        dve.wait_ge(*v_mm[b].n(i + 1))
                        dve.wait_ge(*v_out[b].n(i))
                        nc.vector.tensor_copy(v[:, b, :], ps[:, 5, :]).then_inc(*v_ready[b].inc)
                        dve.wait_ge(*ba_mm[b].n(i + 1))
                        nc.vector.tensor_copy(m.ba[:, bass.ds((2 * i + b) * 8, 8)], ps[:, 6, 0:8]).then_inc(*ba_kept[b].inc)

                make_h(0, 0)
                make_h(0, 1)
                with dve.Fori(0, NT // 2 - 1) as i:
                    drain(i, True)
                drain(NT // 2 - 1, False)
                for b in range(2):
                    dve.wait_ge(*ba_kept[b].n(NT // 2))

            @block.tensor
            def _(pe):
                def left(i, b, s):
                    pe.wait_ge(*s[1 - b].n(i + b))

                pe.wait_ge(*w_in.n(1))
                with pe.Fori(0, NT // 2) as i:
                    for b in range(2):
                        pe.wait_ge(*h_ready[b].n(i + 1))
                        pe.wait_ge(*ht_ready[b].n(i))
                        for k in range(KD):
                            last = nc.tensor.transpose(ps[:, 2 * b + k // 4, (k % 4) * P:(k % 4 + 1) * P], h[:, b, k * P:(k + 1) * P], m.ident)
                        last.then_inc(*tr_done[b].inc)
                    for b in range(2):
                        pe.wait_ge(*ht_ready[b].n(i + 1))
                        for bank, lo, hi, read, done in ((4, 0, GW, z_ready, z_mm), (5, GW, 2 * GW, v_ready, v_mm), (6, 2 * GW, NTOK, ba_kept, ba_mm)):
                            left(i, b, read)
                            for k in range(KD):
                                last = nc.tensor.matmul(ps[:, bank, 0:hi - lo], ht[:, b, k, :], wt[:, k, lo:hi], start=(k == 0), stop=(k == KD - 1))
                            last.then_inc(*done[b].inc)

            @block.scalar
            def _(act):
                with act.Fori(0, NT // 2) as i:
                    for b in range(2):
                        act.wait_ge(*tr_done[b].n(i + 1))
                        act.wait_ge(*ba_mm[b].n(i))
                        act.wait_ge(*ht_kept[b].n(i))
                        nc.scalar.copy(ht[:, b, :, :].rearrange("p k n -> p (k n)"), ps[:, 2 * b:2 * b + 2, :].rearrange("p k n -> p (k n)")).then_inc(*ht_ready[b].inc)
                    for b in range(2):
                        act.wait_ge(*z_mm[b].n(i + 1))
                        act.wait_ge(*z_out[b].n(i))
                        nc.scalar.activation(z[:, b, :], ps[:, 4, :], ACT.Silu).then_inc(*z_ready[b].inc)
                        act.wait_ge(*z_ready[b].n(i + 1))
                        act.dma_start(one(m.z_d, 2 * i + b), z[:, b, :]).then_inc(*z_out[b].inc)
                        act.wait_ge(*v_ready[b].n(i + 1))
                        act.dma_start(one(m.v_d, 2 * i + b), v[:, b, :]).then_inc(*v_out[b].inc)
                for b in range(2):
                    act.wait_ge(*z_out[b].n(NT // 2))
                    act.wait_ge(*v_out[b].n(NT // 2))


def project_channels(nc, m, a):
    HIST = CONV - 1
    with Room(nc, "pc") as R:
        w = R.sb("w", [P, 2, KD, P])
        wc = R.sb("wc", [P, NCONV * CONV])
        pre = R.sb("pre", [P, 2, HIST + T])
        cv = R.sb("cv", [P, 2, T])
        sq = R.sb("sq", [P, 1, T])
        rs = R.sb("rs", [P, 1, T])
        eps = R.sb("eps", [P, 1])
        small_in, zeroed = R.sig("small_in", 16), R.sig("zeroed")
        w_in = R.sigs("w_in", 2, 16)
        mm_done, mm_read = R.sigs("mm_done", 4, credit=2), R.sigs("mm_read", 4)
        cv_ready, silu_ready, sq_ready = R.sigs("cv_ready"), R.sigs("silu_ready"), R.sigs("sq_ready")
        ss_done, std_ready, ready, out = R.sigs("ss_done"), R.sigs("std_ready"), R.sigs("ready"), R.sigs("out", 2, 16)
        dve_self = R.plain("dve_self")
        ps = m.ps
        RUNS = ((0, GH, True, True), (GH, GH // 2, True, False), (NCONV // 2, AW // P, False, False))
        with R.block() as block:
            @block.sync
            def _(sp):
                sp.dma_start(wc[:, :], a["w_conv"]).then_inc(*small_in.inc)

                def load(i):
                    for b in range(2):
                        sp.wait_ge(*mm_done[3].n(2 * i + b - 1))
                        sp.dma_start(w[:, b, :, :], one(a["w_chan"], 2 * i + b)).then_inc(*w_in[b].inc)

                def store(i, conv):
                    for b in range(2):
                        if conv:
                            sp.wait_ge(*ready[b].n(i + 1))
                        else:
                            for g in range(4):
                                sp.wait_ge(*mm_read[g].n(2 * i + b + 1))
                        sp.dma_start(one(m.ch_d, 2 * i + b), cv[:, b, :]).then_inc(*out[b].inc)

                load(0)
                for first, n, conv, norm in RUNS:
                    with sp.Fori(first, first + n - (not conv)) as i:
                        load(i + 1)
                        store(i, conv)
                store(m.NCH // 2 - 1, False)
                for b in range(2):
                    sp.wait_ge(*out[b].n(m.NCH // 2))

            @block.tensor
            def _(pe):
                def norms(i, b):
                    pe.wait_ge(*sq_ready[b].n(i + 1))
                    pe.wait_ge(*std_ready[1 - b].n(i + b))
                    for g in range(4):
                        last = nc.tensor.matmul(ps[:, 4 + g, :], m.ones, sq[:, 0, g * BANK:(g + 1) * BANK], start=True, stop=True)
                    last.then_inc(*ss_done[b].inc)

                def chunk(i, b):
                    pe.wait_ge(*w_in[b].n(i + 1))
                    for g in range(4):
                        pe.wait_ge(*mm_read[g].n(2 * i + b))
                        for k in range(KD):
                            last = nc.tensor.matmul(ps[:, g, :], w[:, b, k, :], m.ht[:, k, g * BANK:(g + 1) * BANK], start=(k == 0), stop=(k == KD - 1))
                        last.then_inc(*mm_done[g].inc)

                for first, n, conv, norm in RUNS:
                    if norm:
                        chunk(first, 0)
                        chunk(first, 1)
                        norms(first, 0)
                    with pe.Fori(first + norm, first + n) as i:
                        chunk(i, 0)
                        if norm:
                            norms(i - 1, 1)
                        chunk(i, 1)
                        if norm:
                            norms(i, 0)
                    if norm:
                        norms(first + n - 1, 1)

            @block.scalar
            def _(act):
                act.wait_ge(*zeroed.n(2))
                for first, n, conv, norm in RUNS:
                    with act.Fori(first, first + n) as i:
                        for b in range(2):
                            if conv:
                                act.wait_ge(*cv_ready[b].n(i))
                                dst = pre[:, b, HIST:]
                            else:
                                act.wait_ge(*out[b].n(i))
                                dst = cv[:, b, :]
                            for g in range(4):
                                act.wait_ge(*mm_done[g].n(2 * i + b + 1))
                                nc.scalar.copy(dst[:, g * BANK:(g + 1) * BANK], ps[:, g, :]).then_inc(*mm_read[g].inc)
                            if conv:
                                act.wait_ge(*cv_ready[b].n(i + 1))
                                nc.scalar.activation(cv[:, b, :], cv[:, b, :], ACT.Silu).then_inc(*(silu_ready if norm else ready)[b].inc)
                            if norm:
                                act.wait_ge(*silu_ready[b].n(i + 1))
                                act.wait_ge(*ss_done[1 - b].n(i + b))
                                nc.scalar.activation(sq[:, 0, :], cv[:, b, :], ACT.Square).then_inc(*sq_ready[b].inc)
                                act.wait_ge(*ss_done[b].n(i + 1))
                                act.wait_ge(*ready[1 - b].n(i + b))
                                nc.scalar.activation(rs[:, 0, :], ps[:, 4:8, :].rearrange("p g n -> p (g n)"), ACT.Sqrt, bias=eps[:, :]).then_inc(*std_ready[b].inc)

            @block.vector
            def _(dve):
                link = Chain(dve, dve_self)
                link(nc.vector.memset(eps[:, :], EPS))
                for b in range(2):
                    nc.vector.memset(pre[:, b, 0:HIST], 0.0).then_inc(*zeroed.inc)
                dve.wait_ge(*small_in.n(1))
                for first, n, conv, norm in RUNS:
                    if not conv:
                        break
                    with link.loop(n, 2 * (3 + norm)) as j:
                        i = j + first
                        for b in range(2):
                            for g in range(4):
                                dve.wait_ge(*mm_read[g].n(2 * i + b + 1))
                            dve.wait_ge(*out[b].n(i))
                            link(nc.vector.tensor_scalar(cv[:, b, :], pre[:, b, 0:T], wc[:, bass.ds((2 * i + b) * CONV, 1)], None, ALU.mult))
                            for s in range(1, CONV):
                                ins = nc.vector.scalar_tensor_tensor(cv[:, b, :], pre[:, b, s:s + T], wc[:, bass.ds((2 * i + b) * CONV + s, 1)], cv[:, b, :], ALU.mult, ALU.add)
                                if s < CONV - 1:
                                    link(ins)
                            ins.then_inc(*cv_ready[b].inc)
                            if norm:
                                dve.wait_ge(*std_ready[b].n(i + 1))
                                link(nc.vector.reciprocal(rs[:, 0, :], rs[:, 0, :]))
                                nc.vector.tensor_tensor(cv[:, b, :], cv[:, b, :], rs[:, 0, :], ALU.mult).then_inc(*ready[b].inc)
def deltanet_gates(nc, m, a):
    N = NT * GH
    with Room(nc, "gg") as R:
        al = R.sb("al", [P, GH])
        dtb = R.sb("dtb", [P, GH])
        y = R.sb("y", [P, NT, GH])
        t = R.sb("t", [P, 3, NT, GH])
        small_in = R.sig("small_in", 16)
        y_ready, act_self, dve_self = R.sig("y_ready"), R.plain("act_self"), R.plain("dve_self")
        sp_ready, g_ready, sums_done, eg_ready, act_done = R.sig("sp_ready"), R.sig("g_ready"), R.sig("sums_done"), R.sig("eg_ready"), R.sig("act_done")
        diff_ready = R.sig("diff_ready")
        ps = m.ps
        ba = m.ba[:, :].rearrange("p (t n) -> p t n", n=8)
        last = ps[:, 1, 0:N]
        with R.block() as block:
            @block.sync
            def _(sp):
                sp.dma_start(al[:, :], row_bc(a["a_log"], GH)).then_inc(*small_in.inc)
                sp.dma_start(dtb[:, :], row_bc(a["dt_bias"], GH)).then_inc(*small_in.inc)

            @block.vector
            def _(dve):
                link = Chain(dve, dve_self)
                dve.wait_ge(*small_in.n(2))
                nc.vector.tensor_tensor(y[:, :, :], ba[:, :, GH:8], dtb[:, :].unsqueeze(1).to_broadcast([P, NT, GH]), ALU.add).then_inc(*y_ready.inc)
                dve.wait_ge(*sp_ready.n(1))
                link(nc.vector.scalar_tensor_tensor(y[:, :, :], y[:, :, :], 0.0, t[:, 1, :, :], ALU.max, ALU.add))
                nc.vector.scalar_tensor_tensor(m.g[:, :, :], y[:, :, :], -1.0, al[:, :].unsqueeze(1).to_broadcast([P, NT, GH]), ALU.mult, ALU.mult).then_inc(*g_ready.inc)
                dve.wait_ge(*sums_done.n(1))
                link(nc.vector.tensor_copy(m.gsum[:, :], ps[:, 0, 0:N]))
                nc.vector.tensor_tensor(m.kdec[:, :], last, m.gsum[:, :], ALU.subtract).then_inc(*diff_ready.inc)
                dve.wait_ge(*eg_ready.n(1))
                link(nc.vector.scalar_tensor_tensor(m.nbe[:, :], m.beta[:, :], -1.0, t[:, 2, :, :].rearrange("p t n -> p (t n)"), ALU.mult, ALU.mult))

            @block.scalar
            def _(act):
                link = Chain(act, act_self)
                act.wait_ge(*y_ready.n(1))
                link(nc.scalar.activation(m.beta[:, :].rearrange("p (t n) -> p t n", n=GH), ba[:, :, 0:GH], ACT.Sigmoid))
                link(nc.scalar.activation(al[:, :], al[:, :], ACT.Exp))
                link(nc.scalar.activation(t[:, 0, :, :], y[:, :, :], ACT.Abs))
                link(nc.scalar.activation(t[:, 0, :, :], t[:, 0, :, :], ACT.Exp, scale=-1.0))
                nc.scalar.activation(t[:, 1, :, :], t[:, 0, :, :], ACT.Ln, bias=1.0).then_inc(*sp_ready.inc)
                act.wait_ge(*diff_ready.n(1))
                link(nc.scalar.activation(m.kdec[:, :], m.kdec[:, :], ACT.Exp))
                link(nc.scalar.activation(m.sdec[:, :], last, ACT.Exp))
                nc.scalar.activation(t[:, 2, :, :].rearrange("p t n -> p (t n)"), m.gsum[:, :], ACT.Exp).then_inc(*eg_ready.inc)

            @block.tensor
            def _(pe):
                pe.wait_ge(*g_ready.n(1))
                g = m.g[:, :, :].rearrange("p t n -> p (t n)")
                nc.tensor.matmul(ps[:, 0, 0:N], m.cst[:, C_UI:C_UI + P], g, start=True, stop=True)
                nc.tensor.matmul(ps[:, 1, 0:N], m.ones, g, start=True, stop=True).then_inc(*sums_done.inc)


def deltanet(nc, m, a):
    LEV = 7
    with Room(nc, "gd") as R:
        def pair(name):
            return R.sb(name, [P, 2, GW])
        qkv = R.sb("qkv", [P, 2, NCONV, P])
        z = pair("z")
        gu = pair("gu")
        d1, d2 = pair("d1"), pair("d2")
        qg, kg, vb = pair("qg"), pair("kg"), pair("vb")
        nt, dd, dt, yy = pair("nt"), pair("dd"), pair("dt"), pair("yy")
        r, u, o, o2 = pair("r"), pair("u"), pair("o"), pair("o2")
        st = R.sb("st", [P, 2, GH])
        state = R.sb("state", [P, GW])
        gain = R.sb("gain", [P, P])
        eps = R.sb("eps", [P, 1])
        ps = m.ps
        S = R.sigs
        gain_in = R.sig("gain_in", 16)
        state_set = R.sig("state_set")
        qkv_in, z_in = S("qkv_in", 2, 16), S("z_in", 2, 16)
        gu_ready, rows_done, dd_ready, dec_ready = S("gu_ready"), S("rows_done"), S("dd_ready"), S("dec_ready")
        erow_ready, qg_ready = S("erow_ready"), S("qg_ready")
        kk_done, kq_done, n_ready, aqk_ready = S("kk_done"), S("kq_done"), S("n_ready"), S("aqk_ready")
        kt_done, vt_done, kg_ready, vb_ready = S("kt_done"), S("vt_done"), S("kg_ready"), S("vb_ready")
        nt_done, nt_ready = S("nt_done"), S("nt_ready")
        d_ready, dt_ready = S("d_ready"), S("dt_ready")
        y_done, y_ready, zz_done, zt_done = S("y_done"), S("y_ready"), S("zz_done"), S("zt_done")
        ks_done, r_ready, u_done, u_ready = S("ks_done"), S("r_ready"), S("u_done"), S("u_ready")
        o_done, ds_done, s_ready, o_ready = S("o_done"), S("ds_done"), S("s_ready"), S("o_ready")
        osq_ready, std_ready, y_out_ready, out = S("osq_ready"), S("std_ready"), S("y_out_ready"), S("out", 2, 16)
        dve_self, pool_self = R.plain("dve_self"), R.plain("pool_self")
        ID4 = m.ident.unsqueeze(1).to_broadcast([P, GH, P])

        def c4(col):
            return m.cst[:, col:col + P].unsqueeze(1).to_broadcast([P, GH, P])

        def h4(ap):
            return ap.rearrange("p (h n) -> p h n", h=GH)

        def hs(h):
            return slice(h * P, (h + 1) * P)

        with R.block() as block:
            @block.sync
            def _(sp):
                sp.dma_start(gain[:, :], row_bc(a["gdn_norm"], P)).then_inc(*gain_in.inc)
                with sp.Fori(0, NT // 2) as i:
                    for b in range(2):
                        sp.wait_ge(*qg_ready[b].n(i))
                        sp.wait_ge(*ks_done[b].n(i))
                        src = m.ch_d[0:NCONV, :, bass.ds((2 * i + b) * P, P)].rearrange("c p n -> p c n")
                        sp.dma_start(qkv[:, b, :, :], src).then_inc(*qkv_in[b].inc)
                        sp.wait_ge(*y_out_ready[b].n(i))
                        sp.dma_start(z[:, b, :], one(m.z_d, 2 * i + b)).then_inc(*z_in[b].inc)
                    for b in range(2):
                        sp.wait_ge(*y_out_ready[b].n(i + 1))
                        sp.dma_start(one(m.y_d, 2 * i + b), o[:, b, :]).then_inc(*out[b].inc)
                for b in range(2):
                    sp.wait_ge(*out[b].n(NT // 2))

            @block.gpsimd
            def _(pool):
                link = Chain(pool, pool_self)
                pool.wait_ge(*gain_in.n(1))
                with link.loop(NT // 2, 0) as i:
                    for b in range(2):
                        pool.wait_ge(*rows_done[b].n(i))
                        nc.gpsimd.tensor_tensor(h4(gu[:, b, :]), c4(C_UI), m.g[:, bass.ds(2 * i + b, 1), :].rearrange("p a h -> p (a h)").unsqueeze(2).to_broadcast([P, GH, P]), ALU.mult).then_inc(*gu_ready[b].inc)
                    for b in range(2):
                        pool.wait_ge(*qkv_in[b].n(i + 1))
                        pool.wait_ge(*erow_ready[b].n(i + 1))
                        pool.wait_ge(*o_done[b].n(i))
                        nc.gpsimd.tensor_tensor(qg[:, b, :], qg[:, b, :], qkv[:, b, 0:GH, :].rearrange("p h n -> p (h n)"), ALU.mult).then_inc(*qg_ready[b].inc)

            @block.tensor
            def _(pe):
                def heads(bank, lhs, rhs, done=None, **kw):
                    for h in range(GH):
                        last = nc.tensor.matmul(ps[:, bank, hs(h)], lhs(h), rhs(h), start=True, stop=True)
                    last.then_inc(*done.inc)

                def q(b, h):
                    return qkv[:, b, h, :]

                def k(b, h):
                    return qkv[:, b, GH + h, :]

                pe.wait_ge(*state_set.n(1))
                with pe.Fori(0, NT // 2) as i:
                    for b in range(2):
                        B = 4 * b
                        pe.wait_ge(*gu_ready[b].n(i + 1))
                        pe.wait_ge(*o_ready[b].n(i))
                        nc.tensor.matmul(ps[:, B, :], m.ones, gu[:, b, :], start=True, stop=True).then_inc(*rows_done[b].inc)
                        pe.wait_ge(*qkv_in[b].n(i + 1))
                        pe.wait_ge(*s_ready[b].n(i))
                        heads(B + 1, lambda h: k(b, h), lambda h: k(b, h), kk_done[b])
                        heads(B + 2, lambda h: k(b, h), lambda h: q(b, h), kq_done[b])
                        for h in range(GH):
                            last = nc.tensor.transpose(ps[:, B + 3, hs(h)], k(b, h), m.ident)
                        last.then_inc(*kt_done[b].inc)
                    for b in range(2):
                        B = 4 * b
                        pe.wait_ge(*n_ready[b].n(i + 1))
                        for h in range(GH):
                            last = nc.tensor.transpose(ps[:, B + 1, hs(h)], yy[:, b, hs(h)], m.ident)
                        last.then_inc(*nt_done[b].inc)
                        pe.wait_ge(*kg_ready[b].n(i + 1))
                        for h in range(GH):
                            last = nc.tensor.transpose(ps[:, B + 3, hs(h)], qkv[:, b, 2 * GH + h, :], m.ident)
                        last.then_inc(*vt_done[b].inc)
                    for l in range(1, LEV):
                        for b in range(2):
                            B = 4 * b
                            if l == 1:
                                pe.wait_ge(*nt_ready[b].n(i + 1))
                                pe.wait_ge(*aqk_ready[b].n(i + 1))
                                pe.wait_ge(*vb_ready[b].n(i + 1))
                                pe.wait_ge(*dec_ready[b].n(2 * i + 2))
                            pe.wait_ge(*d_ready[b].n((LEV - 1) * i + l))
                            heads(B, lambda h: nt[:, b, hs(h)], lambda h: dd[:, b, hs(h)], y_done[b])
                        for b in range(2):
                            B = 4 * b
                            pe.wait_ge(*y_ready[b].n((LEV - 1) * i + l))
                            pe.wait_ge(*dt_ready[b].n(LEV * i + l))
                            if l < LEV - 1:
                                heads(B + 1, lambda h: dt[:, b, hs(h)], lambda h: yy[:, b, hs(h)], zz_done[b])
                            heads(B + 2, lambda h: yy[:, b, hs(h)], lambda h: dt[:, b, hs(h)], zt_done[b])
                    for b in range(2):
                        B = 4 * b
                        pe.wait_ge(*s_ready[1 - b].n(i + b))
                        heads(B + 1, lambda h: k(b, h), lambda h: state[:, hs(h)], ks_done[b])
                        pe.wait_ge(*r_ready[b].n(i + 1))
                        pe.wait_ge(*dt_ready[b].n(LEV * i + LEV))
                        heads(B + 2, lambda h: dt[:, b, hs(h)], lambda h: r[:, b, hs(h)], u_done[b])
                        pe.wait_ge(*u_ready[b].n(i + 1))
                        pe.wait_ge(*qg_ready[b].n(i + 1))
                        heads(B + 3, lambda h: kg[:, b, hs(h)], lambda h: u[:, b, hs(h)], ds_done[b])
                        for h in range(GH):
                            nc.tensor.matmul(ps[:, B, hs(h)], qg[:, b, hs(h)], state[:, hs(h)], start=True, stop=False)
                            last = nc.tensor.matmul(ps[:, B, hs(h)], d2[:, b, hs(h)], u[:, b, hs(h)], start=False, stop=True)
                        last.then_inc(*o_done[b].inc)

            @block.scalar
            def _(act):
                with act.Fori(0, NT // 2) as i:
                    for b in range(2):
                        B = 4 * b
                        act.wait_ge(*rows_done[b].n(i + 1))
                        act.wait_ge(*dd_ready[b].n(i + 1))
                        act.wait_ge(*o_done[b].n(i))
                        nc.scalar.activation(qg[:, b, :], ps[:, B, :], ACT.Exp).then_inc(*erow_ready[b].inc)
                        nc.scalar.activation(d1[:, b, :], d1[:, b, :], ACT.Exp, scale=-1.0).then_inc(*dec_ready[b].inc)
                        nc.scalar.activation(d2[:, b, :], d2[:, b, :], ACT.Exp).then_inc(*dec_ready[b].inc)
                        act.wait_ge(*kt_done[b].n(i + 1))
                        act.wait_ge(*ds_done[b].n(i))
                        for h in range(GH):
                            ins = nc.scalar.activation(kg[:, b, hs(h)], ps[:, B + 3, hs(h)], ACT.Copy, scale=m.kdec[:, bass.ds((2 * i + b) * GH + h, 1)])
                        ins.then_inc(*kg_ready[b].inc)
                    for b in range(2):
                        B = 4 * b
                        act.wait_ge(*nt_done[b].n(i + 1))
                        nc.scalar.copy(nt[:, b, :], ps[:, B + 1, :]).then_inc(*nt_ready[b].inc)
                        act.wait_ge(*vt_done[b].n(i + 1))
                        for h in range(GH):
                            ins = nc.scalar.activation(vb[:, b, hs(h)], ps[:, B + 3, hs(h)], ACT.Copy, scale=m.beta[:, bass.ds((2 * i + b) * GH + h, 1)])
                        ins.then_inc(*vb_ready[b].inc)
                    for b in range(2):
                        B = 4 * b
                        act.wait_ge(*u_done[b].n(i + 1))
                        nc.scalar.copy(u[:, b, :], ps[:, B + 2, :]).then_inc(*u_ready[b].inc)
                        act.wait_ge(*o_done[b].n(i + 1))
                        act.wait_ge(*out[b].n(i))
                        nc.scalar.activation(o[:, b, :], ps[:, B, :], ACT.Copy, scale=float(P) ** -0.5).then_inc(*o_ready[b].inc)
                        act.wait_ge(*osq_ready[b].n(i + 1))
                        nc.scalar.activation(st[:, b, :], st[:, b, :], ACT.Sqrt, bias=eps[:, :], scale=1.0 / P).then_inc(*std_ready[b].inc)

            @block.vector
            def _(dve):
                link = Chain(dve, dve_self)
                link(nc.vector.memset(eps[:, :], EPS))
                nc.vector.memset(state[:, :], 0.0).then_inc(*state_set.inc)
                dve.wait_ge(*gain_in.n(1))
                with link.loop(NT // 2, 2 * 6) as i:
                    def per_head(tab, h):
                        return tab[:, bass.ds(b * GH + 2 * GH * i + h, 1)]

                    for b in range(2):
                        B = 4 * b
                        dve.wait_ge(*rows_done[b].n(i + 1))
                        dve.wait_ge(*aqk_ready[b].n(i))
                        dve.wait_ge(*o_done[b].n(i))
                        for h in range(GH):
                            nc.vector.scalar_tensor_tensor(d1[:, b, hs(h)], ps[:, B, hs(h)], per_head(m.gsum, h), m.cst[:, C_PS:C_PS + P], ALU.subtract, ALU.add)
                            ins = nc.vector.scalar_tensor_tensor(d2[:, b, hs(h)], ps[:, B, hs(h)], per_head(m.gsum, h), m.cst[:, C_NI:C_NI + P], ALU.subtract, ALU.add)
                        ins.then_inc(*dd_ready[b].inc)
                    for b in range(2):
                        B = 4 * b
                        dve.wait_ge(*dec_ready[b].n(2 * i + 1))
                        dve.wait_ge(*kk_done[b].n(i + 1))
                        for h in range(GH):
                            ins = nc.vector.scalar_tensor_tensor(yy[:, b, hs(h)], ps[:, B + 1, hs(h)], per_head(m.beta, h), d1[:, b, hs(h)], ALU.mult, ALU.mult)
                        ins.then_inc(*n_ready[b].inc)
                        dve.wait_ge(*dec_ready[b].n(2 * i + 2))
                        dve.wait_ge(*kq_done[b].n(i + 1))
                        nc.vector.tensor_tensor(d2[:, b, :], d2[:, b, :], ps[:, B + 2, :], ALU.mult).then_inc(*aqk_ready[b].inc)
                    for b in range(2):
                        dve.wait_ge(*n_ready[b].n(i + 1))
                        link(nc.vector.tensor_tensor(h4(dd[:, b, :]), h4(yy[:, b, :]), c4(C_L), ALU.mult))
                        nc.vector.tensor_tensor(h4(dd[:, b, :]), ID4, h4(dd[:, b, :]), ALU.subtract).then_inc(*d_ready[b].inc)
                        dve.wait_ge(*nt_ready[b].n(i + 1))
                        link(nc.vector.tensor_tensor(h4(dt[:, b, :]), h4(nt[:, b, :]), c4(C_L1T), ALU.mult))
                        nc.vector.tensor_tensor(h4(dt[:, b, :]), ID4, h4(dt[:, b, :]), ALU.subtract).then_inc(*dt_ready[b].inc)
                    for l in range(1, LEV):
                        for b in range(2):
                            B = 4 * b
                            dve.wait_ge(*y_done[b].n((LEV - 1) * i + l))
                            nc.vector.tensor_tensor(h4(yy[:, b, :]), ps[:, B, :].rearrange("p (h n) -> p h n", h=GH), c4(C_L + l * P), ALU.mult).then_inc(*y_ready[b].inc)
                        for b in range(2):
                            B = 4 * b
                            if l < LEV - 1:
                                dve.wait_ge(*zz_done[b].n((LEV - 2) * i + l))
                                dve.wait_ge(*d_ready[b].n((LEV - 1) * i + l))
                                nc.vector.tensor_tensor(dd[:, b, :], dd[:, b, :], ps[:, B + 1, :], ALU.subtract).then_inc(*d_ready[b].inc)
                            dve.wait_ge(*zt_done[b].n((LEV - 1) * i + l))
                            dve.wait_ge(*dt_ready[b].n(LEV * i + l))
                            nc.vector.tensor_tensor(dt[:, b, :], dt[:, b, :], ps[:, B + 2, :], ALU.subtract).then_inc(*dt_ready[b].inc)
                    for b in range(2):
                        B = 4 * b
                        dve.wait_ge(*ks_done[b].n(i + 1))
                        dve.wait_ge(*vb_ready[b].n(i + 1))
                        for h in range(GH):
                            ins = nc.vector.scalar_tensor_tensor(r[:, b, hs(h)], ps[:, B + 1, hs(h)], per_head(m.nbe, h), vb[:, b, hs(h)], ALU.mult, ALU.add)
                        ins.then_inc(*r_ready[b].inc)
                        dve.wait_ge(*ds_done[b].n(i + 1))
                        dve.wait_ge(*o_done[b].n(i + 1))
                        for h in range(GH):
                            ins = nc.vector.scalar_tensor_tensor(state[:, hs(h)], state[:, hs(h)], per_head(m.sdec, h), ps[:, B + 3, hs(h)], ALU.mult, ALU.add)
                        ins.then_inc(*s_ready[b].inc)
                        dve.wait_ge(*o_ready[b].n(i + 1))
                        link(nc.vector.tensor_tensor(o2[:, b, :], o[:, b, :], o[:, b, :], ALU.mult))
                        nc.vector.tensor_reduce(st[:, b, :], h4(o2[:, b, :]), AX.X, ALU.add).then_inc(*osq_ready[b].inc)
                        link(nc.vector.tensor_tensor(h4(o[:, b, :]), h4(o[:, b, :]), gain[:, :].unsqueeze(1).to_broadcast([P, GH, P]), ALU.mult))
                        dve.wait_ge(*z_in[b].n(i + 1))
                        link(nc.vector.tensor_tensor(o[:, b, :], o[:, b, :], z[:, b, :], ALU.mult))
                        dve.wait_ge(*std_ready[b].n(i + 1))
                        link(nc.vector.reciprocal(st[:, b, :], st[:, b, :]))
                        nc.vector.tensor_tensor(h4(o[:, b, :]), h4(o[:, b, :]), st[:, b, :].unsqueeze(2).to_broadcast([P, GH, P]), ALU.mult).then_inc(*y_out_ready[b].inc)
                        dve.wait_ge(*s_ready[b].n(i + 1))
def bias_tables(nc, m, a):
    with Room(nc, "bt") as R:
        rel = R.sb("rel", [NE, AH])
        hot = R.sb("hot", [NE, NB * BIAS_W])
        off = R.sb("off", [AH, NB * BIAS_W])
        rows = R.sb("rows", [AH, NB * BIAS_W])
        flip = R.sb("flip", [P, NB, AH, 2 * P])
        small_in, rows_out, flip_in = R.sig("small_in", 16), R.sig("rows_out", 16), R.sig("flip_in", 16)
        rows_done, rows_ready, done, read = R.sig("rows_done"), R.sig("rows_ready"), R.sig("done"), R.sig("read")
        ps = m.ps
        with R.block() as block:
            @block.sync
            def _(sp):
                sp.dma_start(rel[:, :], a["rel_bias"]).then_inc(*small_in.inc)
                sp.dma_start(hot[:, :], a["bucket_one"]).then_inc(*small_in.inc)
                sp.dma_start(off[:, :], a["bucket_off"]).then_inc(*small_in.inc)
                sp.wait_ge(*rows_ready.n(NB))
                sp.dma_start(m.bias_d, rows[:, :]).then_inc(*rows_out.inc)
                sp.wait_ge(*rows_out.n(1))
                for n in range(NB):
                    src = bass.AP(m.bias_d.tensor, n * BIAS_W, [[1, P], [NB * BIAS_W, AH], [1, 2 * P]])
                    sp.dma_start(flip[:, n, :, :], src).then_inc(*flip_in.inc)

            @block.tensor
            def _(pe):
                pe.wait_ge(*small_in.n(3))
                for n in range(NB):
                    nc.tensor.matmul(ps[0:AH, n, 0:BIAS_W], rel[:, :], hot[:, n * BIAS_W:(n + 1) * BIAS_W], start=True, stop=True).then_inc(*rows_done.inc)
                pe.wait_ge(*flip_in.n(NB))
                for n in range(NB):
                    pe.wait_ge(*read.n(n))
                    for h in range(0, AH, 2):
                        last = nc.tensor.matmul(ps[:, 4 + h // 2, :], m.cst[:, C_FLIP:C_FLIP + P], flip[:, n, h:h + 2, :].rearrange("p h k -> p (h k)"), start=True, stop=True)
                    last.then_inc(*done.inc)

            @block.vector
            def _(dve):
                for n in range(NB):
                    dve.wait_ge(*rows_done.n(n + 1))
                    s = slice(n * BIAS_W, (n + 1) * BIAS_W)
                    nc.vector.tensor_tensor(rows[:, s], ps[0:AH, n, 0:BIAS_W], off[:, s], ALU.add).then_inc(*rows_ready.inc)
                for n in range(NB):
                    dve.wait_ge(*done.n(n + 1))
                    nc.vector.tensor_copy(m.bias[:, n, :, :].rearrange("p h k -> p (h k)"), ps[:, 4:8, :].rearrange("p b n -> p (b n)")).then_inc(*read.inc)


def attention(nc, m, a):
    RUNS = (
        (0, 0, 1, (False,), lambda i, j: 0),
        (1, 0, NT // 2 - 1, (True, True), lambda i, j: i * (2 * P) + (1 + j) * P),
        (NT - 1, 0, 1, (True,), lambda i, j: (NT - 1) * P),
        (NT, 1, BR[1][0], (False, True, True, True), lambda i, j: i + j * BR[1][0] * P),
        (2 * NT, 2, BR[2][0] // 2, (False, False), lambda i, j: i * 2 + j),
    )
    STEPS = AH // 2
    UNITS = NB * NT

    def turns(eng, times):
        if times > 1:
            with eng.Fori(0, times) as i:
                yield i
        elif times == 1:
            yield 0

    def numbers(u0, i, j, n):
        return (u0 + j) % 2, i * (n // 2) + (u0 + j) // 2, i * (2 * n) + 2 * (u0 + j)

    with Room(nc, "at") as R:
        qk = R.sb("qk", [P, 2 * STEPS, T])
        qb = R.sb("qb", [P, 2, STEPS, P])
        kb = R.sb("kb", [P, 2, STEPS, 2 * P])
        v = R.sb("v", [P, 2, 2, AW])
        p = R.sb("p", [P, 2, 2, 2 * P])
        pt = R.sb("pt", [P, 2, 2, 2, P])
        o = R.sb("o", [P, 2, AW + 2 * AH])
        ps = m.ps
        qk_in = R.sig("qk_in", 16)
        v_in, out = R.sigs("v_in", 2, 16), R.sigs("out", 2, 16)
        q_ready, k_ready, o_ready = R.sigs("q_ready"), R.sigs("k_ready"), R.sigs("o_ready")
        s_done, s_read, max_ready, p_ready = R.sigs("s_done", credit=3), R.sigs("s_read"), R.sigs("max_ready"), R.sigs("p_ready")
        pt_done, pt_ready, pv_done = R.sigs("pt_done"), R.sigs("pt_ready"), R.sigs("pv_done", credit=3)
        with R.block() as block:
            @block.sync
            def _(sp):
                sp.dma_start(qk[:, :, :], m.ch_d[NCONV:m.NCH, :, :].rearrange("c p n -> p c n")).then_inc(*qk_in.inc)

                def load(u0, i, j, types, branch, first):
                    b, n, n2 = numbers(u0, i, j, len(types))
                    dil = BR[branch][0]
                    sp.wait_ge(*pv_done[1].n(n2 - 2))
                    if types[j]:
                        src = bass.AP(m.v_d.tensor, (first(i, j) - P * dil) * AW, [[dil * AW, P], [P * dil * AW, 2], [1, AW]])
                        sp.dma_start(v[:, b, :, :], src).then_inc(*v_in[b].inc)
                    else:
                        src = bass.AP(m.v_d.tensor, first(i, j) * AW, [[dil * AW, P], [1, AW]])
                        sp.dma_start(v[:, b, 1, :], src).then_inc(*v_in[b].inc)

                for u0, branch, times, types, first in RUNS:
                    for i in turns(sp, times):
                        for j in range(len(types)):
                            load(u0, i, j, types, branch, first)

            @block.gpsimd
            def _(pool):
                pool.wait_ge(*qk_in.n(1))
                for u0, branch, times, types, first in RUNS:
                    dil = BR[branch][0]
                    for i in turns(pool, times):
                        for j, before in enumerate(types):
                            b, n, n2 = numbers(u0, i, j, len(types))
                            pool.wait_ge(*s_done[1].n(n2 - 2))
                            nc.gpsimd.tensor_copy(qb[:, b, :, :], qk[:, 0:STEPS, bass.DynSlice(first(i, j), P, step=dil)]).then_inc(*q_ready[b].inc)
                            lo = 0 if before else P
                            nc.gpsimd.tensor_copy(kb[:, b, :, lo:], qk[:, STEPS:, bass.DynSlice(first(i, j) - (P - lo) * dil, 2 * P - lo, step=dil)]).then_inc(*k_ready[b].inc)

            @block.tensor
            def _(pe):
                def scores(u0, i, j, s, types):
                    b, n, n2 = numbers(u0, i, j, len(types))
                    lo = 0 if types[j] else P
                    if s == 0:
                        pe.wait_ge(*q_ready[b].n(n + 1))
                        pe.wait_ge(*k_ready[b].n(n + 1))
                    pe.wait_ge(*s_read[s % 2].n(n2 + s // 2))
                    for h in range(2):
                        r = slice(h * DH, (h + 1) * DH)
                        last = nc.tensor.matmul(ps[:, 2 * (s % 2) + h, lo:2 * P], qb[r, b, s, :], kb[r, b, s, lo:], start=True, stop=True)
                    last.then_inc(*s_done[s % 2].inc)

                def turn(u0, i, types, last_turn):
                    steps = [(j, s) for j in range(len(types)) for s in range(STEPS)]
                    for at, (j, s) in enumerate(steps):
                        b, n, n2 = numbers(u0, i, j, len(types))
                        blocks = range(0 if types[j] else 1, 2)
                        e, c = s % 2, n2 + s // 2
                        pe.wait_ge(*p_ready[e].n(c + 1))
                        pe.wait_ge(*pt_ready[e].n(c))
                        for h in range(2):
                            for k in blocks:
                                last = nc.tensor.transpose(ps[:, 4 + e, (h * 2 + k) * P:(h * 2 + k + 1) * P], p[:, e, h, k * P:(k + 1) * P], m.ident)
                        last.then_inc(*pt_done[e].inc)
                        if at + 2 < len(steps):
                            scores(u0, i, *steps[at + 2], types)
                        elif not last_turn:
                            scores(u0, i + 1, *steps[at + 2 - len(steps)], types)
                        if s == 0:
                            pe.wait_ge(*v_in[b].n(n + 1))
                            pe.wait_ge(*o_ready[b].n(n))
                        pe.wait_ge(*pt_ready[e].n(c + 1))
                        for h in range(2):
                            for k in blocks:
                                w = slice((2 * s + h) * DH, (2 * s + h + 1) * DH)
                                last = nc.tensor.matmul(ps[:, 6 + b, w], pt[:, e, h, k, :], v[:, b, k, w], start=(k == blocks[0]), stop=(k == 1))
                        last.then_inc(*pv_done[e].inc)

                for u0, branch, times, types, first in RUNS:
                    scores(u0, 0, 0, 0, types)
                    scores(u0, 0, 0, 1, types)
                    for i in turns(pe, times - 1):
                        turn(u0, i, types, False)
                    turn(u0, times - 1, types, True)

            @block.vector
            def _(dve):
                for u0, branch, times, types, first in RUNS:
                    for i in turns(dve, times):
                        for j, before in enumerate(types):
                            b, n, n2 = numbers(u0, i, j, len(types))
                            lo = 0 if before else P
                            dve.wait_ge(*out[b].n(n))
                            for s in range(STEPS):
                                e, c = s % 2, n2 + s // 2
                                dve.wait_ge(*s_done[e].n(c + 1))
                                dve.wait_ge(*pt_done[e].n(c))
                                nc.vector.scalar_tensor_tensor(p[:, e, :, lo:], ps[:, 2 * e:2 * e + 2, lo:2 * P], DH ** -0.5, m.bias[:, branch, 2 * s:2 * s + 2, lo:], ALU.mult, ALU.add).then_inc(*s_read[e].inc)
                                dve.wait_ge(*s_read[e].n(c + 1))
                                nc.vector.tensor_reduce(o[:, b, AW + 2 * s:AW + 2 * s + 2], p[:, e, :, lo:], AX.X, ALU.max, negate=True).then_inc(*max_ready[e].inc)
                            dve.wait_ge(*pv_done[1].n(n2 + 2))
                            nc.vector.tensor_copy(o[:, b, 0:AW], ps[:, 6 + b, :]).then_inc(*o_ready[b].inc)

            @block.scalar
            def _(act):
                for u0, branch, times, types, first in RUNS:
                    dil = BR[branch][0]
                    for i in turns(act, times):
                        for j, before in enumerate(types):
                            b, n, n2 = numbers(u0, i, j, len(types))
                            lo = 0 if before else P
                            for s in range(STEPS):
                                e, c = s % 2, n2 + s // 2
                                act.wait_ge(*max_ready[e].n(c + 1))
                                for h in range(2):
                                    at = AW + 2 * s + h
                                    ins = nc.scalar.activation(p[:, e, h, lo:], p[:, e, h, lo:], ACT.Exp, bias=o[:, b, at:at + 1], accum_out=o[:, b, at + AH:at + AH + 1])
                                ins.then_inc(*p_ready[e].inc)
                                act.wait_ge(*pt_done[e].n(c + 1))
                                act.wait_ge(*pv_done[e].n(c))
                                nc.scalar.copy(pt[:, e, :, lo // P:, :], ps[:, 4 + e, :].rearrange("p (h k n) -> p h k n", h=2, k=2)[:, :, lo // P:, :]).then_inc(*pt_ready[e].inc)
                            act.wait_ge(*o_ready[b].n(n + 1))
                            dst = bass.AP(m.o_d.tensor, branch * T * (AW + 2 * AH) + first(i, j) * (AW + 2 * AH), [[dil * (AW + 2 * AH), P], [1, AW + 2 * AH]])
                            act.dma_start(dst, o[:, b, :]).then_inc(*out[b].inc)
                for b in range(2):
                    act.wait_ge(*out[b].n(UNITS // 2))
def steps(eng, last):
    pairs = (last - 1) // 2
    yield 0, 0, 0
    with eng.Fori(0, pairs) as i:
        yield i * 2 + 1, 1, i
        yield i * 2 + 2, 0, i + 1
    for t in range(2 * pairs + 1, last + 1):
        yield t, t % 2, t // 2


def is_tile(t, n):
    return isinstance(t, int) and t == n


def after(b, q):
    return 1 - b, q + b


def before(b, q):
    return 1 - b, q - 1 + b


def mix_out(nc, m, a):
    OW = AW + 2 * AH
    with Room(nc, "mo") as R:
        w = R.sb("w", [P, KD, D])
        wr = R.sb("wr", [P, KD, NG + NE])
        gain = R.sb("gain", [P, AW])
        eps = R.sb("eps", [P, 1])
        y = R.sb("y", [P, 2, 2 * GW])
        o = R.sb("o", [P, 2, NB, OW])
        x = R.sb("x", [P, 2, D])
        wt = R.sb("wt", [P, 2, NB, AH])
        ws = R.sb("ws", [P, 2, NB, AH])
        lo = R.sb("lo", [P, 2, AH])
        den = R.sb("den", [P, 2, AH])
        ss = R.sb("ss", [P, 2, 2])
        yt = R.sb("yt", [P, 2, KD, P])
        x2 = R.sb("x2", [P, 2, D])
        h = R.sb("h", [P, 2, D])
        ht = R.sb("ht", [P, 2, KD, P])
        junk = R.sb("junk", [P, D])
        ps = m.ps
        S = R.sigs
        w_in, eps_set = R.sig("w_in", 16), R.sig("eps_set")
        tile_in = S("tile_in", 2, 16)
        diff_ready, exp_ready, sum_ready, sq_ready, y_ready = S("diff_ready"), S("exp_ready"), S("sum_ready"), S("sq_ready"), S("y_ready")
        yt_done, yt_ready, w_done = S("yt_done"), S("yt_ready"), S("w_done")
        x2_ready, xsq_ready, h_ready = S("x2_ready"), S("xsq_ready"), S("h_ready")
        x2_out, h_out = S("x2_out", 2, 16), S("h_out", 2, 16)
        ht_done, ht_ready, lg_done, lg_ready = S("ht_done"), S("ht_ready"), S("lg_done"), S("lg_ready")
        dve_self, act_self = R.plain("dve_self"), R.plain("act_self")
        gate, gain2, shift2 = m.mod[:, 2 * D:3 * D], m.mod[:, 4 * D:5 * D], m.mod[:, 3 * D:4 * D]
        with R.block() as block:
            @block.sync
            def _(sp):
                sp.dma_start(gain[:, :], row_bc(a["attn_norm"], AW)).then_inc(*w_in.inc)
                sp.dma_start(w[:, :, :], a["w_out"]).then_inc(*w_in.inc)
                sp.dma_start(wr[:, :, :], a["w_router"]).then_inc(*w_in.inc)
                with sp.Fori(0, NT // 2) as i:
                    for b in range(2):
                        sp.wait_ge(*x2_ready[b].n(i))
                        sp.wait_ge(*yt_done[b].n(i))
                        sp.dma_start(y[:, b, 0:GW], one(m.y_d, 2 * i + b)).then_inc(*tile_in[b].inc)
                        src = m.o_d[:, bass.ds(2 * i + b, 1), :, :].rearrange("n a p w -> p (n a) w")
                        sp.dma_start(o[:, b, :, :], src).then_inc(*tile_in[b].inc)
                        sp.dma_start(x[:, b, :], one(a["x"], 2 * i + b)).then_inc(*tile_in[b].inc)

            @block.tensor
            def _(pe):
                def transposes(src, bank, done):
                    for k in range(KD):
                        last = nc.tensor.transpose(ps[:, bank + k // 4, (k % 4) * P:(k % 4 + 1) * P], src[:, k * P:(k + 1) * P], m.ident)
                    last.then_inc(*done.inc)

                def turn_y(b, q):
                    pe.wait_ge(*y_ready[b].n(q + 1))
                    b1, q1 = before(b, q)
                    pe.wait_ge(*yt_ready[b1].n(q1 + 1))
                    transposes(y[:, b, :], 0, yt_done[b])

                def logits(b, q):
                    pe.wait_ge(*h_ready[b].n(q + 1))
                    b1, q1 = before(b, q)
                    pe.wait_ge(*lg_ready[b1].n(q1 + 1))
                    transposes(h[:, b, :], 6, ht_done[b])
                    pe.wait_ge(*ht_ready[b].n(q + 1))
                    for k in range(KD):
                        last = nc.tensor.matmul(ps[:, 6, 0:NG + NE], ht[:, b, k, :], wr[:, k, :], start=(k == 0), stop=(k == KD - 1))
                    last.then_inc(*lg_done[b].inc)

                pe.wait_ge(*w_in.n(3))
                turn_y(0, 0)
                for t, b, q in steps(pe, NT - 1):
                    pe.wait_ge(*yt_ready[b].n(q + 1))
                    pe.wait_ge(*x2_ready[b].n(q))
                    for n in range(2):
                        for k in range(KD):
                            last = nc.tensor.matmul(ps[:, 2 + 2 * b + n, :], yt[:, b, k, :], w[:, k, n * BANK:(n + 1) * BANK], start=(k == 0), stop=(k == KD - 1))
                    last.then_inc(*w_done[b].inc)
                    if not is_tile(t, NT - 1):
                        turn_y(*after(b, q))
                    if not is_tile(t, 0):
                        logits(*before(b, q))
                logits(1, NT // 2 - 1)

            @block.vector
            def _(dve):
                link = Chain(dve, dve_self)
                nc.vector.memset(eps[:, :], EPS).then_inc(*eps_set.inc)
                dve.wait_ge(*w_in.n(3))

                def put_together(b, q):
                    low = o[:, b, :, AW:AW + AH]
                    dve.wait_ge(*tile_in[b].n(3 * q + 3))
                    link(nc.vector.tensor_tensor(lo[:, b, :], low[:, 0, :], low[:, 1, :], ALU.min))
                    link(nc.vector.tensor_tensor(lo[:, b, :], lo[:, b, :], low[:, 2, :], ALU.min))
                    nc.vector.tensor_tensor(wt[:, b, :, :], lo[:, b, :].unsqueeze(1).to_broadcast([P, NB, AH]), low, ALU.subtract).then_inc(*diff_ready[b].inc)
                    dve.wait_ge(*exp_ready[b].n(q + 1))
                    link(nc.vector.tensor_tensor(ws[:, b, :, :], wt[:, b, :, :], o[:, b, :, AW + AH:OW], ALU.mult))
                    link(nc.vector.tensor_reduce(den[:, b, :], ws[:, b, :, :].rearrange("p n h -> p h n"), AX.X, ALU.add))
                    link(nc.vector.reciprocal(den[:, b, :], den[:, b, :]))
                    link(nc.vector.tensor_tensor(wt[:, b, :, :], wt[:, b, :, :], den[:, b, :].unsqueeze(1).to_broadcast([P, NB, AH]), ALU.mult))
                    for n in range(NB):
                        on = o[:, b, n, 0:AW].rearrange("p (h d) -> p h d", h=AH)
                        ins = nc.vector.tensor_tensor(on, on, wt[:, b, n, :].unsqueeze(2).to_broadcast([P, AH, DH]), ALU.mult)
                    link(ins)
                    link(nc.vector.tensor_tensor(o[:, b, 0, 0:AW], o[:, b, 0, 0:AW], o[:, b, 1, 0:AW], ALU.add))
                    nc.vector.tensor_tensor(o[:, b, 0, 0:AW], o[:, b, 0, 0:AW], o[:, b, 2, 0:AW], ALU.add).then_inc(*sum_ready[b].inc)
                    dve.wait_ge(*sq_ready[b].n(q + 1))
                    link(nc.vector.reciprocal(ss[:, b, 0:1], ss[:, b, 0:1]))
                    nc.vector.scalar_tensor_tensor(y[:, b, GW:2 * GW], o[:, b, 0, 0:AW], ss[:, b, 0:1], gain[:, :], ALU.mult, ALU.mult).then_inc(*y_ready[b].inc)

                def residual(b, q):
                    dve.wait_ge(*w_done[b].n(q + 1))
                    dve.wait_ge(*x2_out[b].n(q))
                    link(nc.vector.tensor_tensor(x2[:, b, :], ps[:, 2 + 2 * b:4 + 2 * b, :].rearrange("p n w -> p (n w)"), gate, ALU.mult))
                    nc.vector.tensor_tensor(x2[:, b, :], x2[:, b, :], x[:, b, :], ALU.add).then_inc(*x2_ready[b].inc)
                    dve.wait_ge(*xsq_ready[b].n(q + 1))
                    link(nc.vector.reciprocal(ss[:, b, 1:2], ss[:, b, 1:2]))
                    dve.wait_ge(*h_out[b].n(q))
                    dve.wait_ge(*ht_done[b].n(q))
                    link(nc.vector.scalar_tensor_tensor(h[:, b, :], x2[:, b, :], ss[:, b, 1:2], gain2, ALU.mult, ALU.mult))
                    nc.vector.tensor_tensor(h[:, b, :], h[:, b, :], shift2, ALU.add).then_inc(*h_ready[b].inc)

                PT, RS = 9, 3
                put_together(0, 0)
                put_together(1, 0)
                residual(0, 0)
                with link.loop(NT // 2 - 1, 2 * (PT + RS)) as i:
                    put_together(0, i + 1)
                    residual(1, i)
                    put_together(1, i + 1)
                    residual(0, i + 1)
                residual(1, NT // 2 - 1)

            @block.scalar
            def _(act):
                link = Chain(act, act_self)
                act.wait_ge(*eps_set.n(1))
                act.wait_ge(*w_in.n(3))

                def put_together(b, q):
                    act.wait_ge(*diff_ready[b].n(q + 1))
                    nc.scalar.activation(wt[:, b, :, :], wt[:, b, :, :], ACT.Exp).then_inc(*exp_ready[b].inc)
                    act.wait_ge(*sum_ready[b].n(q + 1))
                    link(nc.scalar.activation(junk[:, 0:AW], o[:, b, 0, 0:AW], ACT.Square, accum_out=ss[:, b, 0:1]))
                    nc.scalar.activation(ss[:, b, 0:1], ss[:, b, 0:1], ACT.Sqrt, bias=eps[:, :], scale=1.0 / AW).then_inc(*sq_ready[b].inc)
                    act.wait_ge(*yt_done[b].n(q + 1))
                    act.wait_ge(*w_done[b].n(q))
                    nc.scalar.copy(yt[:, b, :, :].rearrange("p k n -> p (k n)"), ps[:, 0:2, :].rearrange("p k n -> p (k n)")).then_inc(*yt_ready[b].inc)

                def router(t, b, q):
                    act.wait_ge(*ht_done[b].n(q + 1))
                    act.wait_ge(*lg_done[b].n(q))
                    nc.scalar.copy(ht[:, b, :, :].rearrange("p k n -> p (k n)"), ps[:, 6:8, :].rearrange("p k n -> p (k n)")).then_inc(*ht_ready[b].inc)
                    act.wait_ge(*lg_done[b].n(q + 1))
                    nc.scalar.copy(m.lg[:, bass.ds(t * (NG + NE), NG + NE)], ps[:, 6, 0:NG + NE]).then_inc(*lg_ready[b].inc)

                def residual(t, b, q):
                    act.wait_ge(*x2_ready[b].n(q + 1))
                    link(nc.scalar.activation(junk[:, :], x2[:, b, :], ACT.Square, accum_out=ss[:, b, 1:2]))
                    nc.scalar.activation(ss[:, b, 1:2], ss[:, b, 1:2], ACT.Sqrt, bias=eps[:, :], scale=1.0 / D).then_inc(*xsq_ready[b].inc)
                    act.dma_start(one(m.x2_d, t), x2[:, b, :]).then_inc(*x2_out[b].inc)
                    act.wait_ge(*h_ready[b].n(q + 1))
                    act.dma_start(one(m.h_d, t), h[:, b, :]).then_inc(*h_out[b].inc)

                put_together(0, 0)
                put_together(1, 0)
                residual(0, 0, 0)
                with link.loop(NT // 2 - 1, 4) as i:
                    put_together(0, i + 1)
                    router(i * 2, 0, i)
                    residual(i * 2 + 1, 1, i)
                    put_together(1, i + 1)
                    router(i * 2 + 1, 1, i)
                    residual(i * 2 + 2, 0, i + 1)
                router(NT - 2, 0, NT // 2 - 1)
                residual(NT - 1, 1, NT // 2 - 1)
                router(NT - 1, 1, NT // 2 - 1)
                for b in range(2):
                    act.wait_ge(*x2_out[b].n(NT // 2))
                    act.wait_ge(*h_out[b].n(NT // 2))
                    act.wait_ge(*lg_ready[b].n(NT // 2))
def route(nc, m, a):
    LW = NG + NE
    BIG = 64.0
    with Room(nc, "ro") as R:
        gm = R.sb("gm", [P, NT])
        eg = R.sb("eg", [P, NT, NG])
        gs = R.sb("gs", [P, NT])
        gone = R.sb("gone", [P, NT, NG])
        gi = R.sb("gi", [P, NT])
        el = R.sb("el", [P, NT, NE])
        t1 = R.sb("t1", [P, NT, NE])
        mx = R.sb("mx", [P, 2, NT])
        idx = R.sb("idx", [P, NT])
        hot = R.sb("hot", [P, 2, NT, NE])
        both = R.sb("both", [P, NT, NE])
        e2 = R.sb("e2", [P, NT])
        carry = R.sb("carry", [P, NT + 1, NE])
        pad = R.sb("pad", [P, NE])
        padi = R.sb("padi", [P, NE], I32)
        ends = R.sb("ends", [P, NE])
        destf = R.sb("destf", [P, 2, NT])
        pos = R.sb("pos", [P, 2, NT], I32)
        part = R.sb("part", [P, 2, NT], I32)
        cmp = R.sb("cmp", [P, NBLK, NE])
        bef = R.sb("bef", [P, NBLK])
        toki = R.sb("toki", [P, NT], I32)
        zero = R.sb("zero", [P, NBLK], I32)
        ps = m.ps
        dve_self = R.plain("dve_self")
        gsub_ready, gexp_ready, esub_ready, eexp_ready = R.sig("gsub_ready"), R.sig("gexp_ready"), R.sig("esub_ready"), R.sig("eexp_ready")
        both_ready, ranks_done, zero_set, zero_out, pos_ready = R.sig("both_ready"), R.sig("ranks_done"), R.sig("zero_set"), R.sig("zero_out", 16), R.sig("pos_ready")
        tok_out, tok_in = R.plain("tok_out"), R.sig("tok_in", 16)
        tok_all = R.sig("tok_all")
        lg = m.lg[:, :].rearrange("p (t n) -> p t n", n=LW)
        gl = lg[:, :, 0:NG]

        def over(ap, n):
            return ap.unsqueeze(2).to_broadcast([P, ap.shape[1], n])

        def iota(n):
            return m.cst[:, C_IOTA:C_IOTA + n].unsqueeze(1).to_broadcast([P, NT, n])

        with R.block() as block:
            @block.sync
            def _(sp):
                sp.wait_ge(*zero_set.n(1))
                sp.dma_start(m.slot_tok_d, zero[:, :]).then_inc(*zero_out.inc)
                sp.wait_ge(*tok_all.n(1))
                sp.dma_start(m.slot_tok[:, :], m.slot_tok_d).then_inc(*tok_in.inc)
                sp.wait_ge(*tok_in.n(1))

            @block.vector
            def _(dve):
                link = Chain(dve, dve_self)
                V = nc.vector

                def first_of(one_hot, values, top, n):
                    link(V.tensor_tensor(one_hot, values, over(top, n), ALU.is_equal))
                    link(V.tensor_scalar(one_hot, one_hot, -BIG, BIG, ALU.mult, ALU.add))
                    link(V.tensor_tensor(one_hot, one_hot, iota(n), ALU.add))
                    link(V.tensor_reduce(idx[:, :], one_hot, AX.X, ALU.min))
                    link(V.tensor_tensor(one_hot, iota(n), over(idx[:, :], n), ALU.is_equal))

                V.memset(zero[:, :], 0).then_inc(*zero_set.inc)
                link(V.tensor_reduce(gm[:, :], gl, AX.X, ALU.max))
                V.tensor_tensor(eg[:, :, :], gl, over(gm[:, :], NG), ALU.subtract).then_inc(*gsub_ready.inc)
                first_of(gone[:, :, :], gl, gm[:, :], NG)
                dve.wait_ge(*gexp_ready.n(1))
                link(V.tensor_reduce(gs[:, :], eg[:, :, :], AX.X, ALU.add))
                link(V.tensor_scalar(gone[:, :, :], gone[:, :, :], -NEG, NEG, ALU.mult, ALU.add))
                for g in range(NG):
                    ins = V.tensor_tensor(el[:, :, g * EG:(g + 1) * EG], lg[:, :, NG + g * EG:NG + (g + 1) * EG], gone[:, :, g:g + 1].to_broadcast([P, NT, EG]), ALU.add)
                link(ins)
                for n in range(2):
                    link(V.tensor_reduce(mx[:, n, :], el[:, :, :], AX.X, ALU.max))
                    first_of(hot[:, n, :, :], el[:, :, :], mx[:, n, :], NE)
                    if n == 0:
                        link(V.scalar_tensor_tensor(el[:, :, :], hot[:, 0, :, :], 2 * NEG, el[:, :, :], ALU.mult, ALU.add))
                V.tensor_tensor(both[:, :, :], hot[:, 0, :, :], hot[:, 1, :, :], ALU.add).then_inc(*both_ready.inc)
                V.tensor_tensor(e2[:, :], mx[:, 1, :], mx[:, 0, :], ALU.subtract).then_inc(*esub_ready.inc)
                dve.wait_ge(*eexp_ready.n(1))
                link(V.scalar_tensor_tensor(gs[:, :], e2[:, :], 1.0, gs[:, :], ALU.add, ALU.mult))
                link(V.reciprocal(m.gate[:, 0, :], gs[:, :]))
                link(V.tensor_tensor(m.gate[:, 1, :], m.gate[:, 0, :], e2[:, :], ALU.mult))
                dve.wait_ge(*ranks_done.n(1))
                link(V.memset(carry[:, 0, :], 0.0))
                for t in range(NT):
                    link(V.tensor_tensor(carry[:, t + 1, :], carry[:, t, :], ps[:, 1, t * NE:(t + 1) * NE], ALU.add))
                link(V.tensor_scalar(pad[:, :], carry[:, NT, :], float(P - 1), None, ALU.add))
                link(V.tensor_copy(padi[:, :], pad[:, :]))
                link(V.tensor_scalar(padi[:, :], padi[:, :], 7, 7, ALU.arith_shift_right, ALU.logical_shift_left))
                link(V.tensor_copy(pad[:, :], padi[:, :]))
                link(V.tensor_tensor_scan(ends[:, :], m.ones[:, 0:NE], pad[:, :], 0.0, ALU.mult, ALU.add))
                link(V.tensor_tensor(pad[:, :], ends[:, :], pad[:, :], ALU.subtract))
                link(V.tensor_tensor(el[:, :, :], ps[:, 0, :].rearrange("p (t e) -> p t e", e=NE), carry[:, 0:NT, :], ALU.add))
                link(V.tensor_tensor(el[:, :, :], el[:, :, :], pad[:, :].unsqueeze(1).to_broadcast([P, NT, NE]), ALU.add))
                for n in range(2):
                    link(V.tensor_tensor(t1[:, :, :], el[:, :, :], hot[:, n, :, :], ALU.mult))
                    link(V.tensor_reduce(destf[:, n, :], t1[:, :, :], AX.X, ALU.add))
                link(V.tensor_copy(m.dest[:, :, :], destf[:, :, :]))
                link(V.tensor_scalar(part[:, :, :], m.dest[:, :, :], 7, None, ALU.arith_shift_right))
                link(V.tensor_scalar(pos[:, :, :], m.dest[:, :, :], P - 1, None, ALU.bitwise_and))
                link(V.tensor_copy(destf[:, :, :], part[:, :, :]))
                link(V.scalar_tensor_tensor(destf[:, :, :], pos[:, :, :], float(NBLK), destf[:, :, :], ALU.mult, ALU.add))
                link(V.tensor_copy(toki[:, :], m.cst[:, C_TOK:C_TOK + NT]))
                V.tensor_copy(pos[:, :, :], destf[:, :, :]).then_inc(*pos_ready.inc)
                link(V.tensor_tensor(cmp[:, :, :], m.cst[:, C_BLK:C_BLK + NBLK].unsqueeze(2).to_broadcast([P, NBLK, NE]), ends[:, :].unsqueeze(1).to_broadcast([P, NBLK, NE]), ALU.is_ge))
                link(V.tensor_reduce(bef[:, :], cmp[:, :, :], AX.X, ALU.add))
                link(V.tensor_scalar(bef[:, :], bef[:, :], float(NE - 1), None, ALU.min))
                link(V.tensor_copy(m.blk_e[:, :], bef[:, :]))

            @block.scalar
            def _(act):
                act.wait_ge(*gsub_ready.n(1))
                nc.scalar.activation(eg[:, :, :], eg[:, :, :], ACT.Exp).then_inc(*gexp_ready.inc)
                act.wait_ge(*esub_ready.n(1))
                nc.scalar.activation(e2[:, :], e2[:, :], ACT.Exp).then_inc(*eexp_ready.inc)

            @block.tensor
            def _(pe):
                pe.wait_ge(*both_ready.n(1))
                rows = both[:, :, :].rearrange("p t e -> p (t e)")
                nc.tensor.matmul(ps[:, 0, :], m.cst[:, C_US:C_US + P], rows, start=True, stop=True)
                nc.tensor.matmul(ps[:, 1, :], m.ones, rows, start=True, stop=True).then_inc(*ranks_done.inc)

            @block.gpsimd
            def _(pool):
                pool.wait_ge(*pos_ready.n(1))
                pool.wait_ge(*zero_out.n(1))
                flat = m.slot_tok_d.rearrange("p b -> (p b)").unsqueeze(1)
                for t in range(NT):
                    for n in range(2):
                        pool.indirect_dma_start(out=flat, out_offset=bass.IndirectOffsetOnAxis(ap=pos[:, n, t:t + 1].bitcast(U32), axis=0),
                                                in_=toki[:, t:t + 1], in_offset=None).then_inc(tok_out, 16)
                pool.wait_ge(tok_out, 2 * NT * 16)
                pool.sem_inc(*tok_all.inc)


def experts(nc, m, a):
    with Room(nc, "ex") as R:
        idx = R.sb("idx", [P, 2], I32)
        xg = R.sb("xg", [P, 2, D])
        xt = R.sb("xt", [P, 2, KD, P])
        wgu = R.sb("wgu", [P, 2, KD, 2 * DE])
        wd = R.sb("wd", [P, 2, DE // P, D])
        sg = R.sb("sg", [P, 2, DE])
        hid = R.sb("hid", [P, 2, DE])
        hidt = R.sb("hidt", [P, 2, DE // P, P])
        y = R.sb("y", [P, 2, D])
        ps = m.ps
        S = R.sigs
        idx_ready, xg_in, seen = S("idx_ready"), [R.plain("xg_in0"), R.plain("xg_in1")], R.plain("seen")
        wgu_in, wd_in = S("wgu_in", 2, 16), S("wd_in", 2, 16)
        xt_done, xt_ready, gu_done, sg_ready, hid_ready = S("xt_done"), S("xt_ready"), S("gu_done"), S("sg_ready"), S("hid_ready")
        ht_done, ht_ready, y_done, ya_ready, yb_ready, out = S("ht_done"), S("ht_ready"), S("y_done"), S("ya_ready"), S("yb_ready"), S("out", 2, 16)
        last_b = (NBLK - 1) % 2
        with R.block() as block:
            @block.sync
            def _(sp):
                for t, b, q in steps(sp, NBLK - 1):
                    e = sp.value_load(m.blk_e[0:1, bass.ds(t, 1)], min_val=0, max_val=NE - 1)
                    sp.wait_ge(*gu_done[b].n(q))
                    sp.dma_start(wgu[:, b, :, :], one(a["w_gate_up"], e)).then_inc(*wgu_in[b].inc)
                    sp.wait_ge(*y_done[b].n(q))
                    sp.dma_start(wd[:, b, :, :], one(a["w_down"], e)).then_inc(*wd_in[b].inc)

            @block.gpsimd
            def _(pool):
                rows = m.h_d.rearrange("t p n -> (t p) n")
                for t, b, q in steps(pool, NBLK - 1):
                    pool.wait_ge(*xt_done[b].n(q))
                    pool.sem_inc(seen, 1)
                    pool.wait_ge(*idx_ready[b].n(q + 1))
                    pool.sem_inc(seen, 1)
                    pool.indirect_dma_start(out=xg[:, b, :], out_offset=None, in_=rows,
                                            in_offset=bass.IndirectOffsetOnAxis(ap=idx[:, b:b + 1].bitcast(U32), axis=0)).then_inc(xg_in[b], 16)

            @block.tensor
            def _(pe):
                def turn_x(b, q):
                    pe.wait_ge(xg_in[b], q * 16 + 16)
                    b1, q1 = before(b, q)
                    pe.wait_ge(*xt_ready[b1].n(q1 + 1))
                    for k in range(KD):
                        last = nc.tensor.transpose(ps[:, k // 4, (k % 4) * P:(k % 4 + 1) * P], xg[:, b, k * P:(k + 1) * P], m.ident)
                    last.then_inc(*xt_done[b].inc)

                def down(b, q):
                    pe.wait_ge(*ht_ready[b].n(q + 1))
                    pe.wait_ge(*wd_in[b].n(q + 1))
                    b1, q1 = before(b, q)
                    pe.wait_ge(*ya_ready[b1].n(q1 + 1))
                    pe.wait_ge(*yb_ready[b1].n(q1 + 1))
                    for n in range(2):
                        for k in range(DE // P):
                            last = nc.tensor.matmul(ps[:, 6 + n, :], hidt[:, b, k, :], wd[:, b, k, n * BANK:(n + 1) * BANK], start=(k == 0), stop=(k == DE // P - 1))
                    last.then_inc(*y_done[b].inc)

                turn_x(0, 0)
                for t, b, q in steps(pe, NBLK - 1):
                    pe.wait_ge(*xt_ready[b].n(q + 1))
                    pe.wait_ge(*wgu_in[b].n(q + 1))
                    pe.wait_ge(*hid_ready[b].n(q))
                    for k in range(KD):
                        last = nc.tensor.matmul(ps[:, 2 + b, :], xt[:, b, k, :], wgu[:, b, k, :], start=(k == 0), stop=(k == KD - 1))
                    last.then_inc(*gu_done[b].inc)
                    if not is_tile(t, NBLK - 1):
                        turn_x(*after(b, q))
                    if not is_tile(t, 0):
                        down(*before(b, q))
                    pe.wait_ge(*hid_ready[b].n(q + 1))
                    b1, q1 = before(b, q)
                    pe.wait_ge(*ht_ready[b1].n(q1 + 1))
                    for k in range(DE // P):
                        last = nc.tensor.transpose(ps[:, 4, k * P:(k + 1) * P], hid[:, b, k * P:(k + 1) * P], m.ident)
                    last.then_inc(*ht_done[b].inc)
                down(last_b, NBLK // 2)

            @block.scalar
            def _(act):
                def take_x(b, q):
                    act.wait_ge(*xt_done[b].n(q + 1))
                    act.wait_ge(*gu_done[b].n(q))
                    nc.scalar.copy(xt[:, b, :, :].rearrange("p k n -> p (k n)"), ps[:, 0:2, :].rearrange("p k n -> p (k n)")).then_inc(*xt_ready[b].inc)

                def take_y(b, q):
                    act.wait_ge(*y_done[b].n(q + 1))
                    act.wait_ge(*out[b].n(q))
                    nc.scalar.copy(y[:, b, 0:BANK], ps[:, 6, :]).then_inc(*ya_ready[b].inc)

                def store_y(t, b, q):
                    act.wait_ge(*ya_ready[b].n(q + 1))
                    act.wait_ge(*yb_ready[b].n(q + 1))
                    act.dma_start(one(m.ys_d, t), y[:, b, :]).then_inc(*out[b].inc)

                take_x(0, 0)
                for t, b, q in steps(act, NBLK - 1):
                    act.wait_ge(*gu_done[b].n(q + 1))
                    act.wait_ge(*hid_ready[b].n(q))
                    nc.scalar.activation(sg[:, b, :], ps[:, 2 + b, 0:DE], ACT.Silu).then_inc(*sg_ready[b].inc)
                    if not is_tile(t, NBLK - 1):
                        take_x(*after(b, q))
                    if not is_tile(t, 0):
                        take_y(*before(b, q))
                    act.wait_ge(*ht_done[b].n(q + 1))
                    act.wait_ge(*y_done[b].n(q))
                    nc.scalar.copy(hidt[:, b, :, :].rearrange("p k n -> p (k n)"), ps[:, 4, 0:DE]).then_inc(*ht_ready[b].inc)
                    if not is_tile(t, 0):
                        store_y(t - 1, *before(b, q))
                take_y(last_b, NBLK // 2)
                store_y(NBLK - 1, last_b, NBLK // 2)
                act.wait_ge(*out[0].n(NBLK // 2 + 1))
                act.wait_ge(*out[1].n(NBLK // 2))

            @block.vector
            def _(dve):
                def take_y(b, q):
                    dve.wait_ge(*ya_ready[b].n(q + 1))
                    nc.vector.tensor_copy(y[:, b, BANK:], ps[:, 7, :]).then_inc(*yb_ready[b].inc)

                def take_idx(t, b):
                    nc.vector.tensor_copy(idx[:, b:b + 1], m.slot_tok[:, bass.ds(t, 1)]).then_inc(*idx_ready[b].inc)

                take_idx(0, 0)
                take_idx(1, 1)
                for t, b, q in steps(dve, NBLK - 1):
                    if not is_tile(t, 0):
                        take_y(*before(b, q))
                    dve.wait_ge(*gu_done[b].n(q + 1))
                    dve.wait_ge(*sg_ready[b].n(q + 1))
                    dve.wait_ge(*ht_done[b].n(q))
                    nc.vector.tensor_tensor(hid[:, b, :], sg[:, b, :], ps[:, 2 + b, DE:], ALU.mult).then_inc(*hid_ready[b].inc)
                    if not (isinstance(t, int) and t + 2 >= NBLK):
                        dve.wait_ge(xg_in[b], q * 16 + 16)
                        take_idx(t + 2, b)
                take_y(last_b, NBLK // 2)


def finish(nc, m, a):
    with Room(nc, "fi") as R:
        idx = R.sb("idx", [P, 2, 2], I32)
        yg = R.sb("yg", [P, 2, 2, D])
        x = R.sb("x", [P, 2, D])
        gain = R.sb("gain", [P, D])
        o = R.sb("o", [P, 2, D])
        junk = R.sb("junk", [P, D])
        ss = R.sb("ss", [P, 2])
        eps = R.sb("eps", [P, 1])
        S = R.sigs
        gain_in, eps_set = R.sig("gain_in", 16), R.sig("eps_set")
        x_in, yg_in, seen = S("x_in", 2, 16), [R.plain("yg_in0"), R.plain("yg_in1")], R.plain("seen")
        idx_ready, scaled, sum_ready, sq_ready, o_ready, out = S("idx_ready"), S("scaled"), S("sum_ready"), S("sq_ready"), S("o_ready"), S("out", 2, 16)
        dve_self, act_self = R.plain("dve_self"), R.plain("act_self")
        gate = m.mod[:, 5 * D:6 * D]
        N = NT // 2
        with R.block() as block:
            @block.sync
            def _(sp):
                sp.dma_start(gain[:, :], row_bc(a["norm_final"], D)).then_inc(*gain_in.inc)
                with sp.Fori(0, N) as i:
                    for b in range(2):
                        sp.wait_ge(*sum_ready[b].n(i))
                        sp.dma_start(x[:, b, :], one(m.x2_d, 2 * i + b)).then_inc(*x_in[b].inc)

            @block.gpsimd
            def _(pool):
                rows = m.ys_d.rearrange("t p n -> (t p) n")
                with pool.Fori(0, N) as i:
                    for b in range(2):
                        pool.wait_ge(*sum_ready[b].n(i))
                        pool.sem_inc(seen, 1)
                        pool.wait_ge(*idx_ready[b].n(i + 1))
                        pool.sem_inc(seen, 1)
                        for n in range(2):
                            pool.indirect_dma_start(out=yg[:, b, n, :], out_offset=None, in_=rows,
                                                    in_offset=bass.IndirectOffsetOnAxis(ap=idx[:, b, n:n + 1].bitcast(U32), axis=0)).then_inc(yg_in[b], 16)

            @block.scalar
            def _(act):
                link = Chain(act, act_self)
                act.wait_ge(*eps_set.n(1))
                with link.loop(N, 2) as i:
                    for b in range(2):
                        act.wait_ge(yg_in[b], i * 32 + 32)
                        nc.scalar.activation(yg[:, b, 0, :], yg[:, b, 0, :], ACT.Copy, scale=m.gate[:, 0, bass.ds(2 * i + b, 1)]).then_inc(*scaled[b].inc)
                    for b in range(2):
                        act.wait_ge(*sum_ready[b].n(i + 1))
                        link(nc.scalar.activation(junk[:, :], o[:, b, :], ACT.Square, accum_out=ss[:, b:b + 1]))
                        nc.scalar.activation(ss[:, b:b + 1], ss[:, b:b + 1], ACT.Sqrt, bias=eps[:, :], scale=1.0 / D).then_inc(*sq_ready[b].inc)
                    for b in range(2):
                        act.wait_ge(*o_ready[b].n(i + 1))
                        act.dma_start(one(m.out, 2 * i + b), o[:, b, :]).then_inc(*out[b].inc)
                for b in range(2):
                    act.wait_ge(*out[b].n(N))

            @block.vector
            def _(dve):
                link = Chain(dve, dve_self)
                V = nc.vector
                V.memset(eps[:, :], EPS).then_inc(*eps_set.inc)
                dve.wait_ge(*gain_in.n(1))

                def take_idx(t, b):
                    V.tensor_copy(idx[:, b, :], m.dest[:, :, bass.ds(t, 1)].rearrange("p n a -> p (n a)")).then_inc(*idx_ready[b].inc)

                def pair(i, ahead):
                    for b in range(2):
                        dve.wait_ge(*scaled[b].n(i + 1))
                        dve.wait_ge(yg_in[b], i * 32 + 32)
                        if ahead:
                            take_idx(2 * i + 2 + b, b)
                        dve.wait_ge(*out[b].n(i))
                        link(V.scalar_tensor_tensor(o[:, b, :], yg[:, b, 1, :], m.gate[:, 1, bass.ds(2 * i + b, 1)], yg[:, b, 0, :], ALU.mult, ALU.add))
                        link(V.tensor_tensor(o[:, b, :], o[:, b, :], gate, ALU.mult))
                        dve.wait_ge(*x_in[b].n(i + 1))
                        V.tensor_tensor(o[:, b, :], o[:, b, :], x[:, b, :], ALU.add).then_inc(*sum_ready[b].inc)
                    for b in range(2):
                        dve.wait_ge(*sq_ready[b].n(i + 1))
                        link(V.reciprocal(ss[:, b:b + 1], ss[:, b:b + 1]))
                        V.scalar_tensor_tensor(o[:, b, :], o[:, b, :], ss[:, b:b + 1], gain[:, :], ALU.mult, ALU.mult).then_inc(*o_ready[b].inc)

                take_idx(0, 0)
                take_idx(1, 1)
                with link.loop(N - 1, 6) as i:
                    pair(i, True)
                pair(N - 1, False)
class Shared:
    pass


def attention_part(nc, m, a):
    with nc.sbuf_tensor("bias", [P, NB, AH, 2 * P], F32) as m.bias:
        bias_tables(nc, m, a)
        attention(nc, m, a)


PHASES = (adaln, project_tokens, project_channels, deltanet_gates, deltanet, attention_part, mix_out, route, experts, finish)


def block_kernel(nc, a, out):
    m = Shared()
    m.NCH = NCONV + 2 * AW // P
    m.out = out
    with ExitStack() as ctx:
        def sb(name, shape, dt=F32):
            return ctx.enter_context(nc.sbuf_tensor(name, shape, dt))

        def dram(name, shape, dt=F32):
            return nc.dram_tensor(name, shape, dt, kind="Internal").ap()

        m.cst = sb("cst", [P, C_END])
        m.mod = sb("mod", [P, 6 * D])
        m.rstd = sb("rstd", [P, NT])
        m.ba = sb("ba", [P, NT * 8])
        m.g = sb("g", [P, NT, GH])
        m.gsum = sb("gsum", [P, NT * GH])
        m.beta, m.nbe = sb("beta", [P, NT * GH]), sb("nbe", [P, NT * GH])
        m.kdec, m.sdec = sb("kdec", [P, NT * GH]), sb("sdec", [P, NT * GH])
        m.lg = sb("lg", [P, NT * (NG + NE)])
        m.gate = sb("gate", [P, 2, NT])
        m.dest = sb("dest", [P, 2, NT], I32)
        m.blk_e = sb("blk_e", [P, NBLK], I32)
        m.slot_tok = sb("slot_tok", [P, NBLK], I32)
        m.ps = ctx.enter_context(nc.psum_tensor("ps", [P, 8, BANK], F32))
        m.ident, m.ones = m.cst[:, C_ID:C_ID + P], m.cst[:, C_ONE:C_ONE + P]
        m.z_d = dram("z_d", [NT, P, GW])
        m.v_d = dram("v_d", [NT, P, AW])
        m.y_d = dram("y_d", [NT, P, GW])
        m.bias_d = dram("bias_d", [AH, NB * BIAS_W])
        m.o_d = dram("o_d", [NB, NT, P, AW + 2 * AH])
        m.x2_d = dram("x2_d", [NT, P, D])
        m.h_d = dram("h_d", [NT, P, D])
        m.slot_tok_d = dram("slot_tok_d", [P, NBLK], I32)
        m.ys_d = dram("ys_d", [NBLK, P, D])
        m.ch_d = dram("ch_d", [m.NCH, P, T])
        with ExitStack() as early:
            m.ht = early.enter_context(nc.sbuf_tensor("ht", [P, KD, T], F32))
            for phase in PHASES[:3]:
                phase(nc, m, a)
        for phase in PHASES[3:]:
            phase(nc, m, a)


def kernel(**inputs):
    import numpy as np
    import concourse.bacc as bacc
    from concourse import mybir as _mybir
    from concourse.bass_utils import run_bass_kernel_spmd as run

    def chunks(w):
        return np.moveaxis(w.reshape(*w.shape[:-2], w.shape[-2] // P, P, w.shape[-1]), -3, -2)

    x = {k: np.asarray(v) for k, v in inputs.items()}
    w_in = x["w_in"][0]
    s1 = NCONV * P
    s2, s3 = s1 + GW, s1 + GW + 2 * GH
    w_conv = x["w_conv"][0]
    cst, bucket_one, bucket_off = bucket_constants()
    arrays = {
        "x": x["x"].reshape(NT, P, D),
        "c": x["c"].reshape(KD, P).T,
        "w_ada": chunks(x["w_ada"][0]).reshape(P, KD, 6 * D // BANK, BANK).transpose(2, 0, 1, 3),
        "b_ada": x["b_ada"],
        "norm_mix": x["norm_mix"], "norm_ffn": x["norm_ffn"], "norm_final": x["norm_final"],
        "gdn_norm": x["gdn_norm"], "attn_norm": x["attn_norm"],
        "a_log": x["a_log"], "dt_bias": x["dt_bias"], "rel_bias": x["rel_bias"],
        "w_tok": chunks(np.concatenate([w_in[:, s1:s2], w_in[:, s3 + 2 * AW:], w_in[:, s2:s3]], 1)),
        "w_chan": chunks(np.concatenate([w_in[:, :s1], w_in[:, s3:s3 + 2 * AW]], 1)).reshape(P, KD, -1, P).transpose(2, 0, 1, 3),
        "w_conv": w_conv.reshape(CONV, NCONV, P).transpose(2, 1, 0).reshape(P, NCONV * CONV),
        "w_out": chunks(x["w_out"][0]),
        "w_router": chunks(np.concatenate([x["w_router_group"][0], x["w_router_expert"][0]], 1)),
        "w_gate_up": chunks(np.concatenate([x["w_gate"][0], x["w_up"][0]], 2)),
        "w_down": chunks(x["w_down"][0]),
        "cst": cst, "bucket_one": bucket_one, "bucket_off": bucket_off,
    }
    arrays = {k: np.ascontiguousarray(v) for k, v in arrays.items()}
    nc = bacc.Bacc("TRN2", target_bir_lowering=False, num_devices=1)
    aps = {k: nc.dram_tensor(f"in_{k}", v.shape, _mybir.dt.from_np(v.dtype), kind="ExternalInput").ap() for k, v in arrays.items()}
    out = nc.dram_tensor("out_0", (NT, P, D), F32, kind="ExternalOutput").ap()
    block_kernel(nc, aps, out)
    r = run(nc, [{f"in_{k}": v for k, v in arrays.items()}], core_ids=[0])
    return r.results[0]["out_0"].reshape(1, T, D)
```

```python
import concourse.bass as bass
from concourse import mybir
from contextlib import ExitStack, contextmanager

F32 = mybir.dt.float32
I32 = mybir.dt.int32
U32 = mybir.dt.uint32
ALU = mybir.AluOpType
ACT = mybir.ActivationFunctionType
AX = mybir.AxisListType

P = 128
T = 2048
NT = T // P
D = 1024
KD = D // P
EPS = 1e-6
NEG = -1e30
BANK = 512

GH = 4
GW = GH * P
CONV = 4
NCONV = 3 * GH
AH = 8
DH = 64
AW = AH * DH
BR = ((1, 16), (4, 4), (16, 1))
NB = len(BR)
BIAS_W = 384
NE = 32
NG = 4
EG = NE // NG
DE = 256
NBLK = 2 * T // P + NE
NTOK = 2 * GW + 8

C_ID = 0
C_UI = C_ID + P
C_US = C_UI + P
C_ONE = C_US + P
C_FLIP = C_ONE + P
C_NI = C_FLIP + P
C_PS = C_NI + P
C_L = C_PS + P
C_L1T = C_L + 7 * P
C_IOTA = C_L1T + P
C_BLK = C_IOTA + NE
C_TOK = C_BLK + NBLK
C_END = C_TOK + NT


def bucket_constants():
    import math
    import numpy as np
    c = np.zeros((P, C_END), np.float32)
    r, k = np.arange(P)[:, None], np.arange(P)[None, :]
    c[:, C_ID:C_ID + P] = r == k
    c[:, C_UI:C_UI + P] = r <= k
    c[:, C_US:C_US + P] = r < k
    c[:, C_ONE:C_ONE + P] = 1
    c[:, C_FLIP:C_FLIP + P] = r + k == P - 1
    c[:, C_NI:C_NI + P] = np.where(r <= k, 0, NEG)
    c[:, C_PS:C_PS + P] = np.where(r > k, 0, -NEG)
    for n in range(7):
        b = 1 << n
        m = (r // (2 * b) == k // (2 * b)) & (r % (2 * b) >= b) & (k % (2 * b) < b)
        c[:, C_L + n * P:C_L + (n + 1) * P] = m
        if n == 0:
            c[:, C_L1T:C_L1T + P] = m.T
    c[:, C_IOTA:C_IOTA + NE] = np.arange(NE)
    c[:, C_BLK:C_BLK + NBLK] = P * np.arange(NBLK)
    c[:, C_TOK:C_TOK + NT] = np.arange(NT)[None, :] * P + r
    one = np.zeros((NE, NB, BIAS_W), np.float32)
    off = np.full((AH, NB, BIAS_W), NEG, np.float32)
    for n, (dil, _) in enumerate(BR):
        for y in range(P - 1, 2 * P):
            dist = (2 * P - 1 - y) * dil
            if dist < 16:
                b = dist
            else:
                b = 16 + int(np.float32(np.log(np.float32(dist / 16))) / np.float32(math.log(2048 / 16)) * np.float32(16))
            one[min(b, 31), n, y] = 1
            off[:, n, y] = 0
    return c, one.reshape(NE, NB * BIAS_W), off.reshape(AH, NB * BIAS_W)


class Chain:

    def __init__(self, eng, sem):
        self.eng, self.sem, self.base, self.n = eng, sem, 0, 0

    def __call__(self, ins):
        self.n += 1
        ins.then_inc(self.sem, 1)
        self.eng.wait_ge(self.sem, self.base + self.n)

    @contextmanager
    def loop(self, times, per):
        start, self.n = self.base + self.n, 0
        with self.eng.Fori(0, times) as i:
            self.base = i * per + start
            yield i
            assert self.n == per, (self.n, per)
        self.base, self.n = start + times * per, 0


class Signal:

    def __init__(self, sem, step, credit):
        self.inc, self.step, self.credit = (sem, step), step, credit

    def n(self, n):
        return self.inc[0], n * self.step + self.credit * self.step


class Room:

    def __init__(self, nc, tag):
        self.nc, self.tag, self.ctx, self.all, self.sem_list = nc, tag, ExitStack(), [], []

    def __enter__(self):
        return self

    def __exit__(self, *a):
        self.ctx.close()
        if self.sem_list:
            self.nc.clear_and_free_semaphores(self.sem_list)
            self.nc.all_engine_barrier()

    def sb(self, name, shape, dt=F32):
        return self.ctx.enter_context(self.nc.sbuf_tensor(f"{self.tag}_{name}", shape, dt))

    def plain(self, name):
        self.sem_list.append(self.nc.alloc_semaphore(name=f"{self.tag}_{name}"))
        return self.sem_list[-1]

    def sig(self, name, step=1, credit=1):
        s = Signal(self.plain(name), step, credit)
        self.all.append(s)
        return s

    def sigs(self, name, n=2, step=1, credit=1):
        return [self.sig(f"{name}{k}", step, credit) for k in range(n)]

    def block(self):
        for s in self.all:
            self.nc.sync.sem_inc(s.inc[0], s.step * s.credit)
        return self.nc.Block()


def row_bc(ap, n, offset=0):
    return bass.AP(ap.tensor, ap.offset + offset, [[0, P], [1, n]])


def one(ap, i):
    r = ap[(bass.ds(i, 1),) + (slice(None),) * (ap.ndim - 1)]
    names = " ".join("bcde"[:ap.ndim - 2])
    return r.rearrange(f"a p {names} -> (a p) {names}")


def adaln(nc, m, a):
    N = 6 * D // BANK // 2
    with Room(nc, "ada") as R:
        ct = R.sb("ct", [P, KD])
        cb = R.sb("cb", [P, KD, P])
        w = R.sb("w", [P, 2, KD, BANK])
        bb = R.sb("bb", [P, 2, BANK])
        nrm = R.sb("nrm", [P, 2, D])
        xb = R.sb("xb", [P, 2, D])
        junk = R.sb("junk", [P, 2, D])
        eps = R.sb("eps", [P, 1])
        ssq = R.sb("ssq", [P, NT])
        std = R.sb("std", [P, NT])
        c_in, small_in = R.sig("c_in", 16), R.sig("small_in", 16)
        cb_ready, eps_set, std_ready = R.sig("cb_ready"), R.sig("eps_set"), R.sig("std_ready")
        w_in = R.sigs("w_in", 2, 16)
        mm_done, mod_ready = R.sigs("mm_done"), R.sigs("mod_ready")
        x_in, x_used = R.sigs("x_in", 2, 16), R.sigs("x_used")
        dve_self = R.plain("dve_self")
        ps = m.ps
        with R.block() as block:
            @block.sync
            def _(sp):
                sp.dma_start(ct[:, :], a["c"]).then_inc(*c_in.inc)
                sp.dma_start(nrm[:, 0, :], row_bc(a["norm_mix"], D)).then_inc(*small_in.inc)
                sp.dma_start(nrm[:, 1, :], row_bc(a["norm_ffn"], D)).then_inc(*small_in.inc)
                sp.dma_start(m.cst[:, :], a["cst"]).then_inc(*small_in.inc)
                with sp.Fori(0, N) as i:
                    for b in range(2):
                        sp.wait_ge(*mod_ready[b].n(i))
                        sp.dma_start(w[:, b, :, :], one(a["w_ada"], 2 * i + b)).then_inc(*w_in[b].inc)
                        sp.dma_start(bb[:, b, :], row_bc(a["b_ada"], BANK, (2 * i + b) * BANK)).then_inc(*w_in[b].inc)
                sp.wait_ge(*small_in.n(3))

            @block.tensor
            def _(pe):
                pe.wait_ge(*cb_ready.n(1))
                with pe.Fori(0, N) as i:
                    for b in range(2):
                        pe.wait_ge(*w_in[b].n(2 * i + 2))
                        pe.wait_ge(*mod_ready[b].n(i))
                        for k in range(KD):
                            last = nc.tensor.matmul(ps[:, b, :], cb[:, k, :], w[:, b, k, :], start=(k == 0), stop=(k == KD - 1))
                        last.then_inc(*mm_done[b].inc)

            @block.vector
            def _(dve):
                link = Chain(dve, dve_self)
                nc.vector.memset(eps[:, :], EPS).then_inc(*eps_set.inc)
                dve.wait_ge(*c_in.n(1))
                nc.vector.tensor_copy(cb[:, :, :], ct[:, :].unsqueeze(2).to_broadcast([P, KD, P])).then_inc(*cb_ready.inc)
                with dve.Fori(0, N) as i:
                    for b in range(2):
                        dve.wait_ge(*mm_done[b].n(i + 1))
                        nc.vector.tensor_tensor(m.mod[:, bass.ds((2 * i + b) * BANK, BANK)], ps[:, b, :], bb[:, b, :], ALU.add).then_inc(*mod_ready[b].inc)
                for b in range(2):
                    dve.wait_ge(*mod_ready[b].n(N))
                dve.wait_ge(*small_in.n(3))
                for n in range(2):
                    s = m.mod[:, (3 * n + 1) * D:(3 * n + 2) * D]
                    link(nc.vector.scalar_tensor_tensor(s, s, 1.0, nrm[:, n, :], ALU.add, ALU.mult))
                dve.wait_ge(*std_ready.n(1))
                link(nc.vector.reciprocal(m.rstd[:, :], std[:, :]))

            @block.scalar
            def _(act):
                act.wait_ge(*eps_set.n(1))
                with act.Fori(0, NT // 2) as i:
                    for b in range(2):
                        act.wait_ge(*x_used[b].n(i))
                        act.dma_start(xb[:, b, :], one(a["x"], 2 * i + b)).then_inc(*x_in[b].inc)
                    for b in range(2):
                        act.wait_ge(*x_in[b].n(i + 1))
                        nc.scalar.activation(junk[:, b, :], xb[:, b, :], ACT.Square, accum_out=ssq[:, bass.ds(2 * i + b, 1)]).then_inc(*x_used[b].inc)
                for b in range(2):
                    act.wait_ge(*x_used[b].n(NT // 2))
                nc.scalar.activation(std[:, :], ssq[:, :], ACT.Sqrt, bias=eps[:, :], scale=1.0 / D).then_inc(*std_ready.inc)


def project_tokens(nc, m, a):
    with Room(nc, "pt") as R:
        xb = R.sb("xb", [P, 2, D])
        h = R.sb("h", [P, 2, D])
        ht = R.sb("ht", [P, 2, KD, P])
        wt = R.sb("wt", [P, KD, NTOK])
        z = R.sb("z", [P, 2, GW])
        v = R.sb("v", [P, 2, AW])
        w_in = R.sig("w_in", 16)
        x_in, xg_ready, h_ready, tr_done = R.sigs("x_in", 2, 16), R.sigs("xg_ready"), R.sigs("h_ready"), R.sigs("tr_done")
        ht_ready, ht_kept = R.sigs("ht_ready"), R.sigs("ht_kept")
        z_mm, v_mm, ba_mm = R.sigs("z_mm"), R.sigs("v_mm"), R.sigs("ba_mm")
        z_ready, v_ready, ba_kept = R.sigs("z_ready"), R.sigs("v_ready"), R.sigs("ba_kept")
        z_out, v_out = R.sigs("z_out", 2, 16), R.sigs("v_out", 2, 16)
        ps = m.ps
        gain, shift = m.mod[:, D:2 * D], m.mod[:, 0:D]
        with R.block() as block:
            @block.sync
            def _(sp):
                sp.dma_start(wt[:, :, :], a["w_tok"]).then_inc(*w_in.inc)
                with sp.Fori(0, NT // 2) as i:
                    for b in range(2):
                        sp.wait_ge(*xg_ready[b].n(i))
                        sp.dma_start(xb[:, b, :], one(a["x"], 2 * i + b)).then_inc(*x_in[b].inc)

            @block.vector
            def _(dve):
                def make_h(i, b):
                    dve.wait_ge(*x_in[b].n(i + 1))
                    dve.wait_ge(*tr_done[b].n(i))
                    nc.vector.scalar_tensor_tensor(h[:, b, :], xb[:, b, :], m.rstd[:, bass.ds(2 * i + b, 1)], gain, ALU.mult, ALU.mult).then_inc(*xg_ready[b].inc)
                    dve.wait_ge(*xg_ready[b].n(i + 1))
                    nc.vector.tensor_tensor(h[:, b, :], h[:, b, :], shift, ALU.add).then_inc(*h_ready[b].inc)

                def drain(i, ahead):
                    for b in range(2):
                        dve.wait_ge(*ht_ready[b].n(i + 1))
                        nc.vector.tensor_copy(m.ht[:, :, bass.ds((2 * i + b) * P, P)], ht[:, b, :, :]).then_inc(*ht_kept[b].inc)
                        if ahead:
                            make_h(i + 1, b)
                        dve.wait_ge(*v_mm[b].n(i + 1))
                        dve.wait_ge(*v_out[b].n(i))
                        nc.vector.tensor_copy(v[:, b, :], ps[:, 5, :]).then_inc(*v_ready[b].inc)
                        dve.wait_ge(*ba_mm[b].n(i + 1))
                        nc.vector.tensor_copy(m.ba[:, bass.ds((2 * i + b) * 8, 8)], ps[:, 6, 0:8]).then_inc(*ba_kept[b].inc)

                make_h(0, 0)
                make_h(0, 1)
                with dve.Fori(0, NT // 2 - 1) as i:
                    drain(i, True)
                drain(NT // 2 - 1, False)
                for b in range(2):
                    dve.wait_ge(*ba_kept[b].n(NT // 2))

            @block.tensor
            def _(pe):
                def left(i, b, s):
                    pe.wait_ge(*s[1 - b].n(i + b))

                pe.wait_ge(*w_in.n(1))
                with pe.Fori(0, NT // 2) as i:
                    for b in range(2):
                        pe.wait_ge(*h_ready[b].n(i + 1))
                        pe.wait_ge(*ht_ready[b].n(i))
                        for k in range(KD):
                            last = nc.tensor.transpose(ps[:, 2 * b + k // 4, (k % 4) * P:(k % 4 + 1) * P], h[:, b, k * P:(k + 1) * P], m.ident)
                        last.then_inc(*tr_done[b].inc)
                    for b in range(2):
                        pe.wait_ge(*ht_ready[b].n(i + 1))
                        for bank, lo, hi, read, done in ((4, 0, GW, z_ready, z_mm), (5, GW, 2 * GW, v_ready, v_mm), (6, 2 * GW, NTOK, ba_kept, ba_mm)):
                            left(i, b, read)
                            for k in range(KD):
                                last = nc.tensor.matmul(ps[:, bank, 0:hi - lo], ht[:, b, k, :], wt[:, k, lo:hi], start=(k == 0), stop=(k == KD - 1))
                            last.then_inc(*done[b].inc)

            @block.scalar
            def _(act):
                with act.Fori(0, NT // 2) as i:
                    for b in range(2):
                        act.wait_ge(*tr_done[b].n(i + 1))
                        act.wait_ge(*ba_mm[b].n(i))
                        act.wait_ge(*ht_kept[b].n(i))
                        nc.scalar.copy(ht[:, b, :, :].rearrange("p k n -> p (k n)"), ps[:, 2 * b:2 * b + 2, :].rearrange("p k n -> p (k n)")).then_inc(*ht_ready[b].inc)
                    for b in range(2):
                        act.wait_ge(*z_mm[b].n(i + 1))
                        act.wait_ge(*z_out[b].n(i))
                        nc.scalar.activation(z[:, b, :], ps[:, 4, :], ACT.Silu).then_inc(*z_ready[b].inc)
                        act.wait_ge(*z_ready[b].n(i + 1))
                        act.dma_start(one(m.z_d, 2 * i + b), z[:, b, :]).then_inc(*z_out[b].inc)
                        act.wait_ge(*v_ready[b].n(i + 1))
                        act.dma_start(one(m.v_d, 2 * i + b), v[:, b, :]).then_inc(*v_out[b].inc)
                for b in range(2):
                    act.wait_ge(*z_out[b].n(NT // 2))
                    act.wait_ge(*v_out[b].n(NT // 2))


def project_channels(nc, m, a):
    HIST = CONV - 1
    with Room(nc, "pc") as R:
        w = R.sb("w", [P, 2, KD, P])
        wc = R.sb("wc", [P, NCONV * CONV])
        pre = R.sb("pre", [P, 2, HIST + T])
        cv = R.sb("cv", [P, 2, T])
        sq = R.sb("sq", [P, 1, T])
        rs = R.sb("rs", [P, 1, T])
        eps = R.sb("eps", [P, 1])
        small_in, zeroed = R.sig("small_in", 16), R.sig("zeroed")
        w_in = R.sigs("w_in", 2, 16)
        mm_done, mm_read = R.sigs("mm_done", 4, credit=2), R.sigs("mm_read", 4)
        cv_ready, silu_ready, sq_ready = R.sigs("cv_ready"), R.sigs("silu_ready"), R.sigs("sq_ready")
        ss_done, std_ready, ready, out = R.sigs("ss_done"), R.sigs("std_ready"), R.sigs("ready"), R.sigs("out", 2, 16)
        dve_self = R.plain("dve_self")
        ps = m.ps
        RUNS = ((0, GH, True, True), (GH, GH // 2, True, False), (NCONV // 2, AW // P, False, False))
        with R.block() as block:
            @block.sync
            def _(sp):
                sp.dma_start(wc[:, :], a["w_conv"]).then_inc(*small_in.inc)

                def load(i):
                    for b in range(2):
                        sp.wait_ge(*mm_done[3].n(2 * i + b - 1))
                        sp.dma_start(w[:, b, :, :], one(a["w_chan"], 2 * i + b)).then_inc(*w_in[b].inc)

                def store(i, conv):
                    for b in range(2):
                        if conv:
                            sp.wait_ge(*ready[b].n(i + 1))
                        else:
                            for g in range(4):
                                sp.wait_ge(*mm_read[g].n(2 * i + b + 1))
                        sp.dma_start(one(m.ch_d, 2 * i + b), cv[:, b, :]).then_inc(*out[b].inc)

                load(0)
                for first, n, conv, norm in RUNS:
                    with sp.Fori(first, first + n - (not conv)) as i:
                        load(i + 1)
                        store(i, conv)
                store(m.NCH // 2 - 1, False)
                for b in range(2):
                    sp.wait_ge(*out[b].n(m.NCH // 2))

            @block.tensor
            def _(pe):
                def norms(i, b):
                    pe.wait_ge(*sq_ready[b].n(i + 1))
                    pe.wait_ge(*std_ready[1 - b].n(i + b))
                    for g in range(4):
                        last = nc.tensor.matmul(ps[:, 4 + g, :], m.ones, sq[:, 0, g * BANK:(g + 1) * BANK], start=True, stop=True)
                    last.then_inc(*ss_done[b].inc)

                def chunk(i, b):
                    pe.wait_ge(*w_in[b].n(i + 1))
                    for g in range(4):
                        pe.wait_ge(*mm_read[g].n(2 * i + b))
                        for k in range(KD):
                            last = nc.tensor.matmul(ps[:, g, :], w[:, b, k, :], m.ht[:, k, g * BANK:(g + 1) * BANK], start=(k == 0), stop=(k == KD - 1))
                        last.then_inc(*mm_done[g].inc)

                for r, (first, n, conv, norm) in enumerate(RUNS):
                    chunk(first, 0)
                    if r == 1:
                        norms(first - 1, 1)
                    chunk(first, 1)
                    if norm:
                        norms(first, 0)
                    with pe.Fori(first + 1, first + n) as i:
                        chunk(i, 0)
                        if norm:
                            norms(i - 1, 1)
                        chunk(i, 1)
                        if norm:
                            norms(i, 0)

            @block.scalar
            def _(act):
                act.wait_ge(*zeroed.n(2))
                for first, n, conv, norm in RUNS:
                    with act.Fori(first, first + n) as i:
                        for b in range(2):
                            if conv:
                                act.wait_ge(*cv_ready[b].n(i))
                                dst = pre[:, b, HIST:]
                            else:
                                act.wait_ge(*out[b].n(i))
                                dst = cv[:, b, :]
                            for g in range(4):
                                act.wait_ge(*mm_done[g].n(2 * i + b + 1))
                                nc.scalar.copy(dst[:, g * BANK:(g + 1) * BANK], ps[:, g, :]).then_inc(*mm_read[g].inc)
                            if conv:
                                act.wait_ge(*cv_ready[b].n(i + 1))
                                nc.scalar.activation(cv[:, b, :], cv[:, b, :], ACT.Silu).then_inc(*(silu_ready if norm else ready)[b].inc)
                            if norm:
                                act.wait_ge(*silu_ready[b].n(i + 1))
                                act.wait_ge(*ss_done[1 - b].n(i + b))
                                nc.scalar.activation(sq[:, 0, :], cv[:, b, :], ACT.Square).then_inc(*sq_ready[b].inc)
                                act.wait_ge(*ss_done[b].n(i + 1))
                                act.wait_ge(*ready[1 - b].n(i + b))
                                nc.scalar.activation(rs[:, 0, :], ps[:, 4:8, :].rearrange("p g n -> p (g n)"), ACT.Sqrt, bias=eps[:, :]).then_inc(*std_ready[b].inc)

            @block.vector
            def _(dve):
                link = Chain(dve, dve_self)
                link(nc.vector.memset(eps[:, :], EPS))
                for b in range(2):
                    nc.vector.memset(pre[:, b, 0:HIST], 0.0).then_inc(*zeroed.inc)
                dve.wait_ge(*small_in.n(1))
                for first, n, conv, norm in RUNS:
                    if not conv:
                        break
                    with link.loop(n, 2 * (3 + norm)) as j:
                        i = j + first
                        for b in range(2):
                            for g in range(4):
                                dve.wait_ge(*mm_read[g].n(2 * i + b + 1))
                            dve.wait_ge(*out[b].n(i))
                            link(nc.vector.tensor_scalar(cv[:, b, :], pre[:, b, 0:T], wc[:, bass.ds((2 * i + b) * CONV, 1)], None, ALU.mult))
                            for s in range(1, CONV):
                                ins = nc.vector.scalar_tensor_tensor(cv[:, b, :], pre[:, b, s:s + T], wc[:, bass.ds((2 * i + b) * CONV + s, 1)], cv[:, b, :], ALU.mult, ALU.add)
                                if s < CONV - 1:
                                    link(ins)
                            ins.then_inc(*cv_ready[b].inc)
                            if norm:
                                dve.wait_ge(*std_ready[b].n(i + 1))
                                link(nc.vector.reciprocal(rs[:, 0, :], rs[:, 0, :]))
                                nc.vector.tensor_tensor(cv[:, b, :], cv[:, b, :], rs[:, 0, :], ALU.mult).then_inc(*ready[b].inc)
def deltanet_gates(nc, m, a):
    N = NT * GH
    with Room(nc, "gg") as R:
        al = R.sb("al", [P, GH])
        dtb = R.sb("dtb", [P, GH])
        y = R.sb("y", [P, NT, GH])
        t = R.sb("t", [P, 3, NT, GH])
        small_in = R.sig("small_in", 16)
        y_ready, act_self, dve_self = R.sig("y_ready"), R.plain("act_self"), R.plain("dve_self")
        sp_ready, g_ready, sums_done, eg_ready, act_done = R.sig("sp_ready"), R.sig("g_ready"), R.sig("sums_done"), R.sig("eg_ready"), R.sig("act_done")
        diff_ready = R.sig("diff_ready")
        ps = m.ps
        ba = m.ba[:, :].rearrange("p (t n) -> p t n", n=8)
        last = ps[:, 1, 0:N]
        with R.block() as block:
            @block.sync
            def _(sp):
                sp.dma_start(al[:, :], row_bc(a["a_log"], GH)).then_inc(*small_in.inc)
                sp.dma_start(dtb[:, :], row_bc(a["dt_bias"], GH)).then_inc(*small_in.inc)

            @block.vector
            def _(dve):
                link = Chain(dve, dve_self)
                dve.wait_ge(*small_in.n(2))
                nc.vector.tensor_tensor(y[:, :, :], ba[:, :, GH:8], dtb[:, :].unsqueeze(1).to_broadcast([P, NT, GH]), ALU.add).then_inc(*y_ready.inc)
                dve.wait_ge(*sp_ready.n(1))
                link(nc.vector.scalar_tensor_tensor(y[:, :, :], y[:, :, :], 0.0, t[:, 1, :, :], ALU.max, ALU.add))
                nc.vector.scalar_tensor_tensor(m.g[:, :, :], y[:, :, :], -1.0, al[:, :].unsqueeze(1).to_broadcast([P, NT, GH]), ALU.mult, ALU.mult).then_inc(*g_ready.inc)
                dve.wait_ge(*sums_done.n(1))
                link(nc.vector.tensor_copy(m.gsum[:, :], ps[:, 0, 0:N]))
                nc.vector.tensor_tensor(m.kdec[:, :], last, m.gsum[:, :], ALU.subtract).then_inc(*diff_ready.inc)
                dve.wait_ge(*eg_ready.n(1))
                link(nc.vector.scalar_tensor_tensor(m.nbe[:, :], m.beta[:, :], -1.0, t[:, 2, :, :].rearrange("p t n -> p (t n)"), ALU.mult, ALU.mult))

            @block.scalar
            def _(act):
                link = Chain(act, act_self)
                act.wait_ge(*y_ready.n(1))
                link(nc.scalar.activation(m.beta[:, :].rearrange("p (t n) -> p t n", n=GH), ba[:, :, 0:GH], ACT.Sigmoid))
                link(nc.scalar.activation(al[:, :], al[:, :], ACT.Exp))
                link(nc.scalar.activation(t[:, 0, :, :], y[:, :, :], ACT.Abs))
                link(nc.scalar.activation(t[:, 0, :, :], t[:, 0, :, :], ACT.Exp, scale=-1.0))
                nc.scalar.activation(t[:, 1, :, :], t[:, 0, :, :], ACT.Ln, bias=1.0).then_inc(*sp_ready.inc)
                act.wait_ge(*diff_ready.n(1))
                link(nc.scalar.activation(m.kdec[:, :], m.kdec[:, :], ACT.Exp))
                link(nc.scalar.activation(m.sdec[:, :], last, ACT.Exp))
                nc.scalar.activation(t[:, 2, :, :].rearrange("p t n -> p (t n)"), m.gsum[:, :], ACT.Exp).then_inc(*eg_ready.inc)

            @block.tensor
            def _(pe):
                pe.wait_ge(*g_ready.n(1))
                g = m.g[:, :, :].rearrange("p t n -> p (t n)")
                nc.tensor.matmul(ps[:, 0, 0:N], m.cst[:, C_UI:C_UI + P], g, start=True, stop=True)
                nc.tensor.matmul(ps[:, 1, 0:N], m.ones, g, start=True, stop=True).then_inc(*sums_done.inc)


def deltanet(nc, m, a):
    LEV = 7
    with Room(nc, "gd") as R:
        def pair(name):
            return R.sb(name, [P, 2, GW])
        qkv = R.sb("qkv", [P, 2, NCONV, P])
        z = pair("z")
        gu = pair("gu")
        d1, d2 = pair("d1"), pair("d2")
        qg, kg, vb = pair("qg"), pair("kg"), pair("vb")
        nt, dd, dt, yy = pair("nt"), pair("dd"), pair("dt"), pair("yy")
        r, u, o, o2 = pair("r"), pair("u"), pair("o"), pair("o2")
        st = R.sb("st", [P, 2, GH])
        state = R.sb("state", [P, GW])
        gain = R.sb("gain", [P, P])
        eps = R.sb("eps", [P, 1])
        ps = m.ps
        S = R.sigs
        gain_in, later_in = R.sig("gain_in", 16), R.sig("later_in", 16)
        state_set = R.sig("state_set")
        qkv_in, z_in = S("qkv_in", 2, 16), S("z_in", 2, 16)
        gu_ready, rows_done, dd_ready, dec_ready = S("gu_ready"), S("rows_done"), S("dd_ready"), S("dec_ready")
        erow_ready, qg_ready = S("erow_ready"), S("qg_ready")
        kk_done, kq_done, n_ready, aqk_ready = S("kk_done"), S("kq_done"), S("n_ready"), S("aqk_ready")
        kt_done, vt_done, kg_ready, vb_ready = S("kt_done"), S("vt_done"), S("kg_ready"), S("vb_ready")
        nt_done, nt_ready = S("nt_done"), S("nt_ready")
        d_ready, dt_ready = S("d_ready"), S("dt_ready")
        y_done, y_ready, zz_done, zt_done = S("y_done"), S("y_ready"), S("zz_done"), S("zt_done")
        ks_done, r_ready, u_done, u_ready = S("ks_done"), S("r_ready"), S("u_done"), S("u_ready")
        o_done, ds_done, s_ready, o_ready = S("o_done"), S("ds_done"), S("s_ready"), S("o_ready")
        osq_ready, std_ready, y_out_ready, out = S("osq_ready"), R.sig("std_ready"), S("y_out_ready"), S("out", 2, 16)
        rstd_ready = R.sig("rstd_ready")
        dve_self, pool_self = R.plain("dve_self"), R.plain("pool_self")
        ID4 = m.ident.unsqueeze(1).to_broadcast([P, GH, P])

        def c4(col):
            return m.cst[:, col:col + P].unsqueeze(1).to_broadcast([P, GH, P])

        def h4(ap):
            return ap.rearrange("p (h n) -> p h n", h=GH)

        def hs(h):
            return slice(h * P, (h + 1) * P)

        with R.block() as block:
            @block.sync
            def _(sp):
                sp.dma_start(gain[:, :], row_bc(a["gdn_norm"], P)).then_inc(*gain_in.inc)
                def load_qkv(i):
                    for b in range(2):
                        sp.wait_ge(*qg_ready[b].n(i))
                        sp.wait_ge(*ks_done[b].n(i))
                        src = m.ch_d[0:NCONV, :, bass.ds((2 * i + b) * P, P)].rearrange("c p n -> p c n")
                        sp.dma_start(qkv[:, b, :, :], src).then_inc(*qkv_in[b].inc)

                def load_z(i):
                    for b in range(2):
                        sp.wait_ge(*y_out_ready[b].n(i))
                        sp.dma_start(z[:, b, :], one(m.z_d, 2 * i + b)).then_inc(*z_in[b].inc)

                def store(i):
                    for b in range(2):
                        sp.wait_ge(*y_out_ready[b].n(i + 1))
                        sp.dma_start(one(m.y_d, 2 * i + b), o[:, b, :]).then_inc(*out[b].inc)

                load_qkv(0)
                load_z(0)
                sp.dma_start(m.qk[:, :, :], m.ch_d[NCONV:m.NCH, :, :].rearrange("c p n -> p c n")).then_inc(*later_in.inc)
                with sp.Fori(0, NT // 2 - 1) as i:
                    load_qkv(i + 1)
                    store(i)
                    load_z(i + 1)
                store(NT // 2 - 1)
                sp.wait_ge(*later_in.n(1))
                for b in range(2):
                    sp.wait_ge(*out[b].n(NT // 2))

            @block.gpsimd
            def _(pool):
                link = Chain(pool, pool_self)
                pool.wait_ge(*gain_in.n(1))

                def decays(i):
                    for b in range(2):
                        pool.wait_ge(*rows_done[b].n(i))
                        nc.gpsimd.tensor_tensor(h4(gu[:, b, :]), c4(C_UI), m.g[:, bass.ds(2 * i + b, 1), :].rearrange("p a h -> p (a h)").unsqueeze(2).to_broadcast([P, GH, P]), ALU.mult).then_inc(*gu_ready[b].inc)

                def decayed_q(i):
                    for b in range(2):
                        pool.wait_ge(*qkv_in[b].n(i + 1))
                        pool.wait_ge(*erow_ready[b].n(i + 1))
                        pool.wait_ge(*o_done[b].n(i))
                        nc.gpsimd.tensor_tensor(qg[:, b, :], qg[:, b, :], qkv[:, b, 0:GH, :].rearrange("p h n -> p (h n)"), ALU.mult).then_inc(*qg_ready[b].inc)

                def norm(i):
                    for b in range(2):
                        pool.wait_ge(*o_ready[b].n(i + 1))
                        link(nc.gpsimd.tensor_tensor(h4(o[:, b, :]), h4(o[:, b, :]), gain[:, :].unsqueeze(1).to_broadcast([P, GH, P]), ALU.mult))
                        pool.wait_ge(*z_in[b].n(i + 1))
                        link(nc.gpsimd.tensor_tensor(o[:, b, :], o[:, b, :], z[:, b, :], ALU.mult))
                    pool.wait_ge(*rstd_ready.n(i + 1))
                    for b in range(2):
                        nc.gpsimd.tensor_tensor(h4(o[:, b, :]), h4(o[:, b, :]), st[:, b, :].unsqueeze(2).to_broadcast([P, GH, P]), ALU.mult).then_inc(*y_out_ready[b].inc)

                decays(0)
                with link.loop(NT // 2 - 1, 4) as i:
                    decayed_q(i)
                    decays(i + 1)
                    norm(i)
                decayed_q(NT // 2 - 1)
                norm(NT // 2 - 1)

            @block.tensor
            def _(pe):
                def heads(bank, lhs, rhs, done=None, **kw):
                    for h in range(GH):
                        last = nc.tensor.matmul(ps[:, bank, hs(h)], lhs(h), rhs(h), start=True, stop=True)
                    last.then_inc(*done.inc)

                def q(b, h):
                    return qkv[:, b, h, :]

                def k(b, h):
                    return qkv[:, b, GH + h, :]

                pe.wait_ge(*state_set.n(1))
                with pe.Fori(0, NT // 2) as i:
                    for b in range(2):
                        B = 4 * b
                        pe.wait_ge(*gu_ready[b].n(i + 1))
                        pe.wait_ge(*o_ready[b].n(i))
                        nc.tensor.matmul(ps[:, B, :], m.ones, gu[:, b, :], start=True, stop=True).then_inc(*rows_done[b].inc)
                        pe.wait_ge(*qkv_in[b].n(i + 1))
                        pe.wait_ge(*s_ready[b].n(i))
                        heads(B + 1, lambda h: k(b, h), lambda h: k(b, h), kk_done[b])
                        heads(B + 2, lambda h: k(b, h), lambda h: q(b, h), kq_done[b])
                        for h in range(GH):
                            last = nc.tensor.transpose(ps[:, B + 3, hs(h)], k(b, h), m.ident)
                        last.then_inc(*kt_done[b].inc)
                    for b in range(2):
                        B = 4 * b
                        pe.wait_ge(*n_ready[b].n(i + 1))
                        for h in range(GH):
                            last = nc.tensor.transpose(ps[:, B + 1, hs(h)], yy[:, b, hs(h)], m.ident)
                        last.then_inc(*nt_done[b].inc)
                        pe.wait_ge(*kg_ready[b].n(i + 1))
                        for h in range(GH):
                            last = nc.tensor.transpose(ps[:, B + 3, hs(h)], qkv[:, b, 2 * GH + h, :], m.ident)
                        last.then_inc(*vt_done[b].inc)
                    for l in range(1, LEV):
                        for b in range(2):
                            B = 4 * b
                            if l == 1:
                                pe.wait_ge(*nt_ready[b].n(i + 1))
                                pe.wait_ge(*aqk_ready[b].n(i + 1))
                                pe.wait_ge(*vb_ready[b].n(i + 1))
                                pe.wait_ge(*dec_ready[b].n(2 * i + 2))
                            pe.wait_ge(*d_ready[b].n((LEV - 1) * i + l))
                            heads(B, lambda h: nt[:, b, hs(h)], lambda h: dd[:, b, hs(h)], y_done[b])
                        for b in range(2):
                            B = 4 * b
                            pe.wait_ge(*y_ready[b].n((LEV - 1) * i + l))
                            pe.wait_ge(*dt_ready[b].n(LEV * i + l))
                            if l < LEV - 1:
                                heads(B + 1, lambda h: dt[:, b, hs(h)], lambda h: yy[:, b, hs(h)], zz_done[b])
                            heads(B + 2, lambda h: yy[:, b, hs(h)], lambda h: dt[:, b, hs(h)], zt_done[b])
                    for b in range(2):
                        B = 4 * b
                        pe.wait_ge(*s_ready[1 - b].n(i + b))
                        heads(B + 1, lambda h: k(b, h), lambda h: state[:, hs(h)], ks_done[b])
                        pe.wait_ge(*r_ready[b].n(i + 1))
                        pe.wait_ge(*dt_ready[b].n(LEV * i + LEV))
                        heads(B + 2, lambda h: dt[:, b, hs(h)], lambda h: r[:, b, hs(h)], u_done[b])
                        pe.wait_ge(*u_ready[b].n(i + 1))
                        pe.wait_ge(*qg_ready[b].n(i + 1))
                        heads(B + 3, lambda h: kg[:, b, hs(h)], lambda h: u[:, b, hs(h)], ds_done[b])
                        for h in range(GH):
                            nc.tensor.matmul(ps[:, B, hs(h)], qg[:, b, hs(h)], state[:, hs(h)], start=True, stop=False)
                            last = nc.tensor.matmul(ps[:, B, hs(h)], d2[:, b, hs(h)], u[:, b, hs(h)], start=False, stop=True)
                        last.then_inc(*o_done[b].inc)

            @block.scalar
            def _(act):
                with act.Fori(0, NT // 2) as i:
                    for b in range(2):
                        B = 4 * b
                        act.wait_ge(*rows_done[b].n(i + 1))
                        act.wait_ge(*dd_ready[b].n(i + 1))
                        act.wait_ge(*o_done[b].n(i))
                        nc.scalar.activation(qg[:, b, :], ps[:, B, :], ACT.Exp).then_inc(*erow_ready[b].inc)
                        nc.scalar.activation(d1[:, b, :], d1[:, b, :], ACT.Exp, scale=-1.0).then_inc(*dec_ready[b].inc)
                        nc.scalar.activation(d2[:, b, :], d2[:, b, :], ACT.Exp).then_inc(*dec_ready[b].inc)
                        act.wait_ge(*kt_done[b].n(i + 1))
                        act.wait_ge(*ds_done[b].n(i))
                        for h in range(GH):
                            ins = nc.scalar.activation(kg[:, b, hs(h)], ps[:, B + 3, hs(h)], ACT.Copy, scale=m.kdec[:, bass.ds((2 * i + b) * GH + h, 1)])
                        ins.then_inc(*kg_ready[b].inc)
                    for b in range(2):
                        B = 4 * b
                        act.wait_ge(*nt_done[b].n(i + 1))
                        nc.scalar.copy(nt[:, b, :], ps[:, B + 1, :]).then_inc(*nt_ready[b].inc)
                        act.wait_ge(*vt_done[b].n(i + 1))
                        for h in range(GH):
                            ins = nc.scalar.activation(vb[:, b, hs(h)], ps[:, B + 3, hs(h)], ACT.Copy, scale=m.beta[:, bass.ds((2 * i + b) * GH + h, 1)])
                        ins.then_inc(*vb_ready[b].inc)
                    for b in range(2):
                        B = 4 * b
                        act.wait_ge(*u_done[b].n(i + 1))
                        nc.scalar.copy(u[:, b, :], ps[:, B + 2, :]).then_inc(*u_ready[b].inc)
                        act.wait_ge(*o_done[b].n(i + 1))
                        act.wait_ge(*out[b].n(i))
                        for h in range(GH):
                            ins = nc.scalar.activation(o2[:, b, hs(h)], ps[:, B, hs(h)], ACT.Square, scale=float(P) ** -0.5, accum_out=st[:, b, h:h + 1])
                        ins.then_inc(*osq_ready[b].inc)
                        nc.scalar.activation(o[:, b, :], ps[:, B, :], ACT.Copy, scale=float(P) ** -0.5).then_inc(*o_ready[b].inc)
                    for b in range(2):
                        act.wait_ge(*osq_ready[b].n(i + 1))
                    nc.scalar.activation(st[:, :, :], st[:, :, :], ACT.Sqrt, bias=eps[:, :], scale=1.0 / P).then_inc(*std_ready.inc)
            @block.vector
            def _(dve):
                link = Chain(dve, dve_self)
                link(nc.vector.memset(eps[:, :], EPS))
                nc.vector.memset(state[:, :], 0.0).then_inc(*state_set.inc)
                dve.wait_ge(*gain_in.n(1))

                def reciprocals(i):
                    dve.wait_ge(*std_ready.n(i + 1))
                    nc.vector.reciprocal(st[:, :, :], st[:, :, :]).then_inc(*rstd_ready.inc)

                def pair_of_chunks(i, first):
                    def per_head(tab, h):
                        return tab[:, bass.ds(b * GH + 2 * GH * i + h, 1)]

                    for b in range(2):
                        B = 4 * b
                        dve.wait_ge(*rows_done[b].n(i + 1))
                        dve.wait_ge(*aqk_ready[b].n(i))
                        dve.wait_ge(*o_done[b].n(i))
                        for h in range(GH):
                            nc.vector.scalar_tensor_tensor(d1[:, b, hs(h)], ps[:, B, hs(h)], per_head(m.gsum, h), m.cst[:, C_PS:C_PS + P], ALU.subtract, ALU.add)
                            ins = nc.vector.scalar_tensor_tensor(d2[:, b, hs(h)], ps[:, B, hs(h)], per_head(m.gsum, h), m.cst[:, C_NI:C_NI + P], ALU.subtract, ALU.add)
                        ins.then_inc(*dd_ready[b].inc)
                    if not first:
                        reciprocals(i - 1)
                    for b in range(2):
                        B = 4 * b
                        dve.wait_ge(*dec_ready[b].n(2 * i + 1))
                        dve.wait_ge(*kk_done[b].n(i + 1))
                        for h in range(GH):
                            ins = nc.vector.scalar_tensor_tensor(yy[:, b, hs(h)], ps[:, B + 1, hs(h)], per_head(m.beta, h), d1[:, b, hs(h)], ALU.mult, ALU.mult)
                        ins.then_inc(*n_ready[b].inc)
                        dve.wait_ge(*dec_ready[b].n(2 * i + 2))
                        dve.wait_ge(*kq_done[b].n(i + 1))
                        nc.vector.tensor_tensor(d2[:, b, :], d2[:, b, :], ps[:, B + 2, :], ALU.mult).then_inc(*aqk_ready[b].inc)
                    for b in range(2):
                        dve.wait_ge(*n_ready[b].n(i + 1))
                        link(nc.vector.tensor_tensor(h4(dd[:, b, :]), h4(yy[:, b, :]), c4(C_L), ALU.mult))
                        nc.vector.tensor_tensor(h4(dd[:, b, :]), ID4, h4(dd[:, b, :]), ALU.subtract).then_inc(*d_ready[b].inc)
                        dve.wait_ge(*nt_ready[b].n(i + 1))
                        link(nc.vector.tensor_tensor(h4(dt[:, b, :]), h4(nt[:, b, :]), c4(C_L1T), ALU.mult))
                        nc.vector.tensor_tensor(h4(dt[:, b, :]), ID4, h4(dt[:, b, :]), ALU.subtract).then_inc(*dt_ready[b].inc)
                    for l in range(1, LEV):
                        for b in range(2):
                            B = 4 * b
                            dve.wait_ge(*y_done[b].n((LEV - 1) * i + l))
                            nc.vector.tensor_tensor(h4(yy[:, b, :]), ps[:, B, :].rearrange("p (h n) -> p h n", h=GH), c4(C_L + l * P), ALU.mult).then_inc(*y_ready[b].inc)
                        for b in range(2):
                            B = 4 * b
                            if l < LEV - 1:
                                dve.wait_ge(*zz_done[b].n((LEV - 2) * i + l))
                                dve.wait_ge(*d_ready[b].n((LEV - 1) * i + l))
                                nc.vector.tensor_tensor(dd[:, b, :], dd[:, b, :], ps[:, B + 1, :], ALU.subtract).then_inc(*d_ready[b].inc)
                            dve.wait_ge(*zt_done[b].n((LEV - 1) * i + l))
                            dve.wait_ge(*dt_ready[b].n(LEV * i + l))
                            nc.vector.tensor_tensor(dt[:, b, :], dt[:, b, :], ps[:, B + 2, :], ALU.subtract).then_inc(*dt_ready[b].inc)
                    for b in range(2):
                        B = 4 * b
                        dve.wait_ge(*ks_done[b].n(i + 1))
                        dve.wait_ge(*vb_ready[b].n(i + 1))
                        for h in range(GH):
                            ins = nc.vector.scalar_tensor_tensor(r[:, b, hs(h)], ps[:, B + 1, hs(h)], per_head(m.nbe, h), vb[:, b, hs(h)], ALU.mult, ALU.add)
                        ins.then_inc(*r_ready[b].inc)
                        dve.wait_ge(*ds_done[b].n(i + 1))
                        dve.wait_ge(*o_done[b].n(i + 1))
                        for h in range(GH):
                            ins = nc.vector.scalar_tensor_tensor(state[:, hs(h)], state[:, hs(h)], per_head(m.sdec, h), ps[:, B + 3, hs(h)], ALU.mult, ALU.add)
                        ins.then_inc(*s_ready[b].inc)
                        dve.wait_ge(*s_ready[b].n(i + 1))

                pair_of_chunks(0, True)
                with link.loop(NT // 2 - 1, 2 * 2) as i:
                    pair_of_chunks(i + 1, False)
                reciprocals(NT // 2 - 1)
def bias_tables(nc, m, a):
    with Room(nc, "bt") as R:
        rel = R.sb("rel", [NE, AH])
        hot = R.sb("hot", [NE, NB * BIAS_W])
        off = R.sb("off", [AH, NB * BIAS_W])
        rows = R.sb("rows", [AH, NB * BIAS_W])
        flip = R.sb("flip", [P, NB, AH, 2 * P])
        small_in, rows_out, flip_in = R.sig("small_in", 16), R.sig("rows_out", 16), R.sig("flip_in", 16)
        rows_done, rows_ready, done, read = R.sig("rows_done"), R.sig("rows_ready"), R.sig("done"), R.sig("read")
        ps = m.ps
        with R.block() as block:
            @block.sync
            def _(sp):
                sp.dma_start(rel[:, :], a["rel_bias"]).then_inc(*small_in.inc)
                sp.dma_start(hot[:, :], a["bucket_one"]).then_inc(*small_in.inc)
                sp.dma_start(off[:, :], a["bucket_off"]).then_inc(*small_in.inc)
                sp.wait_ge(*rows_ready.n(NB))
                sp.dma_start(m.bias_d, rows[:, :]).then_inc(*rows_out.inc)
                sp.wait_ge(*rows_out.n(1))
                for n in range(NB):
                    src = bass.AP(m.bias_d.tensor, n * BIAS_W, [[1, P], [NB * BIAS_W, AH], [1, 2 * P]])
                    sp.dma_start(flip[:, n, :, :], src).then_inc(*flip_in.inc)

            @block.tensor
            def _(pe):
                pe.wait_ge(*small_in.n(3))
                for n in range(NB):
                    nc.tensor.matmul(ps[0:AH, n, 0:BIAS_W], rel[:, :], hot[:, n * BIAS_W:(n + 1) * BIAS_W], start=True, stop=True).then_inc(*rows_done.inc)
                pe.wait_ge(*flip_in.n(NB))
                for n in range(NB):
                    pe.wait_ge(*read.n(n))
                    for h in range(0, AH, 2):
                        last = nc.tensor.matmul(ps[:, 4 + h // 2, :], m.cst[:, C_FLIP:C_FLIP + P], flip[:, n, h:h + 2, :].rearrange("p h k -> p (h k)"), start=True, stop=True)
                    last.then_inc(*done.inc)

            @block.vector
            def _(dve):
                for n in range(NB):
                    dve.wait_ge(*rows_done.n(n + 1))
                    s = slice(n * BIAS_W, (n + 1) * BIAS_W)
                    nc.vector.tensor_tensor(rows[:, s], ps[0:AH, n, 0:BIAS_W], off[:, s], ALU.add).then_inc(*rows_ready.inc)
                for n in range(NB):
                    dve.wait_ge(*done.n(n + 1))
                    nc.vector.tensor_copy(m.bias[:, n, :, :].rearrange("p h k -> p (h k)"), ps[:, 4:8, :].rearrange("p b n -> p (b n)")).then_inc(*read.inc)


def attention(nc, m, a):
    RUNS = (
        (0, 0, 1, (False,), lambda i, j: 0),
        (1, 0, NT // 2 - 1, (True, True), lambda i, j: i * (2 * P) + (1 + j) * P),
        (NT - 1, 0, 1, (True,), lambda i, j: (NT - 1) * P),
        (NT, 1, BR[1][0], (False, True, True, True), lambda i, j: i + j * BR[1][0] * P),
        (2 * NT, 2, BR[2][0] // 2, (False, False), lambda i, j: i * 2 + j),
    )
    STEPS = AH // 2
    UNITS = NB * NT

    def units(eng):
        prev = None
        for run in RUNS:
            times, types = run[2], run[3]
            for j in range(len(types)):
                yield (run, 0, j), prev
                prev = (run, 0, j)
            if times > 1:
                with eng.Fori(0, times - 1) as i:
                    prev = (run, i, len(types) - 1)
                    for j in range(len(types)):
                        yield (run, i + 1, j), prev
                        prev = (run, i + 1, j)
                prev = (run, times - 1, len(types) - 1)
        yield None, prev

    def numbers(unit):
        (u0, _, _, types, _), i, j = unit
        return (u0 + j) % 2, i * (len(types) // 2) + (u0 + j) // 2, i * (2 * len(types)) + 2 * (u0 + j)

    def first_key(unit):
        return 0 if unit[0][3][unit[2]] else P

    def place(unit):
        (_, branch, _, _, first), i, j = unit
        return branch, BR[branch][0], first(i, j)

    with Room(nc, "at") as R:
        qk = m.qk
        qb = R.sb("qb", [P, 2, STEPS, P])
        kb = R.sb("kb", [P, 2, STEPS, 2 * P])
        v = R.sb("v", [P, 2, 2, AW])
        p = R.sb("p", [P, STEPS, 2, 2 * P])
        pt = R.sb("pt", [P, 2, 2, 2, P])
        low = R.sb("low", [P, 2, 2 * AH])
        o = R.sb("o", [P, 2, AW + 2 * AH])
        ps = m.ps
        later_in = R.sig("later_in", 16)
        v_in, out = R.sigs("v_in", 2, 16), R.sigs("out", 2, 16)
        q_ready, k_ready, o_ready = R.sigs("q_ready"), R.sigs("k_ready"), R.sigs("o_ready")
        s_done, s_read, max_ready, p_ready = R.sigs("s_done", credit=3), R.sigs("s_read"), R.sigs("max_ready"), R.sigs("p_ready")
        pt_done, pt_ready, pv_done = R.sigs("pt_done", credit=2), R.sigs("pt_ready"), R.sigs("pv_done", credit=3)
        with R.block() as block:
            @block.sync
            def _(sp):
                for unit, prev in units(sp):
                    if unit:
                        b, n, n2 = numbers(unit)
                        branch, dil, first = place(unit)
                        sp.wait_ge(*pv_done[1].n(n2 - 2))
                        if first_key(unit) == 0:
                            src = bass.AP(m.v_d.tensor, (first - P * dil) * AW, [[dil * AW, P], [P * dil * AW, 2], [1, AW]])
                            sp.dma_start(v[:, b, :, :], src).then_inc(*v_in[b].inc)
                        else:
                            src = bass.AP(m.v_d.tensor, first * AW, [[dil * AW, P], [1, AW]])
                            sp.dma_start(v[:, b, 1, :], src).then_inc(*v_in[b].inc)
                    if prev:
                        b, n, n2 = numbers(prev)
                        branch, dil, first = place(prev)
                        OW = AW + 2 * AH
                        sp.wait_ge(*o_ready[b].n(n + 1))
                        dst = bass.AP(m.o_d.tensor, branch * T * OW + first * OW, [[dil * OW, P], [1, OW]])
                        sp.dma_start(dst, o[:, b, :]).then_inc(*out[b].inc)
                for b in range(2):
                    sp.wait_ge(*out[b].n(UNITS // 2))

            @block.gpsimd
            def _(pool):
                for unit, prev in units(pool):
                    if unit:
                        b, n, n2 = numbers(unit)
                        lo = first_key(unit)
                        branch, dil, first = place(unit)
                        pool.wait_ge(*s_done[1].n(n2 - 2))
                        nc.gpsimd.tensor_copy(qb[:, b, :, :], qk[:, 0:STEPS, bass.DynSlice(first, P, step=dil)]).then_inc(*q_ready[b].inc)
                        nc.gpsimd.tensor_copy(kb[:, b, :, lo:], qk[:, STEPS:, bass.DynSlice(first - (P - lo) * dil, 2 * P - lo, step=dil)]).then_inc(*k_ready[b].inc)

            @block.tensor
            def _(pe):
                def scores(unit, s):
                    b, n, n2 = numbers(unit)
                    lo = first_key(unit)
                    if s == 0:
                        pe.wait_ge(*q_ready[b].n(n + 1))
                        pe.wait_ge(*k_ready[b].n(n + 1))
                    pe.wait_ge(*s_read[s % 2].n(n2 + s // 2))
                    for h in range(2):
                        r = slice(h * DH, (h + 1) * DH)
                        last = nc.tensor.matmul(ps[:, 2 * (s % 2) + h, lo:2 * P], qb[r, b, s, :], kb[r, b, s, lo:], start=True, stop=True)
                    last.then_inc(*s_done[s % 2].inc)

                def turn_p(unit, s):
                    b, n, n2 = numbers(unit)
                    e, c = s % 2, n2 + s // 2
                    pe.wait_ge(*p_ready[e].n(c + 1))
                    pe.wait_ge(*pt_ready[e].n(c))
                    for h in range(2):
                        for k in range(first_key(unit) // P, 2):
                            last = nc.tensor.transpose(ps[:, 4 + e, (h * 2 + k) * P:(h * 2 + k + 1) * P], p[:, s, h, k * P:(k + 1) * P], m.ident)
                    last.then_inc(*pt_done[e].inc)

                def sums(unit, s):
                    b, n, n2 = numbers(unit)
                    e, c = s % 2, n2 + s // 2
                    if s == 0:
                        pe.wait_ge(*v_in[b].n(n + 1))
                        pe.wait_ge(*o_ready[b].n(n))
                    pe.wait_ge(*pt_ready[e].n(c + 1))
                    k0 = first_key(unit) // P
                    for h in range(2):
                        for k in range(k0, 2):
                            w = slice((2 * s + h) * DH, (2 * s + h + 1) * DH)
                            last = nc.tensor.matmul(ps[:, 6 + b, w], pt[:, e, h, k, :], v[:, b, k, w], start=(k == k0), stop=(k == 1))
                    last.then_inc(*pv_done[e].inc)

                for unit, prev in units(pe):
                    for s in range(STEPS):
                        if prev and s + 1 < STEPS:
                            turn_p(prev, s + 1)
                        elif prev and unit:
                            turn_p(unit, 0)
                        if unit:
                            scores(unit, s)
                        if prev:
                            sums(prev, s)
                    if not prev:
                        turn_p(unit, 0)

            @block.vector
            def _(dve):
                for unit, prev in units(dve):
                    if unit:
                        b, n, n2 = numbers(unit)
                        lo = first_key(unit)
                        for s in range(STEPS):
                            e, c = s % 2, n2 + s // 2
                            dve.wait_ge(*s_done[e].n(c + 1))
                            dve.wait_ge(*pt_done[e].n(c - 1))
                            nc.vector.scalar_tensor_tensor(p[:, s, :, lo:], ps[:, 2 * e:2 * e + 2, lo:2 * P], DH ** -0.5, m.bias[:, unit[0][1], 2 * s:2 * s + 2, lo:], ALU.mult, ALU.add).then_inc(*s_read[e].inc)
                            dve.wait_ge(*s_read[e].n(c + 1))
                            nc.vector.tensor_reduce(low[:, b, 2 * s:2 * s + 2], p[:, s, :, lo:], AX.X, ALU.max, negate=True).then_inc(*max_ready[e].inc)
                    if prev:
                        b, n, n2 = numbers(prev)
                        dve.wait_ge(*pv_done[1].n(n2 + 2))
                        dve.wait_ge(*p_ready[1].n(n2 + 2))
                        dve.wait_ge(*out[b].n(n))
                        nc.vector.tensor_copy(o[:, b, AW:], low[:, b, :])
                        nc.vector.tensor_copy(o[:, b, 0:AW], ps[:, 6 + b, :]).then_inc(*o_ready[b].inc)

            @block.scalar
            def _(act):
                def take_pt(unit, s):
                    b, n, n2 = numbers(unit)
                    e, c, k = s % 2, n2 + s // 2, first_key(unit) // P
                    act.wait_ge(*pt_done[e].n(c + 1))
                    act.wait_ge(*pv_done[e].n(c))
                    nc.scalar.copy(pt[:, e, :, k:, :], ps[:, 4 + e, :].rearrange("p (h k n) -> p h k n", h=2, k=2)[:, :, k:, :]).then_inc(*pt_ready[e].inc)

                act.dma_start(m.w_out[:, :, :], a["w_out"]).then_inc(*later_in.inc)
                for unit, prev in units(act):
                    for s in range(STEPS):
                        if s >= 2 and unit:
                            take_pt(unit, s - 2)
                        elif s < 2 and prev:
                            take_pt(prev, s + 2)
                        if unit:
                            b, n, n2 = numbers(unit)
                            e, c, lo = s % 2, n2 + s // 2, first_key(unit)
                            act.wait_ge(*max_ready[e].n(c + 1))
                            for h in range(2):
                                at = 2 * s + h
                                ins = nc.scalar.activation(p[:, s, h, lo:], p[:, s, h, lo:], ACT.Exp, bias=low[:, b, at:at + 1], accum_out=low[:, b, at + AH:at + AH + 1])
                            ins.then_inc(*p_ready[e].inc)
                act.wait_ge(*later_in.n(1))
def is_tile(t, n):
    return isinstance(t, int) and t == n


def after(b, q):
    return 1 - b, q + b


def before(b, q):
    return 1 - b, q - 1 + b


def steps(loop):
    yield 0, 0, 0
    yield 1, 1, 0
    with loop(NT // 2 - 2) as i:
        yield i * 2 + 2, 0, i + 1
        yield i * 2 + 3, 1, i + 1
    yield NT - 2, 0, NT // 2 - 1
    yield NT - 1, 1, NT // 2 - 1


def mix_out(nc, m, a):
    OW = AW + 2 * AH
    with Room(nc, "mo") as R:
        w = m.w_out
        wr = R.sb("wr", [P, KD, NG + NE])
        gain = R.sb("gain", [P, AW])
        eps = R.sb("eps", [P, 1])
        y = R.sb("y", [P, 2, 2 * GW])
        o = R.sb("o", [P, 2, NB, OW])
        x = R.sb("x", [P, 2, D])
        wt = R.sb("wt", [P, 2, NB, AH])
        ws = R.sb("ws", [P, 2, NB, AH])
        lo = R.sb("lo", [P, 2, AH])
        den = R.sb("den", [P, 2, AH])
        ss = R.sb("ss", [P, 2, 2])
        yt = R.sb("yt", [P, 2, KD, P])
        x2 = R.sb("x2", [P, 2, D])
        h = R.sb("h", [P, 2, D])
        ht = R.sb("ht", [P, 2, KD, P])
        junk = R.sb("junk", [P, D])
        ps = m.ps
        S = R.sigs
        w_in, eps_set = R.sig("w_in", 16), R.sig("eps_set")
        tile_in, x_in = S("tile_in", 2, 16), S("x_in", 2, 16)
        diff_ready, exp_ready, sum_ready, sq_ready, y_ready = S("diff_ready"), S("exp_ready"), S("sum_ready"), S("sq_ready"), S("y_ready")
        yt_done, yt_ready, w_done = S("yt_done"), S("yt_ready"), S("w_done")
        x2_ready, xsq_ready, h_ready = S("x2_ready"), S("xsq_ready"), S("h_ready")
        x2_out, h_out = S("x2_out", 2, 16), S("h_out", 2, 16)
        ht_done, ht_ready, lg_done, lg_ready = S("ht_done"), S("ht_ready"), S("lg_done"), S("lg_ready")
        dve_self, act_self = R.plain("dve_self"), R.plain("act_self")
        gate, gain2, shift2 = m.mod[:, 2 * D:3 * D], m.mod[:, 4 * D:5 * D], m.mod[:, 3 * D:4 * D]
        with R.block() as block:
            @block.sync
            def _(sp):
                sp.dma_start(gain[:, :], row_bc(a["attn_norm"], AW)).then_inc(*w_in.inc)
                sp.dma_start(wr[:, :, :], a["w_router"]).then_inc(*w_in.inc)

                def load_y(t, b, q):
                    sp.wait_ge(*yt_done[b].n(q))
                    sp.dma_start(y[:, b, 0:GW], one(m.y_d, t)).then_inc(*tile_in[b].inc)
                    src = m.o_d[:, bass.ds(t, 1), :, :].rearrange("n a p w -> p (n a) w")
                    sp.dma_start(o[:, b, :, :], src).then_inc(*tile_in[b].inc)

                def load_x(t, b, q):
                    sp.wait_ge(*x2_ready[b].n(q))
                    sp.dma_start(x[:, b, :], one(a["x"], t)).then_inc(*x_in[b].inc)

                load_y(0, 0, 0)
                load_y(1, 1, 0)
                with sp.Fori(0, NT // 2 - 1) as i:
                    for b in range(2):
                        load_x(2 * i + b, b, i)
                        load_y(2 * i + (2 + b), b, i + 1)
                for b in range(2):
                    load_x(NT - 2 + b, b, NT // 2 - 1)

            @block.tensor
            def _(pe):
                def transposes(src, bank, done):
                    for k in range(KD):
                        last = nc.tensor.transpose(ps[:, bank + k // 4, (k % 4) * P:(k % 4 + 1) * P], src[:, k * P:(k + 1) * P], m.ident)
                    last.then_inc(*done.inc)

                def turn_y(b, q):
                    pe.wait_ge(*y_ready[b].n(q + 1))
                    b1, q1 = before(b, q)
                    pe.wait_ge(*yt_ready[b1].n(q1 + 1))
                    transposes(y[:, b, :], 0, yt_done[b])

                def turn_h(b, q):
                    pe.wait_ge(*h_ready[b].n(q + 1))
                    b1, q1 = before(b, q)
                    pe.wait_ge(*lg_ready[b1].n(q1 + 1))
                    transposes(h[:, b, :], 6, ht_done[b])

                def logits(b, q):
                    pe.wait_ge(*ht_ready[b].n(q + 1))
                    for k in range(KD):
                        last = nc.tensor.matmul(ps[:, 6, 0:NG + NE], ht[:, b, k, :], wr[:, k, :], start=(k == 0), stop=(k == KD - 1))
                    last.then_inc(*lg_done[b].inc)

                pe.wait_ge(*w_in.n(2))
                turn_y(0, 0)
                for t, b, q in steps(lambda times: pe.Fori(0, times)):
                    if not is_tile(t, NT - 1):
                        turn_y(*after(b, q))
                    if not is_tile(t, 0) and not is_tile(t, 1):
                        turn_h(b, q - 1)
                    pe.wait_ge(*yt_ready[b].n(q + 1))
                    pe.wait_ge(*x2_ready[b].n(q))
                    for n in range(2):
                        for k in range(KD):
                            last = nc.tensor.matmul(ps[:, 2 + 2 * b + n, :], yt[:, b, k, :], w[:, k, n * BANK:(n + 1) * BANK], start=(k == 0), stop=(k == KD - 1))
                    last.then_inc(*w_done[b].inc)
                    if not is_tile(t, 0) and not is_tile(t, 1):
                        logits(b, q - 1)
                for b in range(2):
                    turn_h(b, NT // 2 - 1)
                    logits(b, NT // 2 - 1)

            @block.vector
            def _(dve):
                link = Chain(dve, dve_self)
                nc.vector.memset(eps[:, :], EPS).then_inc(*eps_set.inc)
                dve.wait_ge(*w_in.n(2))

                def put_together(b, q):
                    low = o[:, b, :, AW:AW + AH]
                    dve.wait_ge(*tile_in[b].n(2 * q + 2))
                    link(nc.vector.tensor_tensor(lo[:, b, :], low[:, 0, :], low[:, 1, :], ALU.min))
                    link(nc.vector.tensor_tensor(lo[:, b, :], lo[:, b, :], low[:, 2, :], ALU.min))
                    nc.vector.tensor_tensor(wt[:, b, :, :], lo[:, b, :].unsqueeze(1).to_broadcast([P, NB, AH]), low, ALU.subtract).then_inc(*diff_ready[b].inc)
                    dve.wait_ge(*exp_ready[b].n(q + 1))
                    link(nc.vector.tensor_tensor(ws[:, b, :, :], wt[:, b, :, :], o[:, b, :, AW + AH:OW], ALU.mult))
                    link(nc.vector.tensor_reduce(den[:, b, :], ws[:, b, :, :].rearrange("p n h -> p h n"), AX.X, ALU.add))
                    link(nc.vector.reciprocal(den[:, b, :], den[:, b, :]))
                    link(nc.vector.tensor_tensor(wt[:, b, :, :], wt[:, b, :, :], den[:, b, :].unsqueeze(1).to_broadcast([P, NB, AH]), ALU.mult))
                    for n in range(NB):
                        on = o[:, b, n, 0:AW].rearrange("p (h d) -> p h d", h=AH)
                        ins = nc.vector.tensor_tensor(on, on, wt[:, b, n, :].unsqueeze(2).to_broadcast([P, AH, DH]), ALU.mult)
                    link(ins)
                    link(nc.vector.tensor_tensor(o[:, b, 0, 0:AW], o[:, b, 0, 0:AW], o[:, b, 1, 0:AW], ALU.add))
                    nc.vector.tensor_tensor(o[:, b, 0, 0:AW], o[:, b, 0, 0:AW], o[:, b, 2, 0:AW], ALU.add).then_inc(*sum_ready[b].inc)
                    dve.wait_ge(*sq_ready[b].n(q + 1))
                    link(nc.vector.reciprocal(ss[:, b, 0:1], ss[:, b, 0:1]))
                    nc.vector.scalar_tensor_tensor(y[:, b, GW:2 * GW], o[:, b, 0, 0:AW], ss[:, b, 0:1], gain[:, :], ALU.mult, ALU.mult).then_inc(*y_ready[b].inc)

                def residual(b, q):
                    dve.wait_ge(*w_done[b].n(q + 1))
                    dve.wait_ge(*x2_out[b].n(q))
                    link(nc.vector.tensor_tensor(x2[:, b, :], ps[:, 2 + 2 * b:4 + 2 * b, :].rearrange("p n w -> p (n w)"), gate, ALU.mult))
                    dve.wait_ge(*x_in[b].n(q + 1))
                    nc.vector.tensor_tensor(x2[:, b, :], x2[:, b, :], x[:, b, :], ALU.add).then_inc(*x2_ready[b].inc)
                    dve.wait_ge(*xsq_ready[b].n(q + 1))
                    link(nc.vector.reciprocal(ss[:, b, 1:2], ss[:, b, 1:2]))
                    dve.wait_ge(*h_out[b].n(q))
                    dve.wait_ge(*ht_done[b].n(q))
                    link(nc.vector.scalar_tensor_tensor(h[:, b, :], x2[:, b, :], ss[:, b, 1:2], gain2, ALU.mult, ALU.mult))
                    nc.vector.tensor_tensor(h[:, b, :], h[:, b, :], shift2, ALU.add).then_inc(*h_ready[b].inc)

                PT, RS = 9, 3
                put_together(0, 0)
                put_together(1, 0)
                put_together(0, 1)
                with link.loop(NT // 2 - 2, 2 * (PT + RS)) as i:
                    residual(0, i)
                    put_together(1, i + 1)
                    residual(1, i)
                    put_together(0, i + 2)
                residual(0, NT // 2 - 2)
                put_together(1, NT // 2 - 1)
                residual(1, NT // 2 - 2)
                residual(0, NT // 2 - 1)
                residual(1, NT // 2 - 1)

            @block.scalar
            def _(act):
                link = Chain(act, act_self)
                act.wait_ge(*eps_set.n(1))
                act.wait_ge(*w_in.n(2))

                def put_together(b, q):
                    act.wait_ge(*diff_ready[b].n(q + 1))
                    nc.scalar.activation(wt[:, b, :, :], wt[:, b, :, :], ACT.Exp).then_inc(*exp_ready[b].inc)
                    act.wait_ge(*sum_ready[b].n(q + 1))
                    link(nc.scalar.activation(junk[:, 0:AW], o[:, b, 0, 0:AW], ACT.Square, accum_out=ss[:, b, 0:1]))
                    nc.scalar.activation(ss[:, b, 0:1], ss[:, b, 0:1], ACT.Sqrt, bias=eps[:, :], scale=1.0 / AW).then_inc(*sq_ready[b].inc)

                def take_yt(b, q):
                    act.wait_ge(*yt_done[b].n(q + 1))
                    act.wait_ge(*w_done[b].n(q))
                    nc.scalar.copy(yt[:, b, :, :].rearrange("p k n -> p (k n)"), ps[:, 0:2, :].rearrange("p k n -> p (k n)")).then_inc(*yt_ready[b].inc)

                def take_ht(b, q):
                    act.wait_ge(*ht_done[b].n(q + 1))
                    act.wait_ge(*lg_done[b].n(q))
                    nc.scalar.copy(ht[:, b, :, :].rearrange("p k n -> p (k n)"), ps[:, 6:8, :].rearrange("p k n -> p (k n)")).then_inc(*ht_ready[b].inc)

                def take_logits(t, b, q):
                    act.wait_ge(*lg_done[b].n(q + 1))
                    nc.scalar.copy(m.lg[:, bass.ds(t * (NG + NE), NG + NE)], ps[:, 6, 0:NG + NE]).then_inc(*lg_ready[b].inc)

                def residual(t, b, q):
                    act.wait_ge(*x2_ready[b].n(q + 1))
                    link(nc.scalar.activation(junk[:, :], x2[:, b, :], ACT.Square, accum_out=ss[:, b, 1:2]))
                    nc.scalar.activation(ss[:, b, 1:2], ss[:, b, 1:2], ACT.Sqrt, bias=eps[:, :], scale=1.0 / D).then_inc(*xsq_ready[b].inc)
                    act.dma_start(one(m.x2_d, t), x2[:, b, :]).then_inc(*x2_out[b].inc)
                    act.wait_ge(*h_ready[b].n(q + 1))
                    act.dma_start(one(m.h_d, t), h[:, b, :]).then_inc(*h_out[b].inc)

                put_together(0, 0)
                take_yt(0, 0)
                put_together(1, 0)
                for t, b, q in steps(lambda times: link.loop(times, 4)):
                    early = is_tile(t, 0) or is_tile(t, 1)
                    late = is_tile(t, NT - 2) or is_tile(t, NT - 1)
                    if not is_tile(t, NT - 1):
                        take_yt(*after(b, q))
                    if not early:
                        take_ht(b, q - 1)
                    if not is_tile(t, 0):
                        residual(t - 1, *before(b, q))
                    if not late:
                        put_together(b, q + 1)
                    if not early:
                        take_logits(t - 2, b, q - 1)
                q = NT // 2 - 1
                take_ht(0, q)
                take_logits(NT - 2, 0, q)
                residual(NT - 1, 1, q)
                take_ht(1, q)
                take_logits(NT - 1, 1, q)
                for b in range(2):
                    act.wait_ge(*x2_out[b].n(NT // 2))
                    act.wait_ge(*h_out[b].n(NT // 2))
                    act.wait_ge(*lg_ready[b].n(NT // 2))
def route(nc, m, a):
    LW = NG + NE
    BIG = 64.0
    with Room(nc, "ro") as R:
        gm = R.sb("gm", [P, NT])
        eg = R.sb("eg", [P, NT, NG])
        gs = R.sb("gs", [P, NT])
        gone = R.sb("gone", [P, NT, NG])
        gi = R.sb("gi", [P, NT])
        el = R.sb("el", [P, NT, NE])
        t1 = R.sb("t1", [P, NT, NE])
        mx = R.sb("mx", [P, 2, NT])
        idx = R.sb("idx", [P, NT])
        hot = R.sb("hot", [P, 2, NT, NE])
        both = R.sb("both", [P, NT, NE])
        e2 = R.sb("e2", [P, NT])
        carry = R.sb("carry", [P, NT + 1, NE])
        pad = R.sb("pad", [P, NE])
        padi = R.sb("padi", [P, NE], I32)
        ends = R.sb("ends", [P, NE])
        destf = R.sb("destf", [P, 2, NT])
        pos = R.sb("pos", [P, 2, NT], I32)
        part = R.sb("part", [P, 2, NT], I32)
        cmp = R.sb("cmp", [P, NBLK, NE])
        some = R.sb("some", [P, NE])
        rank = R.sb("rank", [P, NE])
        first = R.sb("first", [P, NE + 1])
        none = R.sb("none", [P, NE])
        started = R.sb("started", [P, NBLK])
        starti = R.sb("starti", [P, NBLK], I32)
        sq = R.sb("sq", [P, NE, NE])
        sq2 = R.sb("sq2", [P, NE, NE])
        toki = R.sb("toki", [P, NT], I32)
        zero = R.sb("zero", [P, NBLK], I32)
        ps = m.ps
        dve_self = R.plain("dve_self")
        gsub_ready, gexp_ready, esub_ready, eexp_ready = R.sig("gsub_ready"), R.sig("gexp_ready"), R.sig("esub_ready"), R.sig("eexp_ready")
        both_ready, ranks_done, zero_set, zero_out, pos_ready = R.sig("both_ready"), R.sig("ranks_done"), R.sig("zero_set"), R.sig("zero_out", 16), R.sig("pos_ready")
        tok_out, tok_in = R.plain("tok_out"), R.sig("tok_in", 16)
        tok_all = R.sig("tok_all")
        lg = m.lg[:, :].rearrange("p (t n) -> p t n", n=LW)
        gl = lg[:, :, 0:NG]

        def over(ap, n):
            return ap.unsqueeze(2).to_broadcast([P, ap.shape[1], n])

        def iota(n):
            return m.cst[:, C_IOTA:C_IOTA + n].unsqueeze(1).to_broadcast([P, NT, n])

        with R.block() as block:
            @block.sync
            def _(sp):
                sp.wait_ge(*zero_set.n(1))
                sp.dma_start(m.slot_tok_d, zero[:, :]).then_inc(*zero_out.inc)
                sp.wait_ge(*tok_all.n(1))
                sp.dma_start(m.slot_tok[:, 0:NBLK], m.slot_tok_d).then_inc(*tok_in.inc)
                sp.wait_ge(*tok_in.n(1))

            @block.vector
            def _(dve):
                link = Chain(dve, dve_self)
                V = nc.vector

                def first_of(one_hot, values, top, n):
                    link(V.tensor_tensor(one_hot, values, over(top, n), ALU.is_equal))
                    link(V.tensor_scalar(one_hot, one_hot, -BIG, BIG, ALU.mult, ALU.add))
                    link(V.tensor_tensor(one_hot, one_hot, iota(n), ALU.add))
                    link(V.tensor_reduce(idx[:, :], one_hot, AX.X, ALU.min))
                    link(V.tensor_tensor(one_hot, iota(n), over(idx[:, :], n), ALU.is_equal))

                V.memset(zero[:, :], 0).then_inc(*zero_set.inc)
                link(V.memset(m.slot_tok[:, NBLK:NBLK + 1], 0))
                link(V.tensor_reduce(gm[:, :], gl, AX.X, ALU.max))
                V.tensor_tensor(eg[:, :, :], gl, over(gm[:, :], NG), ALU.subtract).then_inc(*gsub_ready.inc)
                first_of(gone[:, :, :], gl, gm[:, :], NG)
                dve.wait_ge(*gexp_ready.n(1))
                link(V.tensor_reduce(gs[:, :], eg[:, :, :], AX.X, ALU.add))
                link(V.tensor_scalar(gone[:, :, :], gone[:, :, :], -NEG, NEG, ALU.mult, ALU.add))
                for g in range(NG):
                    ins = V.tensor_tensor(el[:, :, g * EG:(g + 1) * EG], lg[:, :, NG + g * EG:NG + (g + 1) * EG], gone[:, :, g:g + 1].to_broadcast([P, NT, EG]), ALU.add)
                link(ins)
                for n in range(2):
                    link(V.tensor_reduce(mx[:, n, :], el[:, :, :], AX.X, ALU.max))
                    first_of(hot[:, n, :, :], el[:, :, :], mx[:, n, :], NE)
                    if n == 0:
                        link(V.scalar_tensor_tensor(el[:, :, :], hot[:, 0, :, :], 2 * NEG, el[:, :, :], ALU.mult, ALU.add))
                V.tensor_tensor(both[:, :, :], hot[:, 0, :, :], hot[:, 1, :, :], ALU.add).then_inc(*both_ready.inc)
                V.tensor_tensor(e2[:, :], mx[:, 1, :], mx[:, 0, :], ALU.subtract).then_inc(*esub_ready.inc)
                dve.wait_ge(*eexp_ready.n(1))
                link(V.scalar_tensor_tensor(gs[:, :], e2[:, :], 1.0, gs[:, :], ALU.add, ALU.mult))
                link(V.reciprocal(m.gate[:, 0, :], gs[:, :]))
                link(V.tensor_tensor(m.gate[:, 1, :], m.gate[:, 0, :], e2[:, :], ALU.mult))
                dve.wait_ge(*ranks_done.n(1))
                link(V.memset(carry[:, 0, :], 0.0))
                for t in range(NT):
                    link(V.tensor_tensor(carry[:, t + 1, :], carry[:, t, :], ps[:, 1, t * NE:(t + 1) * NE], ALU.add))
                link(V.tensor_scalar(pad[:, :], carry[:, NT, :], float(P - 1), None, ALU.add))
                link(V.tensor_copy(padi[:, :], pad[:, :]))
                link(V.tensor_scalar(padi[:, :], padi[:, :], 7, 7, ALU.arith_shift_right, ALU.logical_shift_left))
                link(V.tensor_copy(pad[:, :], padi[:, :]))
                link(V.tensor_tensor_scan(ends[:, :], m.ones[:, 0:NE], pad[:, :], 0.0, ALU.mult, ALU.add))
                link(V.tensor_tensor(pad[:, :], ends[:, :], pad[:, :], ALU.subtract))
                link(V.tensor_tensor(el[:, :, :], ps[:, 0, :].rearrange("p (t e) -> p t e", e=NE), carry[:, 0:NT, :], ALU.add))
                link(V.tensor_tensor(el[:, :, :], el[:, :, :], pad[:, :].unsqueeze(1).to_broadcast([P, NT, NE]), ALU.add))
                for n in range(2):
                    link(V.tensor_tensor(t1[:, :, :], el[:, :, :], hot[:, n, :, :], ALU.mult))
                    link(V.tensor_reduce(destf[:, n, :], t1[:, :, :], AX.X, ALU.add))
                link(V.tensor_copy(m.dest[:, :, :], destf[:, :, :]))
                link(V.tensor_scalar(part[:, :, :], m.dest[:, :, :], 7, None, ALU.arith_shift_right))
                link(V.tensor_scalar(pos[:, :, :], m.dest[:, :, :], P - 1, None, ALU.bitwise_and))
                link(V.tensor_copy(destf[:, :, :], part[:, :, :]))
                link(V.scalar_tensor_tensor(destf[:, :, :], pos[:, :, :], float(NBLK), destf[:, :, :], ALU.mult, ALU.add))
                link(V.tensor_copy(toki[:, :], m.cst[:, C_TOK:C_TOK + NT]))
                V.tensor_copy(pos[:, :, :], destf[:, :, :]).then_inc(*pos_ready.inc)
                link(V.tensor_tensor(some[:, :], ends[:, :], pad[:, :], ALU.is_gt))
                link(V.tensor_tensor_scan(rank[:, :], m.ones[:, 0:NE], some[:, :], 0.0, ALU.mult, ALU.add))
                link(V.tensor_tensor(rank[:, :], rank[:, :], some[:, :], ALU.mult))
                iota_n = m.cst[:, C_IOTA:C_IOTA + NE].unsqueeze(2).to_broadcast([P, NE, NE])
                link(V.tensor_scalar(rank[:, :], rank[:, :], -1.0, None, ALU.add))
                link(V.tensor_tensor(sq[:, :, :], iota_n, rank[:, :].unsqueeze(1).to_broadcast([P, NE, NE]), ALU.is_equal))
                link(V.tensor_tensor(sq2[:, :, :], sq[:, :, :], m.cst[:, C_IOTA:C_IOTA + NE].unsqueeze(1).to_broadcast([P, NE, NE]), ALU.mult))
                link(V.tensor_reduce(none[:, :], sq2[:, :, :], AX.X, ALU.add))
                link(V.tensor_copy(m.by_expert[:, 0, :], none[:, :]))
                link(V.tensor_tensor(sq2[:, :, :], sq[:, :, :], pad[:, :].unsqueeze(1).to_broadcast([P, NE, NE]), ALU.mult))
                link(V.memset(first[:, 0:1], 0.0))
                link(V.tensor_reduce(first[:, 1:NE + 1], sq2[:, :, :], AX.X, ALU.add))
                link(V.tensor_reduce(none[:, :], sq[:, :, :], AX.X, ALU.add))
                link(V.tensor_scalar(none[:, :], none[:, :], -1.0, 1.0, ALU.mult, ALU.add))
                link(V.scalar_tensor_tensor(first[:, 1:NE + 1], none[:, :], ends[:, NE - 1:NE], first[:, 1:NE + 1], ALU.mult, ALU.add))
                link(V.tensor_scalar(first[:, :], first[:, :], 1.0 / P, None, ALU.mult))
                link(V.tensor_copy(m.by_expert[:, 1, :], first[:, 0:NE]))
                link(V.tensor_scalar(none[:, :], some[:, :], NEG, -NEG, ALU.mult, ALU.add))
                link(V.tensor_tensor(none[:, :], none[:, :], pad[:, :], ALU.add))
                link(V.tensor_tensor(cmp[:, :, :], m.cst[:, C_BLK:C_BLK + NBLK].unsqueeze(2).to_broadcast([P, NBLK, NE]), none[:, :].unsqueeze(1).to_broadcast([P, NBLK, NE]), ALU.is_ge))
                link(V.tensor_reduce(started[:, :], cmp[:, :, :], AX.X, ALU.add))
                link(V.tensor_copy(starti[:, :], started[:, :]))
                link(V.tensor_scalar(m.by_block[:, 1, :], starti[:, :], 1, None, ALU.arith_shift_right))
                link(V.tensor_scalar(started[:, :], started[:, :], 1.0, None, ALU.add))
                link(V.tensor_copy(starti[:, :], started[:, :]))
                link(V.tensor_scalar(m.by_block[:, 0, :], starti[:, :], 1, None, ALU.arith_shift_right))
                link(V.tensor_scalar(m.by_block[:, 2, :], starti[:, :], 1, None, ALU.bitwise_and))
                link(V.tensor_scalar(none[:, 0:1], ends[:, NE - 1:NE], 1.0 / P, -1.0, ALU.mult, ALU.add))
                link(V.tensor_copy(padi[:, 0:1], none[:, 0:1]))
                link(V.tensor_scalar(m.pairs[:, 0:1], padi[:, 0:1], 1, None, ALU.arith_shift_right))
                link(V.tensor_scalar(m.pairs[:, 1:2], m.pairs[:, 0:1], -1.0, float(NBLK // 2 - 1), ALU.mult, ALU.add))

            @block.scalar
            def _(act):
                act.wait_ge(*gsub_ready.n(1))
                nc.scalar.activation(eg[:, :, :], eg[:, :, :], ACT.Exp).then_inc(*gexp_ready.inc)
                act.wait_ge(*esub_ready.n(1))
                nc.scalar.activation(e2[:, :], e2[:, :], ACT.Exp).then_inc(*eexp_ready.inc)

            @block.tensor
            def _(pe):
                pe.wait_ge(*both_ready.n(1))
                rows = both[:, :, :].rearrange("p t e -> p (t e)")
                nc.tensor.matmul(ps[:, 0, :], m.cst[:, C_US:C_US + P], rows, start=True, stop=True)
                nc.tensor.matmul(ps[:, 1, :], m.ones, rows, start=True, stop=True).then_inc(*ranks_done.inc)

            @block.gpsimd
            def _(pool):
                pool.wait_ge(*pos_ready.n(1))
                pool.wait_ge(*zero_out.n(1))
                flat = m.slot_tok_d.rearrange("p b -> (p b)").unsqueeze(1)
                for t in range(NT):
                    for n in range(2):
                        pool.indirect_dma_start(out=flat, out_offset=bass.IndirectOffsetOnAxis(ap=pos[:, n, t:t + 1].bitcast(U32), axis=0),
                                                in_=toki[:, t:t + 1], in_offset=None).then_inc(tok_out, 16)
                pool.wait_ge(tok_out, 2 * NT * 16)
                pool.sem_inc(*tok_all.inc)


def experts(nc, m, a):
    with Room(nc, "ex") as R:
        idx = R.sb("idx", [P, 2], I32)
        xg = R.sb("xg", [P, 2, D])
        xt = R.sb("xt", [P, 2, KD, P])
        wgu = R.sb("wgu", [P, 2 * KD * 2 * DE])
        wd = R.sb("wd", [P, 2 * (DE // P) * D])
        sg = R.sb("sg", [P, 2, DE])
        hid = R.sb("hid", [P, 2, DE])
        hidt = R.sb("hidt", [P, 2, DE // P, P])
        y = R.sb("y", [P, 2, D])
        zero = R.sb("zero", [P, D])
        ps = m.ps
        S = R.sigs
        idx_ready, xg_in, seen = S("idx_ready"), [R.plain("xg_in0"), R.plain("xg_in1")], R.plain("seen")
        zero_set, zero_out, seen_sp = R.sig("zero_set"), R.sig("zero_out", 16), R.plain("seen_sp")
        seen_act = R.plain("seen_act")
        wgu_in, wd_in = S("wgu_in", 2, 16), S("wd_in", 2, 16)
        gu_done, y_done = R.sig("gu_done"), R.sig("y_done")
        xt_done, xt_ready, sg_ready, hid_ready = S("xt_done"), S("xt_ready"), S("sg_ready"), S("hid_ready")
        ht_done, ht_ready, y_ready, out = S("ht_done"), S("ht_ready"), S("y_ready"), S("out", 2, 16)
        gate = m.mod[:, 5 * D:6 * D]
        WGU, WD = KD * 2 * DE, DE // P * D

        def blocks(eng):
            pairs = eng.value_load(m.pairs[0:1, 0:1], min_val=1, max_val=NBLK // 2 - 1)
            yield 0, 0, 0, True, False
            with eng.Fori(0, NBLK // 2 - 1) as i:
                with eng.If(i < pairs):
                    yield i * 2 + 1, 1, i, False, False
                    yield i * 2 + 2, 0, i + 1, False, False
            yield pairs * 2 + 1, 1, pairs, False, True

        with R.block() as block:
            @block.sync
            def _(sp):
                with sp.Fori(0, NE // 2) as i:
                    for b in range(2):
                        e = sp.value_load(m.by_expert[0:1, 0, bass.ds(2 * i + b, 1)], min_val=0, max_val=NE - 1)
                        free = sp.value_load(m.by_expert[0:1, 1, bass.ds(2 * i + b, 1)], min_val=0, max_val=NBLK)
                        sp.wait_ge(*gu_done.n(free))
                        sp.dma_start(wgu[:, b * WGU:(b + 1) * WGU].rearrange("p (k n) -> p k n", k=KD), one(a["w_gate_up"], e)).then_inc(*wgu_in[b].inc)
                        sp.wait_ge(*y_done.n(free))
                        sp.dma_start(wd[:, b * WD:(b + 1) * WD].rearrange("p (k n) -> p k n", k=DE // P), one(a["w_down"], e)).then_inc(*wd_in[b].inc)
                for b in range(2):
                    sp.wait_ge(*wgu_in[b].n(NE // 2))
                    sp.wait_ge(*wd_in[b].n(NE // 2))
                pairs = sp.value_load(m.pairs[0:1, 0:1], min_val=1, max_val=NBLK // 2 - 1)
                sp.wait_ge(*zero_set.n(1))
                with sp.Fori(0, NBLK // 2 - 1) as i:
                    with sp.If(pairs <= i):
                        for b in range(2):
                            sp.dma_start(one(m.ys_d, 2 * i + (2 + b)), zero[:, :]).then_inc(*zero_out.inc)
                unused = sp.value_load(m.pairs[0:1, 1:2], min_val=0, max_val=NBLK // 2 - 1)
                sp.wait_ge(*zero_out.n(unused * 2))
                sp.sem_inc(seen_sp, 1)

            @block.gpsimd
            def _(pool):
                rows = m.h_d.rearrange("t p n -> (t p) n")
                for t, b, q, head, tail in blocks(pool):
                    pool.wait_ge(*xt_done[b].n(q))
                    pool.sem_inc(seen, 1)
                    pool.wait_ge(*idx_ready[b].n(q + 1))
                    pool.sem_inc(seen, 1)
                    pool.indirect_dma_start(out=xg[:, b, :], out_offset=None, in_=rows,
                                            in_offset=bass.IndirectOffsetOnAxis(ap=idx[:, b:b + 1].bitcast(U32), axis=0)).then_inc(xg_in[b], 16)

            @block.tensor
            def _(pe):
                def turn_x(b, q):
                    pe.wait_ge(xg_in[b], q * 16 + 16)
                    b1, q1 = before(b, q)
                    pe.wait_ge(*xt_ready[b1].n(q1 + 1))
                    for k in range(KD):
                        last = nc.tensor.transpose(ps[:, k // 4, (k % 4) * P:(k % 4 + 1) * P], xg[:, b, k * P:(k + 1) * P], m.ident)
                    last.then_inc(*xt_done[b].inc)

                def weights_of(t):
                    loads = [pe.value_load(m.by_block[0:1, p, bass.ds(t, 1)], min_val=0, max_val=NE // 2) for p in range(2)]
                    return loads, pe.value_load(m.by_block[0:1, 2, bass.ds(t, 1)], min_val=0, max_val=1)

                def wait_for(loaded, loads):
                    for p in range(2):
                        pe.wait_ge(*loaded[p].n(loads[p]))

                def gate_up(b, q, loads, half):
                    wait_for(wgu_in, loads)
                    pe.wait_ge(*xt_ready[b].n(q + 1))
                    pe.wait_ge(*hid_ready[b].n(q))
                    for k in range(KD):
                        last = nc.tensor.matmul(ps[:, 2 + b, :], xt[:, b, k, :], wgu[:, bass.ds(half * WGU + k * 2 * DE, 2 * DE)], start=(k == 0), stop=(k == KD - 1))
                    last.then_inc(*gu_done.inc)

                def down(b, q, loads, half):
                    wait_for(wd_in, loads)
                    pe.wait_ge(*ht_ready[b].n(q + 1))
                    b1, q1 = before(b, q)
                    pe.wait_ge(*y_ready[b1].n(q1 + 1))
                    for n in range(2):
                        for k in range(DE // P):
                            last = nc.tensor.matmul(ps[:, 6 + n, :], hidt[:, b, k, :], wd[:, bass.ds(half * WD + (k * D + n * BANK), BANK)], start=(k == 0), stop=(k == DE // P - 1))
                    last.then_inc(*y_done.inc)

                turn_x(0, 0)
                gate_up(0, 0, *weights_of(0))
                for t, b, q, head, tail in blocks(pe):
                    if not head:
                        weights = weights_of(t - 1)
                    if not tail:
                        next_weights = weights_of(t + 1)
                        turn_x(*after(b, q))
                    if not head:
                        down(*before(b, q), *weights)
                    pe.wait_ge(*hid_ready[b].n(q + 1))
                    b1, q1 = before(b, q)
                    pe.wait_ge(*ht_ready[b1].n(q1 + 1))
                    for k in range(DE // P):
                        last = nc.tensor.transpose(ps[:, 4, k * P:(k + 1) * P], hid[:, b, k * P:(k + 1) * P], m.ident)
                    last.then_inc(*ht_done[b].inc)
                    if not tail:
                        gate_up(*after(b, q), *next_weights)
                down(1, q, *weights_of(t))

            @block.scalar
            def _(act):
                def take_x(t, b, q):
                    act.wait_ge(*xt_done[b].n(q + 1))
                    if not is_tile(t, 0) and not is_tile(t, 1):
                        act.wait_ge(*gu_done.n(t - 1))
                    nc.scalar.copy(xt[:, b, :, :].rearrange("p k n -> p (k n)"), ps[:, 0:2, :].rearrange("p k n -> p (k n)")).then_inc(*xt_ready[b].inc)

                def store_y(t, b, q):
                    act.wait_ge(*y_ready[b].n(q + 1))
                    act.dma_start(one(m.ys_d, t), y[:, b, :]).then_inc(*out[b].inc)

                take_x(0, 0, 0)
                for t, b, q, head, tail in blocks(act):
                    act.wait_ge(*gu_done.n(t + 1))
                    act.wait_ge(*hid_ready[b].n(q))
                    nc.scalar.activation(sg[:, b, :], ps[:, 2 + b, 0:DE], ACT.Silu).then_inc(*sg_ready[b].inc)
                    if not tail:
                        take_x(t + 1, *after(b, q))
                    act.wait_ge(*ht_done[b].n(q + 1))
                    if not is_tile(t, 0) and not is_tile(t, 1):
                        act.wait_ge(*y_done.n(t - 1))
                    nc.scalar.copy(hidt[:, b, :, :].rearrange("p k n -> p (k n)"), ps[:, 4, 0:DE]).then_inc(*ht_ready[b].inc)
                    if not head:
                        store_y(t - 1, *before(b, q))
                store_y(t, 1, q)
                for b in range(2):
                    act.wait_ge(*out[b].n(q + 1))
                    act.sem_inc(seen_act, 1)

            @block.vector
            def _(dve):
                nc.vector.memset(zero[:, :], 0.0).then_inc(*zero_set.inc)

                def take_y(t, b, q):
                    dve.wait_ge(*y_done.n(t + 1))
                    dve.wait_ge(*out[b].n(q))
                    nc.vector.tensor_tensor(y[:, b, :], ps[:, 6:8, :].rearrange("p n w -> p (n w)"), gate, ALU.mult).then_inc(*y_ready[b].inc)

                def take_idx(t, b):
                    nc.vector.tensor_copy(idx[:, b:b + 1], m.slot_tok[:, bass.ds(t, 1)]).then_inc(*idx_ready[b].inc)

                take_idx(0, 0)
                take_idx(1, 1)
                for t, b, q, head, tail in blocks(dve):
                    dve.wait_ge(*gu_done.n(t + 1))
                    dve.wait_ge(*sg_ready[b].n(q + 1))
                    dve.wait_ge(*ht_done[b].n(q))
                    nc.vector.tensor_tensor(hid[:, b, :], sg[:, b, :], ps[:, 2 + b, DE:], ALU.mult).then_inc(*hid_ready[b].inc)
                    if not tail:
                        dve.wait_ge(xg_in[b], q * 16 + 16)
                        take_idx(t + 2, b)
                    if not head:
                        take_y(t - 1, *before(b, q))
                take_y(t, 1, q)


def finish(nc, m, a):
    NBUF = 4
    with Room(nc, "fi") as R:
        idx = R.sb("idx", [P, NBUF, 2], I32)
        yg = R.sb("yg", [P, NBUF, 2, D])
        x = R.sb("x", [P, NBUF, D])
        gain = R.sb("gain", [P, D])
        o = R.sb("o", [P, NBUF, D])
        junk = R.sb("junk", [P, D])
        ss = R.sb("ss", [P, NBUF])
        eps = R.sb("eps", [P, 1])
        def S(name, step=1):
            return R.sigs(name, NBUF, step)

        gain_in, eps_set = R.sig("gain_in", 16), R.sig("eps_set")
        x_in, yg_in, seen = S("x_in", 16), [R.plain(f"yg_in{b}") for b in range(NBUF)], R.plain("seen")
        idx_ready, scaled, sum_ready, sq_ready, o_ready, out = S("idx_ready"), S("scaled"), S("sum_ready"), S("sq_ready"), S("o_ready"), S("out", 16)
        dve_self, act_self = R.plain("dve_self"), R.plain("act_self")
        N = NT // NBUF
        with R.block() as block:
            @block.sync
            def _(sp):
                sp.dma_start(gain[:, :], row_bc(a["norm_final"], D)).then_inc(*gain_in.inc)
                with sp.Fori(0, N) as i:
                    for b in range(NBUF):
                        sp.wait_ge(*sum_ready[b].n(i))
                        sp.dma_start(x[:, b, :], one(m.x2_d, NBUF * i + b)).then_inc(*x_in[b].inc)

            @block.gpsimd
            def _(pool):
                rows = m.ys_d.rearrange("t p n -> (t p) n")
                with pool.Fori(0, N) as i:
                    for b in range(NBUF):
                        pool.wait_ge(*sum_ready[b].n(i))
                        pool.sem_inc(seen, 1)
                        pool.wait_ge(*idx_ready[b].n(i + 1))
                        pool.sem_inc(seen, 1)
                        for n in range(2):
                            pool.indirect_dma_start(out=yg[:, b, n, :], out_offset=None, in_=rows,
                                                    in_offset=bass.IndirectOffsetOnAxis(ap=idx[:, b, n:n + 1].bitcast(U32), axis=0)).then_inc(yg_in[b], 16)

            @block.scalar
            def _(act):
                link = Chain(act, act_self)
                act.wait_ge(*eps_set.n(1))
                with link.loop(N, NBUF) as i:
                    for b in range(NBUF):
                        act.wait_ge(yg_in[b], i * 32 + 32)
                        nc.scalar.activation(yg[:, b, 0, :], yg[:, b, 0, :], ACT.Copy, scale=m.gate[:, 0, bass.ds(NBUF * i + b, 1)]).then_inc(*scaled[b].inc)
                    for b in range(NBUF):
                        act.wait_ge(*sum_ready[b].n(i + 1))
                        link(nc.scalar.activation(junk[:, :], o[:, b, :], ACT.Square, accum_out=ss[:, b:b + 1]))
                        nc.scalar.activation(ss[:, b:b + 1], ss[:, b:b + 1], ACT.Sqrt, bias=eps[:, :], scale=1.0 / D).then_inc(*sq_ready[b].inc)
                    for b in range(NBUF):
                        act.wait_ge(*o_ready[b].n(i + 1))
                        act.dma_start(one(m.out, NBUF * i + b), o[:, b, :]).then_inc(*out[b].inc)
                for b in range(NBUF):
                    act.wait_ge(*out[b].n(N))

            @block.vector
            def _(dve):
                link = Chain(dve, dve_self)
                V = nc.vector
                V.memset(eps[:, :], EPS).then_inc(*eps_set.inc)
                dve.wait_ge(*gain_in.n(1))

                def take_idx(t, b):
                    V.tensor_copy(idx[:, b, :], m.dest[:, :, bass.ds(t, 1)].rearrange("p n a -> p (n a)")).then_inc(*idx_ready[b].inc)

                def tiles(i, ahead):
                    for b in range(NBUF):
                        dve.wait_ge(*scaled[b].n(i + 1))
                        dve.wait_ge(yg_in[b], i * 32 + 32)
                        if ahead:
                            take_idx(NBUF * i + NBUF + b, b)
                        dve.wait_ge(*out[b].n(i))
                        link(V.scalar_tensor_tensor(o[:, b, :], yg[:, b, 1, :], m.gate[:, 1, bass.ds(NBUF * i + b, 1)], yg[:, b, 0, :], ALU.mult, ALU.add))
                        dve.wait_ge(*x_in[b].n(i + 1))
                        V.tensor_tensor(o[:, b, :], o[:, b, :], x[:, b, :], ALU.add).then_inc(*sum_ready[b].inc)
                    for b in range(NBUF):
                        dve.wait_ge(*sq_ready[b].n(i + 1))
                        link(V.reciprocal(ss[:, b:b + 1], ss[:, b:b + 1]))
                        V.scalar_tensor_tensor(o[:, b, :], o[:, b, :], ss[:, b:b + 1], gain[:, :], ALU.mult, ALU.mult).then_inc(*o_ready[b].inc)

                for b in range(NBUF):
                    take_idx(b, b)
                with link.loop(N - 1, 2 * NBUF) as i:
                    tiles(i, True)
                tiles(N - 1, False)
class Shared:
    pass


def attention_part(nc, m, a):
    with nc.sbuf_tensor("bias", [P, NB, AH, 2 * P], F32) as m.bias:
        bias_tables(nc, m, a)
        attention(nc, m, a)


PHASES = (adaln, project_tokens, project_channels, deltanet_gates, deltanet, attention_part, mix_out, route, experts, finish)


def block_kernel(nc, a, out):
    m = Shared()
    m.NCH = NCONV + 2 * AW // P
    m.out = out
    with ExitStack() as ctx:
        def sb(name, shape, dt=F32):
            return ctx.enter_context(nc.sbuf_tensor(name, shape, dt))

        def dram(name, shape, dt=F32):
            return nc.dram_tensor(name, shape, dt, kind="Internal").ap()

        m.cst = sb("cst", [P, C_END])
        m.mod = sb("mod", [P, 6 * D])
        m.rstd = sb("rstd", [P, NT])
        m.ba = sb("ba", [P, NT * 8])
        m.g = sb("g", [P, NT, GH])
        m.gsum = sb("gsum", [P, NT * GH])
        m.beta, m.nbe = sb("beta", [P, NT * GH]), sb("nbe", [P, NT * GH])
        m.kdec, m.sdec = sb("kdec", [P, NT * GH]), sb("sdec", [P, NT * GH])
        m.lg = sb("lg", [P, NT * (NG + NE)])
        m.gate = sb("gate", [P, 2, NT])
        m.dest = sb("dest", [P, 2, NT], I32)
        m.by_expert = sb("by_expert", [P, 2, NE], I32)
        m.by_block = sb("by_block", [P, 3, NBLK], I32)
        m.pairs = sb("pairs", [P, 2], I32)
        m.slot_tok = sb("slot_tok", [P, NBLK + 1], I32)
        m.ps = ctx.enter_context(nc.psum_tensor("ps", [P, 8, BANK], F32))
        m.ident, m.ones = m.cst[:, C_ID:C_ID + P], m.cst[:, C_ONE:C_ONE + P]
        m.z_d = dram("z_d", [NT, P, GW])
        m.v_d = dram("v_d", [NT, P, AW])
        m.y_d = dram("y_d", [NT, P, GW])
        m.bias_d = dram("bias_d", [AH, NB * BIAS_W])
        m.o_d = dram("o_d", [NB, NT, P, AW + 2 * AH])
        m.x2_d = dram("x2_d", [NT, P, D])
        m.h_d = dram("h_d", [NT, P, D])
        m.slot_tok_d = dram("slot_tok_d", [P, NBLK], I32)
        m.ys_d = dram("ys_d", [NBLK, P, D])
        m.ch_d = dram("ch_d", [m.NCH, P, T])
        with ExitStack() as early:
            m.ht = early.enter_context(nc.sbuf_tensor("ht", [P, KD, T], F32))
            for phase in PHASES[:3]:
                phase(nc, m, a)
        with ExitStack() as middle:
            m.qk = middle.enter_context(nc.sbuf_tensor("qk", [P, 2 * AW // P, T], F32))
            for phase in PHASES[3:5]:
                phase(nc, m, a)
            m.w_out = middle.enter_context(nc.sbuf_tensor("w_out", [P, KD, D], F32))
            for phase in PHASES[5:7]:
                phase(nc, m, a)
        for phase in PHASES[7:]:
            phase(nc, m, a)


def kernel(**inputs):
    import numpy as np
    import concourse.bacc as bacc
    from concourse import mybir as _mybir
    from concourse.bass_utils import run_bass_kernel_spmd as run

    def chunks(w):
        return np.moveaxis(w.reshape(*w.shape[:-2], w.shape[-2] // P, P, w.shape[-1]), -3, -2)

    x = {k: np.asarray(v) for k, v in inputs.items()}
    w_in = x["w_in"][0]
    s1 = NCONV * P
    s2, s3 = s1 + GW, s1 + GW + 2 * GH
    w_conv = x["w_conv"][0]
    cst, bucket_one, bucket_off = bucket_constants()
    arrays = {
        "x": x["x"].reshape(NT, P, D),
        "c": x["c"].reshape(KD, P).T,
        "w_ada": chunks(x["w_ada"][0]).reshape(P, KD, 6 * D // BANK, BANK).transpose(2, 0, 1, 3),
        "b_ada": x["b_ada"],
        "norm_mix": x["norm_mix"], "norm_ffn": x["norm_ffn"], "norm_final": x["norm_final"],
        "gdn_norm": x["gdn_norm"], "attn_norm": x["attn_norm"],
        "a_log": x["a_log"], "dt_bias": x["dt_bias"], "rel_bias": x["rel_bias"],
        "w_tok": chunks(np.concatenate([w_in[:, s1:s2], w_in[:, s3 + 2 * AW:], w_in[:, s2:s3]], 1)),
        "w_chan": chunks(np.concatenate([w_in[:, :s1], w_in[:, s3:s3 + 2 * AW]], 1)).reshape(P, KD, -1, P).transpose(2, 0, 1, 3),
        "w_conv": w_conv.reshape(CONV, NCONV, P).transpose(2, 1, 0).reshape(P, NCONV * CONV),
        "w_out": chunks(x["w_out"][0]),
        "w_router": chunks(np.concatenate([x["w_router_group"][0], x["w_router_expert"][0]], 1)),
        "w_gate_up": chunks(np.concatenate([x["w_gate"][0], x["w_up"][0]], 2)),
        "w_down": chunks(x["w_down"][0]),
        "cst": cst, "bucket_one": bucket_one, "bucket_off": bucket_off,
    }
    arrays = {k: np.ascontiguousarray(v) for k, v in arrays.items()}
    nc = bacc.Bacc("TRN2", target_bir_lowering=False, num_devices=1)
    aps = {k: nc.dram_tensor(f"in_{k}", v.shape, _mybir.dt.from_np(v.dtype), kind="ExternalInput").ap() for k, v in arrays.items()}
    out = nc.dram_tensor("out_0", (NT, P, D), F32, kind="ExternalOutput").ap()
    block_kernel(nc, aps, out)
    r = run(nc, [{f"in_{k}": v for k, v in arrays.items()}], core_ids=[0])
    return r.results[0]["out_0"].reshape(1, T, D)
```
